# Optimizing a Trainium2 kernel written in Bass

```python
import math
import jax, jax.numpy as jnp
from jax import lax
import numpy as np

D_MODEL = 1024
BATCH = 1
SEQ = 256
DEPTH = 2

CTX_LEN = 256
GRID_W = 64
N_MIXERS = 3
E_BRANCH = 2 * D_MODEL
MLA_HEADS = D_MODEL // 64
MLA_NOPE = 128
MLA_ROPE = 64
MLA_V = 128
MLA_WIDTH = MLA_HEADS * MLA_V
MLA_Q_RANK = D_MODEL // 4
MLA_KV_RANK = D_MODEL // 8
MLA_SPLITS = (MLA_Q_RANK, MLA_Q_RANK + MLA_KV_RANK, MLA_Q_RANK + MLA_KV_RANK + MLA_ROPE)
MLA_IN = MLA_Q_RANK + MLA_KV_RANK + MLA_ROPE + MLA_WIDTH
ROPE_BASE = 10000.0
Q_BLOCK = 128
S5_GROUP = 16
S5_GROUPS = E_BRANCH // S5_GROUP
S5_STATE = 64
S5_CHUNK = 128
DT_MIN = 0.001
DT_MAX = 0.1
CONV_WIDTH = 31
CONV_PAD = CONV_WIDTH // 2
DEEPNORM_ALPHA = (2.0 * DEPTH) ** 0.25
DEEPNORM_BETA = (8.0 * DEPTH) ** -0.25
NORM_EPS = 1e-6


def _layernorm(x, g, b):
    xf = x.astype(jnp.float32)
    mu = jnp.mean(xf, axis=-1, keepdims=True)
    var = jnp.mean(jnp.square(xf - mu), axis=-1, keepdims=True)
    y = (xf - mu) * lax.rsqrt(var + NORM_EPS) * g.astype(jnp.float32) + b.astype(jnp.float32)
    return y.astype(x.dtype)

def _rmsnorm(x, g):
    xf = x.astype(jnp.float32)
    y = xf * lax.rsqrt(jnp.mean(jnp.square(xf), axis=-1, keepdims=True) + NORM_EPS) * g.astype(jnp.float32)
    return y.astype(x.dtype)

def _axial_rope_tables(rows):
    r, col = jnp.meshgrid(jnp.arange(rows, dtype=jnp.float32), jnp.arange(GRID_W, dtype=jnp.float32), indexing='ij')
    r, col = r.reshape(-1), col.reshape(-1)
    quarter = MLA_ROPE // 4
    inv = ROPE_BASE ** (-jnp.arange(quarter, dtype=jnp.float32) / quarter)
    ang_r = r[:, None] * inv
    ang_c = col[:, None] * inv
    ang = jnp.concatenate([ang_r, ang_r, ang_c, ang_c], axis=-1)
    return jnp.cos(ang), jnp.sin(ang)

def _apply_rope(v, cos, sin):
    x1, x2, x3, x4 = jnp.split(v, 4, axis=-1)
    rot = jnp.concatenate([-x2, x1, -x4, x3], axis=-1)
    return v * cos.astype(v.dtype) + rot * sin.astype(v.dtype)

def _mla_split(h, w_in, kv_norm):
    q_dn, kv_dn, k_rope, gate = jnp.split(h @ w_in, MLA_SPLITS, axis=-1)
    return q_dn, _rmsnorm(kv_dn, kv_norm), k_rope, gate

def _mla_queries(q_dn, q_norm, w_uq, w_uk):
    b, n, _ = q_dn.shape
    q = (_rmsnorm(q_dn, q_norm) @ w_uq).reshape(b, n, MLA_HEADS, MLA_NOPE + MLA_ROPE)
    q_abs = jnp.einsum('bnhd,chd->bnhc', q[..., :MLA_NOPE], w_uk)
    return q_abs, q[..., MLA_NOPE:]

def _mla_output(o_lat, gate, w_uv, w_out):
    b, n = o_lat.shape[:2]
    v = jnp.einsum('bnhc,chv->bnhv', o_lat, w_uv).reshape(b, n, MLA_WIDTH)
    return (v * jax.nn.silu(gate)) @ w_out

def _mla_mixer(h_lat, h_ctx, cos, sin, w_in, q_norm, kv_norm, w_uq, w_uk, w_uv, w_out, with_ctx_out):
    b, s, _ = h_lat.shape
    scale = (MLA_NOPE + MLA_ROPE) ** -0.5
    q_dn_l, ckv_l, kr_l, g_l = _mla_split(h_lat, w_in, kv_norm)
    q_dn_c, ckv_c, kr_c, g_c = _mla_split(h_ctx, w_in, kv_norm)
    qa_l, qr_l = _mla_queries(q_dn_l, q_norm, w_uq, w_uk)
    keys_lat = jnp.concatenate([ckv_l, _apply_rope(kr_l, cos, sin)], axis=-1)
    keys_ctx = jnp.concatenate([ckv_c, kr_c], axis=-1)

    def block(args):
        qa, qr, cs, sn = args
        q_pos = jnp.concatenate([qa, _apply_rope(qr, cs[:, None], sn[:, None])], axis=-1)
        q_free = jnp.concatenate([qa, qr], axis=-1)
        s_all = jnp.concatenate([jnp.einsum('bthd,bkd->bhtk', q_pos, keys_lat),
                                 jnp.einsum('bthd,bkd->bhtk', q_free, keys_ctx)], axis=-1)
        p = jax.nn.softmax(s_all.astype(jnp.float32) * scale, axis=-1).astype(ckv_l.dtype)
        return (jnp.einsum('bhtk,bkc->bthc', p[..., :s], ckv_l)
                + jnp.einsum('bhtk,bkc->bthc', p[..., s:], ckv_c))

    nblk = s // Q_BLOCK
    to_blocks = lambda a: a.reshape(b, nblk, Q_BLOCK, *a.shape[2:]).swapaxes(0, 1)
    o = lax.map(block, (to_blocks(qa_l), to_blocks(qr_l),
                        cos.reshape(nblk, Q_BLOCK, MLA_ROPE), sin.reshape(nblk, Q_BLOCK, MLA_ROPE)))
    o = o.swapaxes(0, 1).reshape(b, s, MLA_HEADS, MLA_KV_RANK)
    y_lat = _mla_output(o, g_l, w_uv, w_out)
    if not with_ctx_out:
        return y_lat, None
    qa_c, qr_c = _mla_queries(q_dn_c, q_norm, w_uq, w_uk)
    q_c = jnp.concatenate([qa_c, qr_c], axis=-1)
    p_c = jax.nn.softmax(jnp.einsum('bthd,bkd->bhtk', q_c, keys_ctx).astype(jnp.float32) * scale,
                         axis=-1).astype(ckv_c.dtype)
    o_c = jnp.einsum('bhtk,bkc->bthc', p_c, ckv_c)
    return y_lat, _mla_output(o_c, g_c, w_uv, w_out)

def _ssm_combine(left, right):
    a_l, b_l = left
    a_r, b_r = right
    return a_r * a_l, a_r * b_l + b_r

def _s5_direction(u_ctx, u_lat, lam, dt, bmat, cmat):
    lam_dt = lam * dt[:, None]
    lam_bar = jnp.exp(lam_dt)
    b_bar = ((lam_bar - 1.0) / lam)[..., None] * bmat
    powers = jnp.exp(lam_dt[None] * jnp.arange(1, S5_CHUNK + 1, dtype=jnp.float32)[:, None, None])

    def step(h, u_chunk):
        bu = jnp.einsum('btgs,gps->btgp', u_chunk.astype(jnp.complex64), b_bar)
        a = jnp.broadcast_to(lam_bar, bu.shape)
        _, xs = lax.associative_scan(_ssm_combine, (a, bu), axis=1)
        xs = xs + powers[None] * h[:, None]
        y = jnp.einsum('btgp,gsp->btgs', xs, cmat).real
        return xs[:, -1], y

    def run(u, h0):
        bsz, n = u.shape[:2]
        nch = n // S5_CHUNK
        chunks = u.reshape(bsz, nch, S5_CHUNK, S5_GROUPS, S5_GROUP).swapaxes(0, 1)
        h_fin, ys = lax.scan(step, h0, chunks)
        return h_fin, ys.swapaxes(0, 1).reshape(bsz, n, S5_GROUPS * S5_GROUP)

    h0 = jnp.zeros((u_lat.shape[0], S5_GROUPS, S5_STATE), jnp.complex64)
    h_ctx, y_ctx = run(u_ctx, h0)
    _, y_lat = run(u_lat, h_ctx)
    return y_ctx, y_lat

def _s5_mixer(h_lat, h_ctx, w_in, lam_re, lam_im, log_dt, b_re, b_im, c_re, c_im, d_skip, w_glu, b_glu, w_out,
              with_ctx_out):
    u_l, g_l = jnp.split(h_lat @ w_in, 2, axis=-1)
    u_c, g_c = jnp.split(h_ctx @ w_in, 2, axis=-1)
    ul, uc = u_l.astype(jnp.float32), u_c.astype(jnp.float32)
    dsk = d_skip.astype(jnp.float32)
    y_l, y_c = dsk * ul, dsk * uc
    f32 = lambda a: a.astype(jnp.float32)
    for direction in range(2):
        lam = lax.complex(jnp.minimum(f32(lam_re[direction]), -1e-4), f32(lam_im[direction]))
        dt = jnp.exp(f32(log_dt[direction]))
        bmat = lax.complex(f32(b_re[direction]), f32(b_im[direction]))
        cmat = lax.complex(f32(c_re[direction]), f32(c_im[direction]))
        if direction == 0:
            yc, yl = _s5_direction(uc, ul, lam, dt, bmat, cmat)
        else:
            yc, yl = _s5_direction(jnp.flip(uc, 1), jnp.flip(ul, 1), lam, dt, bmat, cmat)
            yc, yl = jnp.flip(yc, 1), jnp.flip(yl, 1)
        y_l, y_c = y_l + yl, y_c + yc

    def glu_out(y, g):
        y = jax.nn.gelu(y.astype(g.dtype))
        ya, yb = jnp.split(y @ w_glu + b_glu, 2, axis=-1)
        return ((ya * jax.nn.sigmoid(yb)) * jax.nn.silu(g)) @ w_out

    y_ctx = glu_out(y_c, g_c) if with_ctx_out else None
    return glu_out(y_l, g_l), y_ctx

def _conv_mixer(h_lat, h_ctx, w_in, dw, dw_b, ln_g, ln_b, w_out, with_ctx_out):
    def branch(h):
        a, bgate, g = jnp.split(h @ w_in, 3, axis=-1)
        v = a * jax.nn.sigmoid(bgate)
        v = lax.conv_general_dilated(v, dw[:, None, :], window_strides=(1,), padding=[(CONV_PAD, CONV_PAD)],
                                     dimension_numbers=('NWC', 'WIO', 'NWC'),
                                     feature_group_count=E_BRANCH) + dw_b
        v = jax.nn.silu(_layernorm(v, ln_g, ln_b))
        return (v * jax.nn.silu(g)) @ w_out
    y_ctx = branch(h_ctx) if with_ctx_out else None
    return branch(h_lat), y_ctx

def first_inputs(seed: int = 0) -> dict:
    key = jax.random.key(seed)
    ks = iter(jax.random.split(key, 48))
    f = jnp.float32
    nrm = lambda shape, scale: jax.random.normal(next(ks), shape, f) * scale
    n_a, n_b, n_c = [len(range(k, DEPTH, N_MIXERS)) for k in range(N_MIXERS)]
    D, E, G, P, GS = D_MODEL, E_BRANCH, S5_GROUPS, S5_STATE, S5_GROUP
    lam_im = jnp.broadcast_to(math.pi * jnp.arange(P, dtype=f), (n_b, 2, G, P))
    return {
        'x': nrm((BATCH, SEQ, D), 1.0),
        'c': nrm((BATCH, D), 1.0),
        'ctx': nrm((BATCH, CTX_LEN, D), 1.0),
        'c_ctx': nrm((D,), 1.0),
        'w_mod': nrm((DEPTH, D, 3 * D), 0.5 * D ** -0.5),
        'b_mod': nrm((DEPTH, 3 * D), 0.02),
        'ln_g': 1.0 + nrm((DEPTH, D), 0.02),
        'ln_b': nrm((DEPTH, D), 0.02),
        'mla_w_in': nrm((n_a, D, MLA_IN), D ** -0.5),
        'mla_q_norm': 1.0 + nrm((n_a, MLA_Q_RANK), 0.02),
        'mla_kv_norm': 1.0 + nrm((n_a, MLA_KV_RANK), 0.02),
        'mla_w_uq': nrm((n_a, MLA_Q_RANK, MLA_HEADS * (MLA_NOPE + MLA_ROPE)), MLA_Q_RANK ** -0.5),
        'mla_w_uk': nrm((n_a, MLA_KV_RANK, MLA_HEADS, MLA_NOPE), MLA_NOPE ** -0.5),
        'mla_w_uv': nrm((n_a, MLA_KV_RANK, MLA_HEADS, MLA_V), MLA_KV_RANK ** -0.5),
        'mla_w_out': nrm((n_a, MLA_WIDTH, D), DEEPNORM_BETA * MLA_WIDTH ** -0.5),
        's5_w_in': nrm((n_b, D, 2 * E), D ** -0.5),
        's5_lam_re': -0.5 + nrm((n_b, 2, G, P), 0.01),
        's5_lam_im': lam_im,
        's5_log_dt': jax.random.uniform(next(ks), (n_b, 2, G), f, math.log(DT_MIN), math.log(DT_MAX)),
        's5_b_re': nrm((n_b, 2, G, P, GS), (2.0 * GS) ** -0.5),
        's5_b_im': nrm((n_b, 2, G, P, GS), (2.0 * GS) ** -0.5),
        's5_c_re': nrm((n_b, 2, G, GS, P), P ** -0.5),
        's5_c_im': nrm((n_b, 2, G, GS, P), P ** -0.5),
        's5_d': nrm((n_b, E), 0.5),
        's5_w_glu': nrm((n_b, E, 2 * E), E ** -0.5),
        's5_b_glu': nrm((n_b, 2 * E), 0.02),
        's5_w_out': nrm((n_b, E, D), DEEPNORM_BETA * E ** -0.5),
        'cv_w_in': nrm((n_c, D, 3 * E), D ** -0.5),
        'cv_dw': nrm((n_c, CONV_WIDTH, E), CONV_WIDTH ** -0.5),
        'cv_dw_b': nrm((n_c, E), 0.02),
        'cv_ln_g': 1.0 + nrm((n_c, E), 0.02),
        'cv_ln_b': nrm((n_c, E), 0.02),
        'cv_w_out': nrm((n_c, E, D), DEEPNORM_BETA * E ** -0.5),
    }

def first_block(x, c, ctx, c_ctx, w_mod, b_mod, ln_g, ln_b,
              mla_w_in, mla_q_norm, mla_kv_norm, mla_w_uq, mla_w_uk, mla_w_uv, mla_w_out,
              s5_w_in, s5_lam_re, s5_lam_im, s5_log_dt, s5_b_re, s5_b_im, s5_c_re, s5_c_im, s5_d,
              s5_w_glu, s5_b_glu, s5_w_out,
              cv_w_in, cv_dw, cv_dw_b, cv_ln_g, cv_ln_b, cv_w_out):
    n_tokens = x.shape[1]
    ROWS = n_tokens // GRID_W
    cos, sin = _axial_rope_tables(ROWS)
    cond = jax.nn.silu(c)
    cond_ctx = jax.nn.silu(c_ctx)
    for i in range(DEPTH):
        kind, j = i % N_MIXERS, i // N_MIXERS
        with_ctx_out = i < DEPTH - 1
        sh, sc, gt = jnp.split(cond @ w_mod[i] + b_mod[i], 3, axis=-1)
        sh_c, sc_c, gt_c = jnp.split(cond_ctx @ w_mod[i] + b_mod[i], 3, axis=-1)
        h_lat = x * (1.0 + sc[:, None]) + sh[:, None]
        h_ctx = ctx * (1.0 + sc_c) + sh_c
        if kind == 0:
            y_lat, y_ctx = _mla_mixer(h_lat, h_ctx, cos, sin, mla_w_in[j], mla_q_norm[j], mla_kv_norm[j],
                                      mla_w_uq[j], mla_w_uk[j], mla_w_uv[j], mla_w_out[j], with_ctx_out)
        elif kind == 1:
            y_lat, y_ctx = _s5_mixer(h_lat, h_ctx, s5_w_in[j], s5_lam_re[j], s5_lam_im[j], s5_log_dt[j],
                                     s5_b_re[j], s5_b_im[j], s5_c_re[j], s5_c_im[j], s5_d[j],
                                     s5_w_glu[j], s5_b_glu[j], s5_w_out[j], with_ctx_out)
        else:
            y_lat, y_ctx = _conv_mixer(h_lat, h_ctx, cv_w_in[j], cv_dw[j], cv_dw_b[j], cv_ln_g[j], cv_ln_b[j],
                                       cv_w_out[j], with_ctx_out)
        x = _layernorm(DEEPNORM_ALPHA * x + gt[:, None] * y_lat, ln_g[i], ln_b[i])
        if with_ctx_out:
            ctx = _layernorm(DEEPNORM_ALPHA * ctx + gt_c * y_ctx, ln_g[i], ln_b[i])
    return x


DEPTH_2 = 1

N_MEM = 256
D_MIX = D_MODEL
POOL_WIDTH = D_MIX // 2
POOL_WINDOWS = (2, 4, 8, 16)
POOL_GROUPS = len(POOL_WINDOWS)
POOL_GROUP_DIM = POOL_WIDTH // POOL_GROUPS
SGU_WIDTH = D_MIX - POOL_WIDTH
SGU_HEADS = 4
SGU_HEAD_DIM = SGU_WIDTH // SGU_HEADS
CHUNK = 128
D_IN_PROJ = POOL_WIDTH + 2 * SGU_WIDTH
XATTN_HEADS = 4
XATTN_HEAD_DIM = D_MODEL // XATTN_HEADS
D_FF = 2816
CONV_WIDTH_2 = 3
EPS = 1e-6


def rmsnorm(x, g):
    xf = x.astype(jnp.float32)
    y = xf * lax.rsqrt(jnp.mean(xf * xf, axis=-1, keepdims=True) + EPS)
    return (y * g.astype(jnp.float32)).astype(x.dtype)

def layernorm_nobias(x, g):
    xf = x.astype(jnp.float32)
    mu = jnp.mean(xf, axis=-1, keepdims=True)
    xc = xf - mu
    y = xc * lax.rsqrt(jnp.mean(xc * xc, axis=-1, keepdims=True) + EPS)
    return (y * g.astype(jnp.float32)).astype(x.dtype)

def pool_mixer(p, pool_w, pool_scale):
    B, S, _ = p.shape
    pf = p.astype(jnp.float32)
    c = jnp.pad(jnp.cumsum(pf, axis=1), ((0, 0), (1, 0), (0, 0)))
    t = jnp.arange(S)
    diffs = []
    for gi, win in enumerate(POOL_WINDOWS):
        sl = slice(gi * POOL_GROUP_DIM, (gi + 1) * POOL_GROUP_DIM)
        cg = c[..., sl]
        prev = jnp.pad(cg, ((0, 0), (win - 1, 0), (0, 0)))[:, :S]
        count = jnp.minimum(t + 1, win).astype(jnp.float32)[None, :, None]
        diffs.append((cg[:, 1:] - prev) / count - pf[..., sl])
    d = jnp.stack(diffs, axis=2).astype(p.dtype)
    y = jnp.einsum('bsgc,gcd->bsgd', d, pool_w).reshape(B, S, POOL_WIDTH)
    return y * pool_scale

def sgu_mixer(u, v, sgu_g, sgu_w, sgu_b):
    B, S, _ = u.shape
    vn = layernorm_nobias(v, sgu_g)
    vc = vn.reshape(B, S // CHUNK, CHUNK, SGU_HEADS, SGU_HEAD_DIM)
    mask = jnp.tril(jnp.ones((CHUNK, CHUNK), dtype=bool))
    w_masked = jnp.where(mask[None], sgu_w, jnp.zeros_like(sgu_w))
    z = jnp.einsum('hts,bnshd->bnthd', w_masked, vc) + sgu_b.T[:, :, None]
    return u * z.reshape(B, S, SGU_WIDTH)

def mem_cross_attention(xn, mem, mem_g, wq, wk, wv, wo):
    B, S, _ = xn.shape
    memn = rmsnorm(mem, mem_g)
    q = (xn @ wq).reshape(B, S, XATTN_HEADS, XATTN_HEAD_DIM)
    k = (memn @ wk).reshape(B, N_MEM, XATTN_HEADS, XATTN_HEAD_DIM)
    v = (memn @ wv).reshape(B, N_MEM, XATTN_HEADS, XATTN_HEAD_DIM)
    s = jnp.einsum('bshd,bmhd->bhsm', q, k).astype(jnp.float32) * (XATTN_HEAD_DIM ** -0.5)
    pr = jax.nn.softmax(s, axis=-1).astype(v.dtype)
    o = jnp.einsum('bhsm,bmhd->bshd', pr, v).reshape(B, S, D_MODEL)
    return o @ wo

def conv_ffn(xn, w_up, conv_w, conv_b, w_down):
    S = xn.shape[1]
    h = xn @ w_up
    hp = jnp.pad(h, ((0, 0), (CONV_WIDTH_2 - 1, 0), (0, 0)))
    hc = conv_b + sum(conv_w[k] * hp[:, k:k + S] for k in range(CONV_WIDTH_2))
    gate, val = jnp.split(hc, 2, axis=-1)
    return (jax.nn.silu(gate) * val) @ w_down

def second_inputs(seed: int = 0) -> dict:
    key = jax.random.key(seed)
    ks = jax.random.split(key, 24)
    f32 = jnp.float32
    n = lambda k, shape, s: (jax.random.normal(k, shape, f32) * s)
    gain = lambda k, shape: 1.0 + 0.05 * jax.random.normal(k, shape, f32)
    L = DEPTH_2
    return {
        "x": jax.random.normal(ks[0], (BATCH, SEQ, D_MODEL), f32),
        "mem": jax.random.normal(ks[1], (BATCH, N_MEM, D_MODEL), f32),
        "norm_mix_g": gain(ks[2], (L, D_MODEL)),
        "w_in": n(ks[3], (L, D_MODEL, D_IN_PROJ), D_MODEL ** -0.5),
        "pool_w": n(ks[4], (L, POOL_GROUPS, POOL_GROUP_DIM, POOL_GROUP_DIM), POOL_GROUP_DIM ** -0.5),
        "pool_scale": 1.0 + 0.1 * jax.random.normal(ks[5], (L, POOL_WIDTH), f32),
        "sgu_g": gain(ks[6], (L, SGU_WIDTH)),
        "sgu_w": n(ks[7], (L, SGU_HEADS, CHUNK, CHUNK), CHUNK ** -0.5),
        "sgu_b": 1.0 + 0.05 * jax.random.normal(ks[8], (L, SGU_HEADS, CHUNK), f32),
        "w_out": n(ks[9], (L, D_MIX, D_MODEL), D_MIX ** -0.5),
        "norm_xattn_g": gain(ks[10], (L, D_MODEL)),
        "mem_norm_g": gain(ks[11], (L, D_MODEL)),
        "wq": n(ks[12], (L, D_MODEL, D_MODEL), D_MODEL ** -0.5),
        "wk": n(ks[13], (L, D_MODEL, D_MODEL), D_MODEL ** -0.5),
        "wv": n(ks[14], (L, D_MODEL, D_MODEL), D_MODEL ** -0.5),
        "wo": n(ks[15], (L, D_MODEL, D_MODEL), D_MODEL ** -0.5),
        "norm_ffn_g": gain(ks[16], (L, D_MODEL)),
        "w_up": n(ks[17], (L, D_MODEL, 2 * D_FF), D_MODEL ** -0.5),
        "conv_w": n(ks[18], (L, CONV_WIDTH_2, 2 * D_FF), CONV_WIDTH_2 ** -0.5),
        "conv_b": n(ks[19], (L, 2 * D_FF), 0.02),
        "w_down": n(ks[20], (L, D_FF, D_MODEL), D_FF ** -0.5),
        "final_norm_g": gain(ks[21], (D_MODEL,)),
    }

def second_block(x, mem, norm_mix_g, w_in, pool_w, pool_scale, sgu_g, sgu_w, sgu_b, w_out,
              norm_xattn_g, mem_norm_g, wq, wk, wv, wo,
              norm_ffn_g, w_up, conv_w, conv_b, w_down, final_norm_g):
    h = x
    for l in range(DEPTH_2):
        xn = rmsnorm(h, norm_mix_g[l])
        proj = xn @ w_in[l]
        p = proj[..., :POOL_WIDTH]
        uv = jax.nn.gelu(proj[..., POOL_WIDTH:], approximate=False)
        u, v = uv[..., :SGU_WIDTH], uv[..., SGU_WIDTH:]
        y_pool = pool_mixer(p, pool_w[l], pool_scale[l])
        y_sgu = sgu_mixer(u, v, sgu_g[l], sgu_w[l], sgu_b[l])
        h = h + jnp.concatenate([y_pool, y_sgu], axis=-1) @ w_out[l]
        xn = rmsnorm(h, norm_xattn_g[l])
        h = h + mem_cross_attention(xn, mem, mem_norm_g[l], wq[l], wk[l], wv[l], wo[l])
        xn = rmsnorm(h, norm_ffn_g[l])
        h = h + conv_ffn(xn, w_up[l], conv_w[l], conv_b[l], w_down[l])
    return rmsnorm(h, final_norm_g)


def setup_inputs(seed=0):
    out = dict(first_inputs(seed))
    for name, value in second_inputs(seed + 1).items():
        if name != "x":
            out[name + "_2"] = value
    return out


def reference(
    x, c, ctx, c_ctx, w_mod, b_mod, ln_g, ln_b, mla_w_in, mla_q_norm, mla_kv_norm, mla_w_uq,
    mla_w_uk, mla_w_uv, mla_w_out, s5_w_in, s5_lam_re, s5_lam_im, s5_log_dt, s5_b_re, s5_b_im,
    s5_c_re, s5_c_im, s5_d, s5_w_glu, s5_b_glu, s5_w_out, cv_w_in, cv_dw, cv_dw_b, cv_ln_g,
    cv_ln_b, cv_w_out, mem_2, norm_mix_g_2, w_in_2, pool_w_2, pool_scale_2, sgu_g_2, sgu_w_2,
    sgu_b_2, w_out_2, norm_xattn_g_2, mem_norm_g_2, wq_2, wk_2, wv_2, wo_2, norm_ffn_g_2,
    w_up_2, conv_w_2, conv_b_2, w_down_2, final_norm_g_2,
):
    x = first_block(
        x, c, ctx, c_ctx, w_mod, b_mod, ln_g, ln_b, mla_w_in, mla_q_norm, mla_kv_norm, mla_w_uq,
        mla_w_uk, mla_w_uv, mla_w_out, s5_w_in, s5_lam_re, s5_lam_im, s5_log_dt, s5_b_re,
        s5_b_im, s5_c_re, s5_c_im, s5_d, s5_w_glu, s5_b_glu, s5_w_out, cv_w_in, cv_dw, cv_dw_b,
        cv_ln_g, cv_ln_b, cv_w_out,
    )
    return second_block(
        x, mem_2, norm_mix_g_2, w_in_2, pool_w_2, pool_scale_2, sgu_g_2, sgu_w_2, sgu_b_2,
        w_out_2, norm_xattn_g_2, mem_norm_g_2, wq_2, wk_2, wv_2, wo_2, norm_ffn_g_2, w_up_2,
        conv_w_2, conv_b_2, w_down_2, final_norm_g_2,
    )


_drawn_inputs = setup_inputs


def setup_inputs(seed=0):
    import zlib

    import numpy as np

    out = dict(_drawn_inputs(seed))
    spreads = {}
    factors = {'ctx': 8.0,
     'c_ctx': 7.028,
     'b_mod': 8.0,
     'mla_w_in': 2.99,
     'mla_q_norm': 8.0,
     'mla_kv_norm': 8.0,
     'mla_w_uq': 7.061,
     'mla_w_uk': 7.741,
     'mla_w_uv': 3.095,
     'mla_w_out': 3.271,
     's5_w_in': 3.889,
     's5_lam_re': 64.0,
     's5_lam_im': 64.0,
     's5_log_dt': 64.0,
     's5_b_re': 64.0,
     's5_b_im': 64.0,
     's5_c_re': 64.0,
     's5_c_im': 64.0,
     's5_d': 4.265,
     's5_w_glu': 3.85,
     's5_b_glu': 8.0,
     's5_w_out': 3.813,
     'sgu_g_2': 4.266,
     'sgu_b_2': 3.0,
     'norm_xattn_g_2': 8.0,
     'mem_norm_g_2': 7.997,
     'conv_b_2': 26.591,
     'norm_ffn_g_2': 8.0}
    for name, (base, spread) in spreads.items():
        noise = np.random.default_rng([zlib.crc32(name.encode()), seed]).standard_normal(out[name].shape)
        drawn = base * np.exp(spread * noise) if base else spread * noise
        out[name] = __import__('jax').numpy.asarray(drawn.astype(out[name].dtype))
    for name, factor in factors.items():
        out[name] = (out[name] * factor).astype(out[name].dtype)
    return out
```

```python
from contextlib import ExitStack, contextmanager

import numpy as np

import concourse.bass as bass
from concourse import mybir

ALU = mybir.AluOpType
ACT = mybir.ActivationFunctionType
AX = mybir.AxisListType
F32 = mybir.dt.float32
I32 = mybir.dt.int32

P = 128
D = 1024
KD = D // P
S = 256
T = 2 * S
DEPTH = 2
E_BR = 2 * D
KE = E_BR // P
HEADS = 16
PAIRS = HEADS // 2
NOPE, ROPE, VDIM = 128, 64, 128
QR, KVR = D // 4, D // 8
HQ = NOPE + ROPE
SM_SCALE = float(HQ) ** -0.5
GRID_W = 64
G5, CH5, ST5 = 128, 16, 64
L5 = 8
NC5 = T // L5
NCL = S // L5
GP5 = G5 // 2
BLK = 4
NB5 = GP5 // BLK
NPW = L5 + 1
KW5 = (2 * L5 - 1) * CH5
ALPHA = (2.0 * DEPTH) ** 0.25
EPS = 1e-6
POOLW = (2, 4, 8, 16)
XH, XHD = 4, 256
FF = 2816
KF = FF // P
NSLOT = 4
MT2 = 256
MAGIC = 12582912.0
LOG2E, LN2_HI, LN2_LO = 1.4426950408889634, 0.693359375, -2.12194440e-4
INV_2PI = 0.15915494309189535
PI2_A = 6.28125
PI2_B = 2029.0 / 2 ** 20
PI2_C = 6.283185307179586 - PI2_A - PI2_B
TWO_PI_DOWN = 6.2831845

C_ID, C_ROT, C_COS, C_SIN = 0, 128, 256, 512
C_CNT, C_MASK, C_IOTA, C_HPI, C_EPS = 768, 832, 960, 1024, 1025
C_COLS = 1026

VEC_TILES = [
    [("b_mod", 48), ("ln_g", 16), ("ln_b", 16), ("mla_q_norm", 2), ("mla_kv_norm", 1), ("s5_b_glu", 32), ("c", 8)],
    [("c_ctx", 8), ("norm_mix_g_2", 8), ("pool_scale_2", 4), ("sgu_g_2", 4), ("norm_xattn_g_2", 8),
     ("mem_norm_g_2", 8), ("norm_ffn_g_2", 8), ("conv_b_2", 44), ("final_norm_g_2", 8)],
    [("conv_w_2", 132)],
]
NVT = 4


def shape_constants():
    c = np.zeros((P, C_COLS), np.float32)
    c[:, C_ID:C_ID + P] = np.eye(P)
    q = ROPE // 4
    for h in range(2):
        for j in range(q):
            for a, b in ((0, 1), (2, 3)):
                lo, hi = h * ROPE + a * q + j, h * ROPE + b * q + j
                c[hi, C_ROT + lo] = -1.0
                c[lo, C_ROT + hi] = 1.0
    inv = (np.float32(10000.0) ** (-np.arange(q, dtype=np.float32) / np.float32(q))).astype(np.float32)
    tok = np.arange(S)
    row = (tok // GRID_W).astype(np.float32)[:, None] * inv
    col = (tok % GRID_W).astype(np.float32)[:, None] * inv
    ang = np.concatenate([row, row, col, col], axis=1).T
    c[:, C_COS:C_COS + S] = np.tile(np.cos(ang), (2, 1))
    c[:, C_SIN:C_SIN + S] = np.tile(np.sin(ang), (2, 1))
    for g, w in enumerate(POOLW):
        c[:, C_CNT + 16 * g:C_CNT + 16 * g + 16] = 1.0 / np.minimum(np.arange(16) + 1, w)
    c[:, C_MASK:C_MASK + P] = np.triu(np.ones((P, P)))
    c[:, C_IOTA:C_IOTA + NC5] = np.arange(NC5)
    c[:, C_HPI] = np.pi / 2
    c[:, C_EPS] = EPS
    return c


class Step:

    def __init__(self, turn, per):
        self.turn, self.per = turn, per

    def __mul__(self, k):
        return self.turn * (self.per * k)

    def __floordiv__(self, k):
        assert self.per % k == 0
        return self.turn * (self.per // k)

    def __add__(self, k):
        return self.turn * self.per + k


class Link:

    def __init__(self, eng, sem):
        self.eng, self.sem, self.at, self.i, self.k = eng, sem, 0, 0, 0

    def __call__(self, ins):
        ins.then_inc(self.sem, 1)
        self.k += 1
        self.eng.wait_ge(self.sem, self.i + (self.at + self.k))

    def begin(self, i, per):
        self.at, self.k, self.i, self.per = self.at + self.k, 0, i * per, per

    def end(self, turns):
        assert self.k == self.per, (self.k, self.per)
        self.at, self.k, self.i = self.at + turns * self.per, 0, 0


def program(nc, a, out, spill_b, spill_c):
    ctx = ExitStack()
    with ctx:
        def sb(name, *shape):
            return ctx.enter_context(nc.sbuf_tensor(name, [P, *shape], F32))

        def sem(name):
            return ctx.enter_context(nc.semaphore(name))

        ring = sb("ring", NSLOT, 8, MT2)
        xc = sb("xc", KD, S)
        xl = sb("xl", KD, S)
        ht = sb("ht", KD, T)
        gate = sb("gate", KE, T)
        cst = sb("cst", C_COLS)
        col = sb("col", NVT * P)
        mod = sb("mod", DEPTH, 24, 2)
        cond = sb("cond", KD, 2)
        avg_d = sb("avg_d", P)
        avg_q = sb("avg_q", P)
        avg_kv = sb("avg_kv", P)
        avg_sgu = sb("avg_sgu", P)
        pw = sb("pw", 2, NPW, P)
        phi = sb("phi", P)
        r8 = sb("r8", P)
        dcol = sb("dcol", G5)
        NA = 23500
        arena = sb("arena", NA)

        psum = [ctx.enter_context(nc.psum_tensor(f"bank{i}", [P, 512], F32)) for i in range(8)]

        def carve(at, *dims, base=arena):
            n = int(np.prod(dims))
            v = base[:, at:at + n]
            if len(dims) == 1:
                return v
            names = "abcdefg"[:len(dims)]
            return v.rearrange(f"p ({' '.join(names)}) -> p {' '.join(names)}", **dict(zip(names, dims)))

        class Carver:
            def __init__(self, at=0):
                self.at = at

            def __call__(self, *dims):
                v = carve(self.at, *dims)
                self.at += int(np.prod(dims))
                assert self.at <= NA, self.at
                return v

        ident = cst[:, C_ID:C_ID + P]
        rot = cst[:, C_ROT:C_ROT + P]
        cos = cst[:, C_COS:C_COS + S]
        sin = cst[:, C_SIN:C_SIN + S]
        iota = cst[:, C_IOTA:C_IOTA + NC5]
        half_pi = cst[:, C_HPI:C_HPI + 1]
        eps = cst[:, C_EPS:C_EPS + 1]

        at_col = {}
        for t, names in enumerate(VEC_TILES):
            n = t * P
            for name, rows in names:
                at_col[name] = n
                n += rows

        def vec(name, i):
            j = at_col[name] + i
            return col[:, j:j + 1]

        def vecr(name, i):
            return col[:, bass.ds(i + at_col[name], 1)]

        def by_chunk(row):
            return row.rearrange("p (s h c) -> p c h s", s=4, h=2)

        c0 = Carver()
        xtok = c0(4, D)
        vrow = c0(NVT, P)
        raw_b = c0(2, ST5 * 2 * CH5)
        raw_c = c0(2, ST5 * 2 * CH5)
        lam_rows = c0(2, P)
        d_rows = c0(L5, CH5)
        d_raw = c0(CH5)
        dt_raw = c0(2)
        dt_t = [c0(2) for _ in range(6)]
        dt_exp = c0(2, ST5)
        pars = [c0(P) for _ in range(20)]
        tmp_b = raw_b.rearrange("p a b -> p (a b)").rearrange("p (z q c) -> p z q c", z=2, c=CH5)
        bcol = gate[:, 0:8, :].rearrange("p a b -> p (a b)").rearrange("p (z q c) -> p z q c", z=2, c=CH5)
        ccol = gate[:, 8:16, :].rearrange("p a b -> p (a b)").rearrange("p (z q c) -> p z q c", z=2, c=CH5)
        pn = carve(0, 2, NPW, P)

        ln_rs = carve(22400, T)
        c1 = Carver()
        qd = c1(2, T)
        kvd = c1(T)
        sq1 = c1(3, T)
        rs1 = c1(2, T)
        qn = c1(2, T)
        ckv = c1(T)
        ckv_tok = c1(4, P)
        kr = c1(T)
        kr_rot = c1(S)
        rot_t = c1(S)
        att_uq = [c1(2, 2 * HQ) for _ in range(2)]
        att_uk = [c1(2 * NOPE) for _ in range(2)]
        att_uv = [c1(2 * VDIM) for _ in range(2)]
        qh = [c1(T) for _ in range(2)]
        kh = [c1(T) for _ in range(2)]
        q_rope = c1(T)
        q_rot = c1(S)
        prob = [c1(4, T) for _ in range(2)]
        prob_t = c1(1536)
        pt_ctx = prob_t[:, 0:512].rearrange("p (t k q) -> p t k q", t=2, k=2)
        pt_lat = prob_t[:, 512:1536].rearrange("p (t k q) -> p t k q", t=2, k=4)
        o_lat = c1(T)
        sm = c1(2, 4, 4)

        c2 = Carver()
        u5 = c2(GP5, 2, NC5)
        bt = c2(2, 2, BLK, L5, CH5)
        bmat = c2(2, 2, BLK, P)
        cp = [c2(2, 2, BLK, NPW, CH5) for _ in range(2)]
        bbd = c2(2, 2, BLK, 2, CH5)
        kf = c2(BLK, KW5)
        t0 = [c2(BLK, 2, P) for _ in range(2)]
        utok = t0[0].rearrange("p q g c -> p (q g c)").rearrange("p (g s c) -> p g s c", s=4, c=CH5)
        ub = c2(BLK, 2, NC5)
        bb = c2(2, 2, BLK, CH5)
        cc = c2(2, 2, BLK, CH5)
        xr5 = c2(2, BLK, NCL)
        xi5 = c2(2, BLK, NCL)
        y2 = c2(BLK, 2, NCL)
        ytok = c2(4, P)
        td = c2(BLK, 2, NCL)
        pwb = c2(2, NPW, 2, BLK)

        hflat = ht[:, :, :].rearrange("p a b -> p (a b)")
        zt = [hflat[:, 512 * i:512 * i + 512].rearrange("p (d q c) -> p d q c", d=2, q=BLK) for i in range(8)]
        ang, cos5, sin5, dec5, z1, z2, z3, z4 = zt
        xcflat = xc[:, :, :].rearrange("p a b -> p (a b)")
        gen_v = [xcflat[:, 576 * i:576 * i + 576] for i in range(2)]
        gen_p = [xcflat[:, 1152 + 448 * i:1152 + 448 * i + 448] for i in range(2)]
        gl = gate[:, 0:8, :].rearrange("p a b -> p (a b)").rearrange("p (k t) -> p k t", k=KE)
        yt = gate[:, 8:16, :].rearrange("p a b -> p (a b)").rearrange("p (k t) -> p k t", k=KE)

        c3 = Carver()
        sgm = c3(2, S)
        glu_t = c3(2, S)
        sy = c3(4, S)
        sq = c3(KD, S)
        rstd = c3(S)
        mem_tok = c3(2, D)
        mem_sq = c3(D)
        mem_s = c3(2, 2)
        mem_t = c3(KD, S)
        pp = [c3(4, 16 + S) for _ in range(3)]
        uu = c3(4, S)
        vv = c3(4, S)
        vtok = c3(2, 512)
        pool_w = c3(4, P)
        sgu_w = c3(4, P)
        sgu_wt = c3(4, P)
        sgu_bb = c3(4, P)
        sgu_z = c3(4, S)
        end_sgu = c3.at

        cat = gate[:, 0:4, :].rearrange("p a b -> p (a b)").rearrange("p (k t) -> p k t", k=KD)
        k2 = gate[:, 4:8, :].rearrange("p a b -> p (a b)").rearrange("p (k t) -> p k t", k=KD)
        v2 = gate[:, 8:12, :].rearrange("p a b -> p (a b)").rearrange("p (k t) -> p k t", k=2)
        q2 = gate[:, 12:16, :].rearrange("p a b -> p (a b)").rearrange("p (k t) -> p k t", k=KD)
        xn = ht[:, 0:4, :].rearrange("p a b -> p (a b)").rearrange("p (k t) -> p k t", k=KD)
        o2 = ht[:, 4:8, :].rearrange("p a b -> p (a b)").rearrange("p (k t) -> p k t", k=KD)
        prob2 = pp[0].rearrange("p a b -> p (a b)")[:, 0:1024].rearrange("p (b t m) -> p b t m", b=2, t=2)
        prob2_t = pp[1].rearrange("p a b -> p (a b)")[:, 0:512].rearrange("p (m t) -> p m t", m=2)
        sm2 = carve(c3.at, 2, 2, 4)
        ff = carve(mem_off := 4096, KF, S)
        hp = carve(mem_off + KF * S, 4, S + 2)
        cv = carve(mem_off + KF * S + 4 * (S + 2), 4, S)
        orow = carve(0, 2, D)

        const_in = sem("const_in")
        x_in = sem("x_in")
        vec_clear = sem("vec_clear")
        vec_in = sem("vec_in")
        s5par_in = sem("s5par_in")
        ones_set = sem("ones_set")
        vec_t = sem("vec_t")
        vec_out = sem("vec_out")
        cond_set = sem("cond_set")
        w_in_ = [sem(f"slot{i}_loaded") for i in range(NSLOT)]
        slot_done = sem("slot_done")
        unit_free = [sem(f"unit{i}_free") for i in range(2)]
        p0_t = sem("p0_transposed")
        mod_set = sem("mod_set")
        xt_act = sem("xt_odd_set")
        xt_dve = sem("xt_even_set")
        dt_set = sem("dt_set")
        par_t = sem("s5par_transposed")
        par_got = sem("s5par_got")
        act_tanh = sem("tanh_done")
        act_trig = sem("trig_done")
        arg_set = sem("trig_args")
        bc_got = sem("bc_evacuated")
        bc_scaled = sem("bc_scaled")
        bc_spilled = sem("bc_spilled")
        v_link = sem("v_link")
        a_link = sem("a_link")
        p_link = sem("p_link")
        h_ctx = sem("h_ctx_set")
        h_lat = sem("h_lat_set")
        alpha_set = sem("alpha_set")
        qkv_copied = sem("qkv_copied")
        sq_set = sem("sq_set")
        stat = sem("stat_ready")
        root_set = sem("root_set")
        normed = sem("normed")
        ctok_t = sem("ctok_transposed")
        ctok_set = sem("ctok_set")
        att_in = [sem(f"att_weights{i}") for i in range(2)]
        proj_done = sem("proj_done")
        proj_free = [sem(f"proj_free{i}") for i in range(2)]
        qk_set = sem("qk_set")
        qrot_set = sem("qrot_set")
        score_done = sem("score_done")
        bias_set = sem("bias_set")
        exp_done = sem("exp_done")
        prob_set = sem("prob_set")
        pt_done = sem("pt_done")
        pt_v = sem("pt_evacuated_v")
        pt_a = sem("pt_evacuated_a")
        olat_set = sem("olat_set")
        uv_done = sem("uv_done")
        av_set = sem("av_set")
        x_new = sem("x_new")
        ln_sum = sem("ln_sum")
        ln_centered = sem("ln_centered")
        ln_sq = sem("ln_sq")
        ln_var = sem("ln_var")
        ln_norm = sem("ln_norm")
        ln_out = sem("ln_out")
        utok_set = sem("utok_set")
        ut_done = sem("ut_done")
        ut_free = [sem(f"ut_free{i}") for i in range(2)]
        gl_set = sem("gl_set")
        bc_in = sem("bc_in")
        cc_in = sem("cc_in")
        bt_set = sem("bt_set")
        bbd_set = sem("bbd_set")
        cp_set = sem("cp_set")
        btt_done = sem("btt_done")
        bmat_set = sem("bmat_set")
        kf_done = sem("kf_done")
        kf_set = sem("kf_set")
        t0_in = [sem(f"t0_in{i}") for i in range(2)]
        ub_set = sem("ub_set")
        in_done = sem("in_done")
        ang_set = sem("ang_set")
        trig5 = sem("trig5_set")
        z_set = sem("z_set")
        x5_set = sem("x5_set")
        td_set = sem("td_set")
        y_done = sem("y_done")
        y2_set = sem("y2_set")
        t1_done = sem("t1_done")
        ytok_set = sem("ytok_set")
        t2_done = sem("t2_done")
        yt_set = sem("yt_set")
        sg_set = sem("sigmoid_set")
        glu_set = sem("glu_set")
        sy_set = sem("s5_out_gated")
        sq_done = sem("sq_done")
        ms_done = sem("ms_done")
        xn_set = sem("xn_set")
        mem_in = sem("mem_in")
        mix_in = sem("mix_in")
        mem_set = sem("mem_set")
        memt_done = sem("memt_done")
        memt_set = sem("memt_set")
        pcol_set = sem("pool_in_set")
        uv_set = sem("uv_set")
        dpool_set = sem("dpool_set")
        pool_done = sem("pool_done")
        cat_set = sem("cat_set")
        vsq_set = sem("vsq_set")
        sgu_stat = sem("sgu_stat")
        vn_set = sem("vn_set")
        vt_done = sem("vt_done")
        vtok_set = sem("vtok_set")
        z_done = sem("z_done")
        kv2_set = sem("kv2_set")
        q2_set = sem("q2_set")
        s2_done = sem("s2_done")
        b2_set = sem("b2_set")
        e2_done = sem("e2_done")
        p2_set = sem("p2_set")
        p2t_done = sem("p2t_done")
        p2t_set = sem("p2t_set")
        o2_done = sem("o2_done")
        o2_set = sem("o2_set")
        h2_set = sem("h2_set")
        conv_in = sem("conv_in")
        conv_out = sem("conv_out")
        silu_set = sem("silu_set")
        ff_set = sem("ff_set")
        fin_t = sem("fin_transposed")
        fin_set = sem("fin_set")
        stored = sem("stored")
        pool_passed = sem("pool_passed")
        sp_passed = sem("sp_passed")
        pe_passed = sem("pe_passed")

        block = ctx.enter_context(nc.Block())

        RM = []
        PHASES = [("mod0", 12), ("mod1", 12), ("mla_head", 2), ("mla_gate", 8), ("mla_out", 8),
                  ("s5_u", 8), ("s5_g", 8), ("glu", 32), ("s5_out", 8), ("w_in", 6), ("wk", 4), ("wv", 4),
                  ("w_out", 4), ("wq", 4), ("wo", 4), ("w_up", 22), ("w_down", 12)]
        ring_at = {}
        n = 0
        for name, k in PHASES:
            ring_at[name] = n
            n += k
        UNITS = [("stage0", 12), ("mla_head", 2), ("mla_gate", 8), ("mla_out", 4), ("s5_u", 8), ("s5_g", 8),
                 ("glu", 16), ("s5_out", 4), ("w_in", 6), ("mem", 4), ("wk", 4), ("wv", 4), ("w_out", 4),
                 ("wq", 4), ("wo", 4), ("w_up", 22), ("w_down", 4)]
        unit_at = {}
        n = 0
        for name, k in UNITS:
            unit_at[name] = n
            n += k

        @contextmanager
        def turns(eng, lot, per):
            assert lot % per == 0
            with eng.Fori(0, lot // per) as t:
                yield Step(t, per)

        @block.sync
        def _(sp):
            sp.dma_start(cst[:, :], a["consts"]).then_inc(const_in, 16)
            sp.dma_start(xtok[:, 0:2, :], a["ctx"].rearrange("b (t p) d -> p (b t) d", p=P)).then_inc(x_in, 16)
            sp.dma_start(xtok[:, 2:4, :], a["x"].rearrange("b (t p) d -> p (b t) d", p=P)).then_inc(x_in, 16)
            sp.wait_ge(vec_clear, 1)
            for t, names in enumerate(VEC_TILES):
                r = 0
                for name, rows in names:
                    v = a[name]
                    v = v.rearrange({1: "(r p) -> r p", 2: "l (r p) -> (l r) p", 3: "l k (r p) -> (l k r) p"}[len(v.shape)], p=P)
                    first = min(rows, P - r)
                    sp.dma_start(vrow[r:r + first, t, :], v[0:first, :]).then_inc(vec_in, 16)
                    if rows > first:
                        sp.dma_start(vrow[0:rows - first, t + 1, :], v[first:rows, :]).then_inc(vec_in, 16)
                    r += rows

            def load(slot, src):
                sp.dma_start(ring[:, slot, 0:src.shape[1], 0:src.shape[2]], src).then_inc(w_in_[slot], 16)

            def rows8(w, kg, c0, n=MT2, k=8):
                return w[kg * 8 * P:(kg * 8 + k) * P, bass.ds(c0, n)].rearrange("(c p) m -> p c m", p=P)

            wm = a["w_mod"]
            for s in range(NSLOT):
                load(s, rows8(wm[0], 0, s * MT2))
            for z, n in ((0, "s5_lam_re"), (1, "s5_lam_im")):
                sp.dma_start(lam_rows[:, z, :], a[n][0].rearrange("d (q g) s -> (d q) (g s)", g=2)).then_inc(s5par_in, 16)
            sp.dma_start(dt_raw, a["s5_log_dt"][0].rearrange("d (q g) -> (d q) g", g=2)).then_inc(s5par_in, 16)
            sp.dma_start(d_raw, a["s5_d"][0].rearrange("(g c) -> g c", c=CH5)).then_inc(s5par_in, 16)
            for z, n in ((0, "s5_b_re"), (1, "s5_b_im")):
                sp.dma_start(raw_b[:, z, :], a[n][0].rearrange("d (q g) s c -> (d q) (g s c)", g=2)).then_inc(s5par_in, 16)
            for z, n in ((0, "s5_c_re"), (1, "s5_c_im")):
                for g in range(2):
                    sp.dma_start(raw_c[:, z, :].rearrange("p (c g s) -> p c g s", c=CH5, g=2)[:, :, g, :],
                                 a[n][0].rearrange("d (q g) c s -> g (d q) c s", g=2)[g]).then_inc(s5par_in, 16)
            with turns(sp, 8, 4) as i:
                for s in range(NSLOT):
                    sp.wait_ge(slot_done, i + s + 1)
                    sp.sem_inc(sp_passed, 1)
                    load(s, rows8(wm[0], 0, (i + (s + 4)) * MT2))
            at = ring_at["mod1"]
            with turns(sp, 12, 4) as i:
                for s in range(NSLOT):
                    sp.wait_ge(slot_done, i + (at + s - NSLOT + 1))
                    sp.sem_inc(sp_passed, 1)
                    load(s, rows8(wm[1], 0, (i + s) * MT2))

            def stream(name, w, groups, units, last=8):
                at = ring_at[name]
                lot = groups * units
                whole = lot // NSLOT * NSLOT if NSLOT % groups == 0 else 0
                if whole > NSLOT:
                    with turns(sp, whole, NSLOT) as i:
                        for s in range(NSLOT):
                            sp.wait_ge(slot_done, i + (at + s - NSLOT + 1))
                            sp.sem_inc(sp_passed, 1)
                            c0 = (i + s) * MT2 if groups == 1 else i * (MT2 // groups) + s // groups * MT2
                            load((at + s) % NSLOT, rows8(w, s % groups, c0))
                else:
                    whole = 0
                for s in range(whole, lot):
                    sp.wait_ge(slot_done, at + s - NSLOT + 1)
                    kg = s % groups
                    load((at + s) % NSLOT, rows8(w, kg, s // groups * MT2, k=last if kg == groups - 1 else 8))

            wi = a["mla_w_in"][0]
            at = ring_at["mla_head"]
            for s, n in ((0, QR), (1, KVR + ROPE)):
                sp.wait_ge(slot_done, at + s - NSLOT + 1)
                load((at + s) % NSLOT, rows8(wi, 0, s * QR, n))
            stream("mla_gate", wi[:, QR + KVR + ROPE:], 1, 8)

            def load_heads(p, b):
                for c in range(2):
                    src = a["mla_w_uq"][0][c * P:(c + 1) * P, bass.ds(p * (2 * HQ), 2 * HQ)].rearrange("p (h m) -> p h m", h=2)
                    for lo, n, to in ((0, NOPE, 0), (NOPE, ROPE, 2 * NOPE)):
                        sp.dma_start(att_uq[b][:, c, to:to + 2 * n].rearrange("p (h m) -> p h m", h=2), src[:, :, lo:lo + n])\
                            .then_inc(att_in[b], 16)
                sp.dma_start(att_uk[b], a["mla_w_uk"][0].rearrange("c h d -> c (h d)")[:, bass.ds(p * (2 * NOPE), 2 * NOPE)])\
                    .then_inc(att_in[b], 16)
                sp.dma_start(att_uv[b], a["mla_w_uv"][0].rearrange("c h d -> c (h d)")[:, bass.ds(p * (2 * VDIM), 2 * VDIM)])\
                    .then_inc(att_in[b], 16)

            sp.wait_ge(bc_spilled, 32)
            sp.wait_ge(par_got, 6)
            for p in range(2):
                load_heads(p, p)
            with turns(sp, 6, 2) as i:
                for b in range(2):
                    sp.wait_ge(uv_done, i * 2 + (2 * b + 2))
                    sp.sem_inc(sp_passed, 1)
                    load_heads(i + (b + 2), b)
            stream("mla_out", a["mla_w_out"][0], 2, 4)
            w5 = a["s5_w_in"][0]
            stream("s5_u", w5[:, 0:E_BR], 1, 8)
            stream("s5_g", w5[:, E_BR:2 * E_BR], 1, 8)

            def load_bc(b):
                sp.dma_start(bb.rearrange("p z d q c -> p (z d) (q c)"),
                             spill_b[:, :, bass.ds(b * (BLK * CH5), BLK * CH5)]).then_inc(bc_in, 16)
                sp.dma_start(cc.rearrange("p z d q c -> p (z d) (q c)"),
                             spill_c[:, :, bass.ds(b * (BLK * CH5), BLK * CH5)]).then_inc(cc_in, 16)

            def spread(par):
                for s in range(L5):
                    for g in range(2):
                        lo = (L5 - 1 - s) * CH5
                        sp.dma_start(t0[par][s * CH5:(s + 1) * CH5, :, g, :],
                                     kf[g * CH5:(g + 1) * CH5, :, lo:lo + P]).then_inc(t0_in[par], 16)

            sp.wait_ge(av_set, HEADS)
            load_bc(0)
            sp.wait_ge(kf_set, 2)
            spread(0)
            sp.wait_ge(bt_set, 2)
            sp.wait_ge(bbd_set, 1)
            sp.wait_ge(cp_set, 1)
            load_bc(1)
            with turns(sp, 14, 2) as i:
                for par in range(2):
                    sp.wait_ge(kf_set, i * 2 + (2 * par + 4))
                    sp.sem_inc(sp_passed, 1)
                    spread((par + 1) % 2)
                    sp.wait_ge(bt_set, i * 2 + (2 * par + 4))
                    sp.sem_inc(sp_passed, 1)
                    sp.wait_ge(bbd_set, i + (par + 2))
                    sp.sem_inc(sp_passed, 1)
                    sp.wait_ge(cp_set, i + (par + 2))
                    sp.sem_inc(sp_passed, 1)
                    load_bc(i + (par + 2))
            sp.wait_ge(kf_set, 2 * NB5)
            spread(1)

            wg = a["s5_w_glu"][0]
            at = ring_at["glu"]
            with turns(sp, 32, NSLOT) as i:
                for s in range(NSLOT):
                    sp.wait_ge(slot_done, i + (at + s - NSLOT + 1))
                    sp.sem_inc(sp_passed, 1)
                    load((at + s) % NSLOT, rows8(wg, s % 2, i * (MT2 // 4) + s // 2 * E_BR))
            stream("s5_out", a["s5_w_out"][0], 2, 4)
            stream("w_in", a["w_in_2"][0], 1, 6)
            sp.wait_ge(yt_set, NB5 + 1)
            sp.wait_ge(glu_set, 18)
            sp.dma_start(mem_tok, a["mem_2"].rearrange("b (t p) d -> p (b t) d", p=P)).then_inc(mem_in, 16)
            sp.dma_start(pool_w, a["pool_w_2"][0].rearrange("g c d -> c g d")).then_inc(mix_in, 16)
            sp.dma_start(sgu_w, a["sgu_w_2"][0].rearrange("h t s -> t h s")).then_inc(mix_in, 16)
            sp.dma_start(sgu_bb.rearrange("p h t -> p (h t)"),
                         a["sgu_b_2"][0].rearrange("h t -> (h t)").partition_broadcast(P)).then_inc(mix_in, 16)
            stream("wk", a["wk_2"][0], 1, 4)
            stream("wv", a["wv_2"][0], 1, 4)
            stream("w_out", a["w_out_2"][0], 1, 4)
            stream("wq", a["wq_2"][0], 1, 4)
            stream("wo", a["wo_2"][0], 1, 4)
            wu = a["w_up_2"][0]
            at = ring_at["w_up"]
            with turns(sp, 20, NSLOT) as i:
                for s in range(NSLOT):
                    sp.wait_ge(slot_done, i + (at + s - NSLOT + 1))
                    sp.sem_inc(sp_passed, 1)
                    load((at + s) % NSLOT, rows8(wu, 0, i * (MT2 // 2) + (s // 2 * MT2 + s % 2 * FF)))
            for s in range(20, 22):
                sp.wait_ge(slot_done, at + s - NSLOT + 1)
                load((at + s) % NSLOT, rows8(wu, 0, s // 2 * MT2 + s % 2 * FF))
            stream("w_down", a["w_down_2"][0], 3, 4, last=KF - 16)
            sp.wait_ge(fin_set, 4)
            sp.dma_start(out.rearrange("b (t p) d -> p (b t) d", p=P), orow).then_inc(stored, 16)
            sp.wait_ge(stored, 16)

        @block.tensor
        def _(pe):
            def free(u):
                return unit_free[u % 2], 2 * (u // 2)

            pe.wait_ge(const_in, 16)
            pe.wait_ge(vec_in, 16 * (sum(len(t) for t in VEC_TILES) + 1))
            for t in range(NVT):
                mm = pe.transpose(psum[4][:, t * P:(t + 1) * P], vrow[:, t, :], ident)
            mm.then_inc(vec_t, 1)
            pe.wait_ge(x_in, 32)
            for k in range(KD):
                u = k // 2
                if u >= 2 and k % 2 == 0:
                    pe.wait_ge(*free(u))
                for t in range(4):
                    mm = pe.transpose(psum[2 * (u % 2) + k % 2][:, t * P:(t + 1) * P],
                                      xtok[:, t, k * P:(k + 1) * P], ident)
                mm.then_inc(p0_t, 1)
            pe.wait_ge(s5par_in, 10 * 16)
            pe.wait_ge(dt_set, 2)
            for z in range(2):
                pe.transpose(psum[5][:, z * P:(z + 1) * P], lam_rows[:, z, :], ident)
            pe.transpose(psum[5][:, 2 * P:3 * P], dt_exp.rearrange("p g s -> p (g s)"), ident)
            pe.transpose(psum[5][:, 3 * P:4 * P], d_rows.rearrange("p t c -> p (t c)"), ident).then_inc(par_t, 1)
            for f in range(16):
                u = 4 + f // 2
                if f % 2 == 0:
                    pe.wait_ge(*free(u))
                z, c4 = f // 4, f % 4
                for j in range(4):
                    c = 4 * c4 + j
                    if z < 2:
                        src = raw_b[:, z, :].rearrange("p (r c) -> p c r", c=CH5)[:, c, :]
                    else:
                        src = raw_c[:, z - 2, c * 2 * ST5:(c + 1) * 2 * ST5]
                    mm = pe.transpose(psum[2 * (u % 2) + f % 2][:, j * P:(j + 1) * P], src, ident)
                mm.then_inc(p0_t, 1)

            pe.wait_ge(cond_set, 2)
            for l, name in enumerate(("mod0", "mod1")):
                at = ring_at[name]
                with turns(pe, 12, NSLOT) as i:
                    for s in range(NSLOT):
                        pe.wait_ge(w_in_[s], i * 4 + (16 * (at // NSLOT) + 16))
                        for m in range(2):
                            o = psum[6 + l][:, bass.ds(i * 4 + (4 * s + 2 * m), 2)]
                            for k in range(KD):
                                mm = pe.matmul(o, ring[:, s, k, m * P:(m + 1) * P], cond[:, k, :],
                                               start=(k == 0), stop=(k == KD - 1))
                        mm.then_inc(slot_done, 1)

            def linear(name, groups, units, moving, last=8):
                at, u0 = ring_at[name], unit_at[name]
                lot = groups * units

                def step(i, s, upt):
                    sl = (at + s) % NSLOT
                    u = u0 + s // groups
                    kg = s % groups
                    pe.wait_ge(w_in_[sl], i * (16 // NSLOT) + (16 * ((at + s) // NSLOT) + 16))
                    if kg == 0:
                        pe.wait_ge(unit_free[u % 2], i * (upt // 4 if upt % 4 == 0 else 0) + 2 * (u // 2)
                                   if upt != 2 else i // 2 + 2 * (u // 2))
                    for m in range(2):
                        nk = last if kg == groups - 1 else 8
                        for k in range(nk):
                            mv = moving(kg * 8 + k)
                            mm = pe.matmul(psum[2 * (u % 2) + m][:, 0:mv.free_size()], ring[:, sl, k, m * P:(m + 1) * P], mv,
                                           start=(kg == 0 and k == 0), stop=(kg == groups - 1 and k == nk - 1))
                    mm.then_inc(slot_done, 1)

                whole = lot // NSLOT * NSLOT if NSLOT % groups == 0 else 0
                if whole > NSLOT:
                    assert u0 % 2 == 0 and whole % NSLOT == 0
                    with turns(pe, whole, NSLOT) as i:
                        for s in range(NSLOT):
                            sl = (at + s) % NSLOT
                            u = u0 + s // groups
                            kg = s % groups
                            pe.wait_ge(w_in_[sl], i * 4 + (16 * ((at + s) // NSLOT) + 16))
                            if kg == 0:
                                pe.wait_ge(unit_free[u % 2], (i if groups == 1 else i // 2) + 2 * (u // 2))
                            for m in range(2):
                                for k in range(8):
                                    mv = moving(kg * 8 + k)
                                    mm = pe.matmul(psum[2 * (u % 2) + m][:, 0:mv.free_size()],
                                                   ring[:, sl, k, m * P:(m + 1) * P], mv,
                                                   start=(kg == 0 and k == 0), stop=(kg == groups - 1 and k == 7))
                            mm.then_inc(slot_done, 1)
                else:
                    whole = 0
                for s in range(whole, lot):
                    step(0, s, 4)

            pe.wait_ge(h_ctx, KD)
            pe.wait_ge(h_lat, KD)
            at, u0 = ring_at["mla_head"], unit_at["mla_head"]
            for s in range(2):
                sl = (at + s) % NSLOT
                pe.wait_ge(w_in_[sl], 16 * ((at + s) // NSLOT) + 16)
                pe.wait_ge(*free(u0 + s))
                for m in range(2):
                    M = ROPE if s == 1 and m == 1 else P
                    for k in range(KD):
                        mm = pe.matmul(psum[2 * s + m][0:M, :], ring[:, sl, k, m * P:m * P + M], ht[:, k, :],
                                       start=(k == 0), stop=(k == KD - 1))
                mm.then_inc(slot_done, 1)
            linear("mla_gate", 1, 8, lambda k: ht[:, k, :])
            pe.wait_ge(sq_set, 3)
            pe.matmul(psum[4][:, :], avg_q[:, :], sq1[:, 0, :], start=True, stop=False)
            pe.matmul(psum[4][:, :], avg_q[:, :], sq1[:, 1, :], start=False, stop=True).then_inc(stat, 1)
            pe.matmul(psum[5][:, :], avg_kv[:, :], sq1[:, 2, :], start=True, stop=True).then_inc(stat, 1)
            pe.matmul(psum[7][:, 0:S], rot, kr[:, S:T], start=True, stop=True).then_inc(stat, 1)
            pe.wait_ge(normed, 3)
            for t in range(4):
                mm = pe.transpose(psum[6][:, t * P:(t + 1) * P], ckv[:, t * P:(t + 1) * P], ident)
            mm.then_inc(ctok_t, 1)
            pe.wait_ge(ctok_set, 1)
            pe.wait_ge(normed, 4)

            PROJ0, PROJN = 8, 10

            class Proj:
                def __init__(self, pair, fill0):
                    self.p, self.f, self.f0 = pair, 0, fill0

                def bank(self):
                    b = self.f % 2
                    uses = self.f0 // 2 + self.f // 2
                    pe.wait_ge(proj_free[b], self.p * (PROJN // 2) + uses)
                    self.f += 1
                    return psum[b]

            def project(pr, b, h0_wait, pair):
                pe.wait_ge(att_in[b], h0_wait)
                bank = pr.bank()
                for c in range(2):
                    mm = pe.matmul(bank[:, :], att_uq[b][:, c, 2 * NOPE:2 * HQ],
                                   qn[:, c, :], start=(c == 0), stop=(c == 1))
                mm.then_inc(proj_done, 1)
                bank = pr.bank()
                pe.wait_ge(qk_set, pair * 5 + 1)
                pe.matmul(bank[:, 0:S], rot, q_rope[:, S:T], start=True, stop=True).then_inc(proj_done, 1)
                for h in range(2):
                    bank = pr.bank()
                    for c in range(2):
                        mm = pe.matmul(bank[:, :], att_uq[b][:, c, h * NOPE:(h + 1) * NOPE], qn[:, c, :],
                                       start=(c == 0), stop=(c == 1))
                    mm.then_inc(proj_done, 1)
                    bank = pr.bank()
                    pe.matmul(bank[:, :], att_uk[b][:, h * NOPE:(h + 1) * NOPE], ckv, start=True, stop=True)\
                        .then_inc(proj_done, 1)

            def scores(pair, e, first):
                pe.wait_ge(qk_set, pair * 5 + (3 + 2 * e))
                pe.wait_ge(qrot_set, pair + 1)
                r = slice(e * ROPE, (e + 1) * ROPE)
                for t in range(4):
                    if not first:
                        pe.wait_ge(exp_done, pair * 8 + (4 * e + t - 3))
                    tok = slice(t * P, (t + 1) * P)
                    bank = psum[2 + t]
                    if t < 2:
                        pe.matmul(bank[:, 0:S], qh[e][:, tok], kh[e][:, 0:S], start=True, stop=False)
                        mm = pe.matmul(bank[:, 0:S], q_rope[r, tok], kr[r, 0:S], start=False, stop=True)
                    else:
                        pe.matmul(bank[:, 0:S], qh[e][:, tok], kh[e][:, 0:S], start=True, stop=False)
                        pe.matmul(bank[:, 0:S], q_rope[r, tok], kr[r, 0:S], start=False, stop=True)
                        pe.matmul(bank[:, S:T], qh[e][:, tok], kh[e][:, S:T], start=True, stop=False)
                        mm = pe.matmul(bank[:, S:T], q_rot[r, (t - 2) * P:(t - 1) * P], kr_rot[r, :], start=False, stop=True)
                    mm.then_inc(score_done, 1)

            def values(pr, pair, e, b, first):
                for f in range(3):
                    bank = psum[6 + (3 * e + f) % 2]
                    if not (first and f < 2):
                        if f == 2:
                            pe.wait_ge(pt_v, pair * 2 + (e + 1))
                        else:
                            pe.wait_ge(pt_a, pair * 4 + (2 * e + f - 1))
                    for t in ((0, 1), (2,), (3,))[f]:
                        pe.wait_ge(prob_set, pair * 8 + (4 * e + t + 1))
                        nk = 2 if t < 2 else 4
                        for k in range(nk):
                            at = (t * 2 + k) if t < 2 else k
                            mm = pe.transpose(bank[:, at * P:(at + 1) * P], prob[e][:, t, k * P:(k + 1) * P], ident)
                    mm.then_inc(pt_done, 1)
                bank = pr.bank()
                pe.wait_ge(pt_v, pair * 2 + (e + 1))
                for k in range(2):
                    pe.matmul(bank[:, 0:S], ckv_tok[:, k, :], pt_ctx[:, :, k, :], start=(k == 0), stop=(k == 1))
                pe.wait_ge(pt_a, pair * 4 + (2 * e + 2))
                for k in range(4):
                    mm = pe.matmul(bank[:, S:T], ckv_tok[:, k, :], pt_lat[:, :, k, :], start=(k == 0), stop=(k == 3))
                mm.then_inc(proj_done, 1)
                bank = pr.bank()
                pe.wait_ge(olat_set, pair * 2 + (e + 1))
                pe.matmul(bank[:, :], att_uv[b][:, e * VDIM:(e + 1) * VDIM], o_lat, start=True, stop=True).then_inc(uv_done, 1)

            pr = Proj(0, 0)
            project(pr, 0, 96, 0)
            scores(0, 0, True)
            scores(0, 1, False)
            values(pr, 0, 0, 0, True)

            def pair_step(p, b, wait_in):
                pr = Proj(p, PROJ0 - PROJN)
                project(pr, b, wait_in, p)
                scores(p, 0, False)
                values(pr, p - 1, 1, 1 - b, False)
                scores(p, 1, False)
                values(pr, p, 0, b, False)

            pair_step(1, 1, 96)
            with turns(pe, 6, 2) as i:
                for b in range(2):
                    pair_step(i + (b + 2), b, i * 48 + 192)
            pr = Proj(PAIRS, PROJ0 - PROJN)
            values(pr, PAIRS - 1, 1, 1, False)

            def layer_sums(n, with_ctx, base_new):
                pe.wait_ge(x_new, base_new)
                halves = ([(xc, 0)] if with_ctx else []) + [(xl, S)]
                for x, lo in halves:
                    for k in range(KD):
                        mm = pe.matmul(psum[4][:, lo:lo + S], avg_d[:, :], x[:, k, :], start=(k == 0), stop=(k == KD - 1))
                mm.then_inc(ln_sum, 1)
                for h, (x, lo) in enumerate(halves):
                    pe.wait_ge(ln_sq, n + h + 1)
                    for k in range(KD):
                        mm = pe.matmul(psum[5][:, lo:lo + S], avg_d[:, :], ht[:, k, lo:lo + S], start=(k == 0),
                                       stop=(k == KD - 1))
                mm.then_inc(ln_var, 1)

            pe.wait_ge(av_set, HEADS)
            linear("mla_out", 2, 4, lambda k: gate[:, k, :])
            layer_sums(0, True, 16)

            pe.wait_ge(h_ctx, 2 * KD)
            pe.wait_ge(h_lat, 2 * KD)
            at, u0 = ring_at["s5_u"], unit_at["s5_u"]
            for q in range(2):
                pe.sem_inc(ut_free[q], 4)
            with turns(pe, 8, NSLOT) as i:
                for s in range(NSLOT):
                    sl = (at + s) % NSLOT
                    u = u0 + s
                    pe.wait_ge(w_in_[sl], i * 4 + (16 * ((at + s) // NSLOT) + 16))
                    pe.wait_ge(unit_free[u % 2], i + 2 * (u // 2))
                    for s4 in range(4):
                        for k in range(KD):
                            mm = pe.matmul(psum[2 * (u % 2) + s4 // 2][:, s4 % 2 * S:(s4 % 2 + 1) * S],
                                           ht[:, k, s4 * P:(s4 + 1) * P], ring[:, sl, k, :], start=(k == 0), stop=(k == KD - 1))
                    mm.then_inc(slot_done, 1)
                    pe.wait_ge(utok_set, i * 2 + (2 * s + 2))
                    for q in range(2):
                        pe.wait_ge(ut_free[q], i * 4 + (4 * s + 4))
                        for j in range(4):
                            g = (4 * q + j) * 2
                            mm = pe.transpose(psum[4 + q][:, j * P:(j + 1) * P],
                                              utok[:, g:g + 2, :, :].rearrange("p g s c -> p (g s c)"), ident)
                        mm.then_inc(ut_done, 1)
            linear("s5_g", 1, 8, lambda k: ht[:, k, :].rearrange("p (j c) -> p j c", c=NC5)[:, :, NCL:NC5])

            def tables(b):
                pe.wait_ge(bt_set, b * 2 + 2)
                for z in range(2):
                    for d in range(2):
                        f = 2 * z + d
                        pe.wait_ge(bmat_set, b * 4 + max(f - 1, 0))
                        for q in range(BLK):
                            mm = pe.transpose(psum[d][:, q * P:(q + 1) * P], bt[:, z, d, q, :, :].rearrange("p s c -> p (s c)"), ident)
                        mm.then_inc(btt_done, 1)

            def responses(b, par):
                pe.wait_ge(cp_set, b + 1)
                pe.wait_ge(bbd_set, b + 1)
                for f in range(2):
                    pe.wait_ge(kf_set, b * 2 + f)
                    for j in range(2):
                        q = 2 * f + j
                        o = psum[2 + f][0:2 * CH5, j * KW5:(j + 1) * KW5]
                        for n, (d, z) in enumerate(((1, 0), (1, 1), (0, 0), (0, 1))):
                            lo = 0 if d == 1 else (L5 - 1) * CH5
                            mm = pe.matmul(o[:, lo:lo + P], bbd[:, z, d, q, :, :].rearrange("p g c -> p (g c)"),
                                           cp[par][:, z, d, q, :, :].rearrange("p i c -> p (i c)")[:, d * CH5:d * CH5 + P],
                                           start=(n == 0), stop=(n == 3), skip_group_check=True)
                    mm.then_inc(kf_done, 1)

            def inputs(b):
                pe.wait_ge(bmat_set, b * 4 + 4)
                pe.wait_ge(ub_set, b + 1)
                pe.wait_ge(yt_set, b + 1)
                for z in range(2):
                    for d in range(2):
                        for q in range(BLK):
                            for g in range(2):
                                mv = ub[:, q, g, :].rearrange("p (h c) -> p h c", h=2)
                                if d == 1:
                                    mv = mv[:, :, ::-1]
                                mm = pe.matmul(psum[4 + z][g * ST5:(g + 1) * ST5, (d * BLK + q) * NC5:(d * BLK + q + 1) * NC5],
                                               bmat[:, z, d, q, g * ST5:(g + 1) * ST5], mv, start=True, stop=True)
                    mm.then_inc(in_done, 1)

            def outputs(b, par, n_use):
                pe.wait_ge(t0_in[par], n_use)
                pe.wait_ge(x5_set, b * 2 + 2)
                for g in range(2):
                    r = slice(g * ST5, (g + 1) * ST5)
                    for q in range(BLK):
                        o = psum[6 + g][:, q * NCL:(q + 1) * NCL]
                        pe.matmul(o, t0[par][:, q, g, :], ub[:, q, g, NCL:NC5], start=True, stop=False)
                        for d in range(2):
                            for z, x in enumerate((xr5, xi5)):
                                mv = x[r, d, q, :]
                                if d == 1:
                                    mv = mv[:, ::-1]
                                lo = CH5 if d == 0 else 0
                                mm = pe.matmul(o, cp[par][r, z, d, q, :, :].rearrange("p i c -> p (i c)")[:, lo:lo + P], mv,
                                               start=False, stop=(d == 1 and z == 1))
                mm.then_inc(y_done, 1)

            def back(b):
                pe.wait_ge(y2_set, b * 4 + 8)
                for j in range(2):
                    mm = pe.transpose(psum[4][:, j * P:(j + 1) * P],
                                      y2[:, 2 * j:2 * j + 2, :, :].rearrange("p q h c -> p (q h c)"), ident)
                mm.then_inc(t1_done, 1)
                pe.wait_ge(ytok_set, b * 4 + 4)
                pe.sem_inc(pe_passed, 1)
                for s4 in range(4):
                    mm = pe.transpose(psum[5][:, s4 * 64:(s4 + 1) * 64], ytok[0:64, s4, :], ident[0:64, 0:64])
                mm.then_inc(t2_done, 1)

            pe.sem_inc(yt_set, 1)
            for q in range(2):
                pe.wait_ge(unit_free[q], unit_at["glu"])
            tables(0)
            responses(0, 0)
            with turns(pe, 14, 2) as i:
                for par in range(2):
                    inputs(i + par)
                    tables(i + (par + 1))
                    responses(i + (par + 1), 1 - par)
                    outputs(i + par, par, i * 128 + 256)
                    back(i + par)
            inputs(14)
            tables(15)
            responses(15, 1)
            outputs(14, 0, 256 * 8)
            back(14)
            inputs(15)
            outputs(15, 1, 256 * 8)
            back(15)

            pe.wait_ge(yt_set, NB5 + 1)
            at, u0 = ring_at["glu"], unit_at["glu"]
            with turns(pe, 32, NSLOT) as i:
                for s in range(NSLOT):
                    sl = (at + s) % NSLOT
                    u, kg = u0 + s // 2, s % 2
                    pe.wait_ge(w_in_[sl], i * 4 + (16 * ((at + s) // NSLOT) + 16))
                    if kg == 0:
                        pe.wait_ge(unit_free[u % 2], i // 2 + 2 * (u // 2))
                    for m in range(2):
                        for k in range(8):
                            mm = pe.matmul(psum[2 * (u % 2) + m][:, 0:S], ring[:, sl, k, m * P:(m + 1) * P],
                                           yt[:, kg * 8 + k, :], start=(kg == 0 and k == 0), stop=(kg == 1 and k == 7))
                    mm.then_inc(slot_done, 1)
            pe.wait_ge(glu_set, 18)
            linear("s5_out", 2, 4, lambda k: gl[:, k, :])
            layer_sums(2, False, 16 + 8)

            def mean_square(n):
                pe.wait_ge(sq_done, n + 1)
                for k in range(KD):
                    mm = pe.matmul(psum[4][:, 0:S], avg_d[:, :], sq[:, k, :], start=(k == 0), stop=(k == KD - 1))
                mm.then_inc(ms_done, 1)

            mean_square(0)
            pe.wait_ge(xn_set, 1)
            linear("w_in", 1, 6, lambda k: xn[:, k, :])
            pe.wait_ge(mem_set, 2)
            u0 = unit_at["mem"]
            for k in range(KD):
                u = u0 + k // 2
                if k % 2 == 0:
                    pe.wait_ge(*free(u))
                for t in range(2):
                    mm = pe.transpose(psum[2 * (u % 2) + k % 2][:, t * P:(t + 1) * P], mem_tok[:, t, k * P:(k + 1) * P], ident)
                mm.then_inc(memt_done, 1)
            pe.wait_ge(mix_in, 48)
            pe.wait_ge(dpool_set, 4)
            for g in range(4):
                mm = pe.matmul(psum[6 + g // 2][:, g % 2 * S:(g % 2 + 1) * S], pool_w[:, g, :], pp[1][:, g, 16:16 + S],
                               start=True, stop=True)
            mm.then_inc(pool_done, 1)
            for h in range(4):
                mm = pe.transpose(psum[5][:, h * P:(h + 1) * P], sgu_w[:, h, :], ident)
            mm.then_inc(sgu_stat, 1)
            pe.wait_ge(uv_set, 8)
            for k in range(4):
                mm = pe.matmul(psum[4][:, 0:S], avg_sgu[:, :], vv[:, k, :], start=(k == 0), stop=(k == 3))
            mm.then_inc(sgu_stat, 1)
            pe.wait_ge(vsq_set, 1)
            for k in range(4):
                mm = pe.matmul(psum[4][:, S:T], avg_sgu[:, :], sq[:, k, :], start=(k == 0), stop=(k == 3))
            mm.then_inc(sgu_stat, 1)
            pe.wait_ge(memt_set, KD)
            linear("wk", 1, 4, lambda k: mem_t[:, k, :])
            at, u0 = ring_at["wv"], unit_at["wv"]
            for s in range(4):
                sl = (at + s) % NSLOT
                pe.wait_ge(w_in_[sl], 16 * ((at + s) // NSLOT) + 16)
                pe.wait_ge(*free(u0 + s))
                for m in range(2):
                    for k in range(KD):
                        mm = pe.matmul(psum[2 * ((u0 + s) % 2) + m][:, 0:MT2], mem_t[:, k, m * P:(m + 1) * P], ring[:, sl, k, :],
                                       start=(k == 0), stop=(k == KD - 1))
                mm.then_inc(slot_done, 1)
            pe.wait_ge(vn_set, 4)
            pe.wait_ge(cat_set, 4)
            for t in range(2):
                for k in range(4):
                    mm = pe.transpose(psum[6 + t][:, k * P:(k + 1) * P], vv[:, k, t * P:(t + 1) * P], ident)
                mm.then_inc(vt_done, 1)
            pe.wait_ge(vtok_set, 2)
            for h in range(4):
                for t in range(2):
                    mm = pe.matmul(psum[6 + h // 2][:, (h % 2) * S + t * P:(h % 2) * S + (t + 1) * P],
                                   vtok[:, t, h * P:(h + 1) * P], sgu_wt[:, h, :], start=True, stop=True)
            mm.then_inc(z_done, 1)
            pe.wait_ge(cat_set, 8)
            linear("w_out", 1, 4, lambda k: cat[:, k, :])
            mean_square(1)
            pe.wait_ge(xn_set, 2)
            linear("wq", 1, 4, lambda k: xn[:, k, :])
            pe.wait_ge(kv2_set, 16)
            pe.wait_ge(q2_set, 8)

            def scores2(h):
                for t in range(2):
                    if h >= 1:
                        pe.wait_ge(e2_done, 2 * h - 1 + t)
                    for c in range(2):
                        mm = pe.matmul(psum[4 + t][:, 0:S], q2[:, 2 * h + c, t * P:(t + 1) * P], k2[:, 2 * h + c, :],
                                       start=(c == 0), stop=(c == 1))
                    mm.then_inc(s2_done, 1)

            def values2(h):
                if h >= 1:
                    pe.wait_ge(p2t_set, h)
                for t in range(2):
                    pe.wait_ge(p2_set, 2 * h + t + 1)
                    for m in range(2):
                        mm = pe.transpose(psum[6][:, (2 * m + t) * P:(2 * m + t + 1) * P], prob2[:, h % 2, t, m * P:(m + 1) * P], ident)
                mm.then_inc(p2t_done, 1)
                pe.wait_ge(p2t_set, h + 1)
                if h >= 1:
                    pe.wait_ge(o2_set, h)
                for c in range(2):
                    for m in range(2):
                        mm = pe.matmul(psum[7][:, c * S:(c + 1) * S], v2[:, m, (2 * h + c) * P:(2 * h + c + 1) * P], prob2_t[:, m, :],
                                       start=(m == 0), stop=(m == 1))
                mm.then_inc(o2_done, 1)

            scores2(0)
            for h in range(XH):
                if h + 1 < XH:
                    scores2(h + 1)
                values2(h)
            pe.wait_ge(o2_set, XH)
            linear("wo", 1, 4, lambda k: o2[:, k, :])
            mean_square(2)
            pe.wait_ge(xn_set, 3)
            linear("w_up", 1, 22, lambda k: xn[:, k, :])
            pe.wait_ge(ff_set, KF + 2)
            linear("w_down", 3, 4, lambda k: ff[:, k, :], last=KF - 16)
            mean_square(3)
            pe.wait_ge(xn_set, 4)
            for t in range(2):
                for f in range(2):
                    for j in range(4):
                        mm = pe.transpose(psum[2 * t + f][:, j * P:(j + 1) * P], xn[:, 4 * f + j, t * P:(t + 1) * P], ident)
                    mm.then_inc(fin_t, 1)

        @block.scalar
        def _(act):
            link = Link(act, a_link)
            def root(o, mean, scale=1.0):
                act.activation(o, mean, ACT.Sqrt, bias=eps, scale=scale).then_inc(root_set, 1)

            act.wait_ge(vec_out, 1)
            for j, name in enumerate(("c_ctx", "c")):
                act.activation(cond[:, :, j], col[:, at_col[name]:at_col[name] + KD], ACT.Silu).then_inc(cond_set, 1)
            for k in range(1, KD, 2):
                act.wait_ge(p0_t, k + 1)
                act.copy(xc[:, k, :], psum[2 * (k // 2 % 2) + 1][:, 0:S]).then_inc(xt_act, 1)
                act.copy(xl[:, k, :], psum[2 * (k // 2 % 2) + 1][:, S:T]).then_inc(xt_act, 1)
                act.wait_ge(xt_act, k + 1)
                act.sem_inc(unit_free[k // 2 % 2], 1)
            for f in range(16):
                act.wait_ge(p0_t, KD + f + 1)
                z, c4 = f // 4, f % 4
                dst = (bcol if z < 2 else ccol)[:, z % 2, :, 4 * c4:4 * c4 + 4].rearrange("p q c -> p c q")
                u = 4 + f // 2
                src = psum[2 * (u % 2) + f % 2][:, :].rearrange("p (c q) -> p c q", c=4)
                act.mul(dst, src, -1.0 if z == 3 else 1.0).then_inc(unit_free[u % 2], 1)
            act.wait_ge(arg_set, 1)
            act.activation(pars[4], pars[3], ACT.Tanh, scale=0.5).then_inc(act_tanh, 1)
            act.wait_ge(arg_set, 2)
            act.activation(pars[6], pars[5], ACT.Sin, scale=0.5).then_inc(act_trig, 1)
            link(act.activation(pars[7], pars[5], ACT.Abs))
            act.activation(pars[7], pars[7], ACT.Sin, scale=-0.5, bias=half_pi).then_inc(act_trig, 1)

            def modulate(l):
                for k in range(KD):
                    o, x = ht[:, k, 0:S], xc[:, k, :]
                    if l == 1:
                        o = by_chunk(ht[:, k, :])[:, 0:NCL]
                        x = x.rearrange("p (c h s) -> p c h s", h=2, s=4)
                    act.activation(o, x, ACT.Identity, bias=mod[:, l, k, 0:1],
                                   scale=mod[:, l, KD + k, 0:1]).then_inc(h_ctx, 1)

            act.wait_ge(mod_set, 2)
            act.wait_ge(xt_dve, KD)
            act.wait_ge(xt_act, KD)
            modulate(0)
            for j in range(2):
                act.wait_ge(qkv_copied, j + 1)
                act.activation(sq1[:, j, :], qd[:, j, :], ACT.Square).then_inc(sq_set, 1)
            act.wait_ge(qkv_copied, 3)
            act.activation(sq1[:, 2, :], kvd, ACT.Square).then_inc(sq_set, 1)
            at, u0 = ring_at["mla_gate"], unit_at["mla_gate"]
            act.wait_ge(bc_spilled, 32)
            with turns(act, 8, 4) as i:
                for s in range(4):
                    u = u0 + s
                    act.wait_ge(slot_done, i + (at + s + 1))
                    for m in range(2):
                        act.activation(gate[:, bass.ds(i * 2 + (2 * s + m), 1), :].rearrange("p a t -> p (a t)"),
                                       psum[2 * (u % 2) + m][:, :], ACT.Silu).then_inc(unit_free[u % 2], 1)
            act.wait_ge(stat, 2)
            for j in range(2):
                root(rs1[:, j, :], psum[4 + j][:, :])
            act.wait_ge(ctok_t, 1)
            act.copy(ckv_tok.rearrange("p k c -> p (k c)"), psum[6][:, :]).then_inc(ctok_set, 1)

            def project(pair, d0):
                act.wait_ge(proj_done, d0 + 1)
                act.copy(q_rope, psum[0][:, :]).then_inc(qk_set, 1)
                act.wait_ge(qk_set, pair * 5 + 1)
                act.sem_inc(proj_free[0], 1)
                for e in range(2):
                    act.wait_ge(proj_done, d0 + (3 + 2 * e))
                    act.copy(qh[e], psum[0][:, :]).then_inc(qk_set, 1)
                    act.wait_ge(qk_set, pair * 5 + (2 + 2 * e))
                    act.sem_inc(proj_free[0], 1)
                    act.wait_ge(proj_done, d0 + (4 + 2 * e))
                    act.copy(kh[e], psum[1][:, :]).then_inc(qk_set, 1)
                    act.wait_ge(qk_set, pair * 5 + (3 + 2 * e))
                    act.sem_inc(proj_free[1], 1)

            def exps(pair, e):
                for t in range(4):
                    w = S if t < 2 else T
                    act.wait_ge(bias_set, pair * 8 + (4 * e + t + 1))
                    act.activation(prob[e][:, t, 0:w], psum[2 + t][:, 0:w], ACT.Exp, bias=sm[:, e, 1, t:t + 1],
                                   scale=SM_SCALE, accum_out=sm[:, e, 2, t:t + 1]).then_inc(exp_done, 1)

            def values(pair, e, d0):
                for t in range(2):
                    act.wait_ge(pt_done, pair * 6 + (3 * e + t + 2))
                    act.copy(pt_lat[:, t, :, :].rearrange("p k q -> p (k q)"), psum[6 + (3 * e + t + 1) % 2][:, :]).then_inc(pt_a, 1)
                act.wait_ge(proj_done, d0 + 1)
                act.copy(o_lat, psum[0][:, :]).then_inc(olat_set, 1)
                act.wait_ge(olat_set, pair * 2 + (e + 1))
                act.sem_inc(proj_free[0], 1)

            project(0, 0)
            exps(0, 0)
            exps(0, 1)
            values(0, 0, 6)

            def pair_step(p):
                d0 = p * 8 - 1
                project(p, d0)
                exps(p, 0)
                values(p - 1, 1, d0 + 6)
                exps(p, 1)
                values(p, 0, d0 + 7)

            pair_step(1)
            with turns(act, 6, 2) as i:
                for b in range(2):
                    pair_step(i + (b + 2))
            values(PAIRS - 1, 1, 8 * PAIRS - 1)

            def layer_norm(l, n, with_ctx):
                halves = ([(xc, 0)] if with_ctx else []) + [(xl, S)]
                for h, (x, lo) in enumerate(halves):
                    act.wait_ge(ln_centered, n + h + 1)
                    act.activation(ht[:, :, lo:lo + S], x[:, :, :], ACT.Square).then_inc(ln_sq, 1)
                act.wait_ge(ln_var, l + 1)
                w = slice(halves[0][1], T)
                root(ln_rs[:, w], psum[5][:, w])
                for h, (x, lo) in enumerate(halves):
                    act.wait_ge(ln_norm, n + h + 1)
                    for k in range(KD):
                        act.activation(x[:, k, :], x[:, k, :], ACT.Identity, bias=vec("ln_b", l * KD + k),
                                       scale=vec("ln_g", l * KD + k)).then_inc(ln_out, 1)

            layer_norm(0, 0, True)
            act.wait_ge(ln_out, 2 * KD)
            modulate(1)
            at, u0 = ring_at["s5_u"], unit_at["s5_u"]
            with turns(act, 8, NSLOT) as i:
                for s in range(NSLOT):
                    u = u0 + s
                    act.wait_ge(slot_done, i + (at + s + 1))
                    for m in range(2):
                        act.copy(utok[:, :, 2 * m:2 * m + 2, :].rearrange("p g s c -> p s g c"),
                                 psum[2 * (u % 2) + m][:, :].rearrange("p (s g c) -> p s g c", s=2, c=CH5)).then_inc(utok_set, 1)
                    act.wait_ge(utok_set, i * 2 + (2 * s + 2))
                    act.sem_inc(unit_free[u % 2], 2)
            at, u0 = ring_at["s5_g"], unit_at["s5_g"]
            with turns(act, 8, NSLOT) as i:
                for s in range(4):
                    u = u0 + s
                    act.wait_ge(slot_done, i + (at + s + 1))
                    for m in range(2):
                        act.activation(gl[:, bass.ds(i * 2 + (2 * s + m), 1), :].rearrange("p a t -> p (a t)"),
                                       psum[2 * (u % 2) + m][:, 0:S], ACT.Silu).then_inc(unit_free[u % 2], 1)

            def trig(b):
                act.wait_ge(ang_set, b + 1)
                act.activation(sin5, ang, ACT.Sin, scale=TWO_PI_DOWN).then_inc(trig5, 1)
                link(act.activation(cos5, ang, ACT.Abs))
                act.activation(cos5, cos5, ACT.Sin, scale=-TWO_PI_DOWN, bias=half_pi).then_inc(trig5, 1)

            def bmats(b):
                for f in range(4):
                    act.wait_ge(btt_done, b * 4 + (f + 1))
                    act.copy(bmat[:, f // 2, f % 2, :, :].rearrange("p q r -> p (q r)"), psum[f % 2][:, :]).then_inc(bmat_set, 1)

            def u_block(b):
                act.copy(ub.rearrange("p q g c -> p (q g c)"),
                         u5.rearrange("p q g c -> p (q g c)")[:, bass.ds(b * (BLK * 2 * NC5), BLK * 2 * NC5)]).then_inc(ub_set, 1)

            def back(b):
                act.wait_ge(t2_done, b + 1)
                act.activation(yt[:, bass.ds(b, 1), :].rearrange("p a t -> p (a t)"), psum[5][:, 0:S], ACT.Gelu_apprx_tanh)\
                    .then_inc(yt_set, 1)

            act.wait_ge(ut_free[0], 36)
            act.wait_ge(ut_free[1], 36)
            bmats(0)
            u_block(0)
            trig(0)
            with turns(act, 14, 2) as i:
                link.begin(i // 2, 2)
                for par in range(2):
                    b = i + par
                    act.wait_ge(in_done, b * 2 + 2)
                    bmats(b + 1)
                    act.wait_ge(y_done, b + 1)
                    act.wait_ge(td_set, b + 1)
                    u_block(b + 1)
                    back(b)
                    trig(b + 1)
                link.end(7)
            act.wait_ge(in_done, 30)
            bmats(15)
            act.wait_ge(y_done, 15)
            act.wait_ge(td_set, 15)
            u_block(15)
            back(14)
            trig(15)
            back(15)

            at, u0 = ring_at["glu"], unit_at["glu"]
            act.sem_inc(glu_set, 2)
            with turns(act, 32, NSLOT) as i:
                act.wait_ge(slot_done, i + (at + 4))
                act.wait_ge(glu_set, i // 2 + 2)
                for m in range(2):
                    act.activation(sgm[:, m, :], psum[2 + m][:, 0:S], ACT.Sigmoid,
                                   bias=vecr("s5_b_glu", i // 2 + (16 + m))).then_inc(unit_free[1], 1)
                act.wait_ge(unit_free[1], i // 2 + (2 * ((u0 + 1) // 2) + 2))
                act.sem_inc(sg_set, 1)
            at, u0 = ring_at["s5_out"], unit_at["s5_out"]
            with turns(act, 8, NSLOT) as i:
                for s in range(2):
                    u = u0 + s
                    act.wait_ge(slot_done, i + (at + 2 * s + 2))
                    for m in range(2):
                        act.wait_ge(x_new, i + (16 + 2 * s + m - 4 + 1))
                        g = mod[:, 1, :, :].rearrange("p m j -> p (m j)")[:, bass.ds(i * 2 + (2 * (2 * s + m) + 4 * KD + 1), 1)]
                        act.activation(sy[:, 2 * s + m, :], psum[2 * (u % 2) + m][:, 0:S], ACT.Copy, scale=g).then_inc(sy_set, 1)
                    act.wait_ge(sy_set, i + (2 * s + 2))
                    act.sem_inc(unit_free[u % 2], 2)
            layer_norm(1, 2, False)

            def squares(n, wait):
                act.wait_ge(*wait)
                act.activation(sq, xl[:, :, :], ACT.Square).then_inc(sq_done, 1)
                act.wait_ge(ms_done, n + 1)
                root(rstd, psum[4][:, 0:S])

            squares(0, (ln_out, 3 * KD))
            act.wait_ge(mem_in, 16)
            for t in range(2):
                link(act.activation(mem_sq, mem_tok[:, t, :], ACT.Square, accum_out=mem_s[:, t, 0:1]))
            for t in range(2):
                root(mem_s[:, t, 1:2], mem_s[:, t, 0:1], 1.0 / D)
            at, u0 = ring_at["w_in"], unit_at["w_in"]
            for s in range(2, 6):
                act.wait_ge(slot_done, at + s + 1)
                for m in range(2):
                    t = 2 * (s - 2) + m
                    dst = uu[:, t, :] if t < 4 else vv[:, t - 4, :]
                    act.activation(dst, psum[2 * ((u0 + s) % 2) + m][:, 0:S], ACT.Gelu).then_inc(uv_set, 1)
                act.wait_ge(uv_set, 2 * (s - 1))
                act.sem_inc(unit_free[(u0 + s) % 2], 2)
            act.wait_ge(vn_set, 1)
            act.wait_ge(ms_done, 1)
            act.activation(sq[:, 0:4, :], vv, ACT.Square).then_inc(vsq_set, 1)
            act.wait_ge(sgu_stat, 3)
            root(rstd, psum[4][:, S:T])
            at, u0 = ring_at["wk"], unit_at["wk"]
            for s in range(4):
                act.wait_ge(slot_done, at + s + 1)
                for m in range(2):
                    act.copy(k2[:, 2 * s + m, :], psum[2 * ((u0 + s) % 2) + m][:, 0:S]).then_inc(kv2_set, 1)
                act.wait_ge(kv2_set, 2 * s + 2)
                act.sem_inc(unit_free[(u0 + s) % 2], 2)
            at, u0 = ring_at["wv"], unit_at["wv"]
            for s in range(4):
                act.wait_ge(slot_done, at + s + 1)
                for m in range(2):
                    act.copy(v2[:, m, s * MT2:(s + 1) * MT2], psum[2 * ((u0 + s) % 2) + m][:, 0:MT2]).then_inc(kv2_set, 1)
                act.wait_ge(kv2_set, 8 + 2 * s + 2)
                act.sem_inc(unit_free[(u0 + s) % 2], 2)
            squares(1, (h2_set, 8))
            at, u0 = ring_at["wq"], unit_at["wq"]
            for s in range(4):
                act.wait_ge(slot_done, at + s + 1)
                for m in range(2):
                    act.copy(q2[:, 2 * s + m, :], psum[2 * ((u0 + s) % 2) + m][:, 0:S]).then_inc(q2_set, 1)
                act.wait_ge(q2_set, 2 * s + 2)
                act.sem_inc(unit_free[(u0 + s) % 2], 2)
            for h in range(XH):
                for t in range(2):
                    act.wait_ge(b2_set, 2 * h + t + 1)
                    if h >= 2 and t == 0:
                        act.wait_ge(p2t_done, h - 1)
                    act.activation(prob2[:, h % 2, t, :], psum[4 + t][:, 0:S], ACT.Exp, bias=sm2[:, h % 2, t, 1:2],
                                   scale=float(XHD) ** -0.5, accum_out=sm2[:, h % 2, t, 2:3]).then_inc(e2_done, 1)
            squares(2, (h2_set, 16))

            at, u0 = ring_at["w_up"], unit_at["w_up"]

            def conv(i, s, j):
                u = u0 + s
                act.wait_ge(slot_done, i + (at + s + 1))
                for m in range(2):
                    h = s % 2 * 2 + m
                    ch = j * 2 + (m + s % 2 * KF)
                    act.wait_ge(ff_set, j * 2 + 2)
                    link(act.copy(hp[:, h, 2:2 + S], psum[2 * (u % 2) + m][:, 0:S]))
                    act.activation(cv[:, h, :], psum[2 * (u % 2) + m][:, 0:S], ACT.Identity, bias=vecr("conv_b_2", ch),
                                   scale=vecr("conv_w_2", ch + 2 * 2 * KF)).then_inc(unit_free[u % 2], 1)
                    act.wait_ge(unit_free[u % 2], i + (2 * (u // 2) + m + 1))
                    act.sem_inc(conv_in, 1)

            def silu(j):
                for m in range(2):
                    act.wait_ge(conv_out, j * 4 + (m + 1))
                    act.activation(cv[:, m, :], cv[:, m, :], ACT.Silu).then_inc(silu_set, 1)

            act.wait_ge(ones_set, 2)
            act.sem_inc(ff_set, 2)
            with turns(act, 20, NSLOT) as i:
                link.begin(i // 4, 8)
                for s in range(NSLOT):
                    conv(i, s, i // 2 + s // 2)
                    if s % 2:
                        silu(i // 2 + s // 2)
                link.end(5)
            for s in range(20, 22):
                conv(0, s, 10)
            silu(10)
            squares(3, (h2_set, 24))
            for t in range(2):
                act.wait_ge(fin_t, 2 * t + 2)
                act.copy(orow[:, t, 512:1024], psum[2 * t + 1][:, :]).then_inc(fin_set, 1)

        @block.vector
        def _(dve):
            link = Link(dve, v_link)
            tt, ts, stt = dve.tensor_tensor, dve.tensor_scalar, dve.scalar_tensor_tensor
            dve.memset(vrow, 0.0).then_inc(vec_clear, 1)
            for v, n in ((avg_d, D), (avg_q, QR), (avg_kv, KVR)):
                link(dve.memset(v[:, :], 1.0 / n))
            dve.memset(avg_sgu[:, :], 1.0 / 512).then_inc(ones_set, 1)
            dve.wait_ge(vec_t, 1)
            dve.tensor_copy(col[:, :], psum[4][:, :]).then_inc(vec_out, 1)
            for k in range(0, KD, 2):
                dve.wait_ge(p0_t, k + 1)
                dve.tensor_copy(xc[:, k, :], psum[2 * (k // 2 % 2)][:, 0:S]).then_inc(xt_dve, 1)
                dve.tensor_copy(xl[:, k, :], psum[2 * (k // 2 % 2)][:, S:T]).then_inc(xt_dve, 1)
                dve.wait_ge(xt_dve, k + 2)
                dve.sem_inc(unit_free[k // 2 % 2], 1)

            dve.wait_ge(s5par_in, 10 * 16)
            x, n, r, p, m, e = dt_t
            link(ts(x, dt_raw, 88.0, -87.0, ALU.min, ALU.max))
            link(ts(n, x, LOG2E, MAGIC, ALU.mult, ALU.add))
            link(ts(n, n, -MAGIC, None, ALU.add))
            link(stt(out=r, in0=n, scalar=-LN2_HI, in1=x, op0=ALU.mult, op1=ALU.add))
            link(stt(out=r, in0=n, scalar=-LN2_LO, in1=r, op0=ALU.mult, op1=ALU.add))
            link(ts(p, r, 1.0 / 5040, 1.0 / 720, ALU.mult, ALU.add))
            for c in (1.0 / 120, 1.0 / 24, 1.0 / 6, 0.5, 1.0, 1.0):
                link(tt(p, p, r, ALU.mult))
                link(ts(p, p, c, None, ALU.add))
            link(ts(m, n, 127.0, 8388608.0, ALU.add, ALU.mult))
            link(dve.tensor_copy(e.bitcast(I32), m))
            link(tt(p, p, e, ALU.mult))
            dve.tensor_copy(dt_exp, p.unsqueeze(2).to_broadcast([P, 2, ST5])).then_inc(dt_set, 1)
            dve.tensor_copy(d_rows, d_raw.unsqueeze(1).to_broadcast([P, L5, CH5])).then_inc(dt_set, 1)
            def modulation(l):
                b = at_col["b_mod"] + 24 * l
                dve.wait_ge(slot_done, 12 * (l + 1))
                link(tt(mod[:, l, :, :], psum[6 + l][:, 0:48].rearrange("p (m j) -> p m j", j=2),
                        col[:, b:b + 24].unsqueeze(2).to_broadcast([P, 24, 2]), ALU.add))
                ts(mod[:, l, KD:2 * KD, :], mod[:, l, KD:2 * KD, :], 1.0, None, ALU.add).then_inc(mod_set, 1)

            dve.wait_ge(par_t, 1)
            lr, li, dt, ar, tn, th, sh, ch, E, er, s2, cs, sn, nr, den, t1, t2, fr, fi, x9 = pars
            lbr, lbi = nr, sn
            link(ts(lr, psum[5][:, 0:P], -1e-4, None, ALU.min))
            link(dve.tensor_copy(li, psum[5][:, P:2 * P]))
            link(dve.tensor_copy(dt, psum[5][:, 2 * P:3 * P]))
            dve.tensor_copy(dcol[:, :], psum[5][:, 3 * P:4 * P]).then_inc(par_got, 1)
            tt(ar, lr, dt, ALU.mult).then_inc(arg_set, 1)
            link(tt(t1, li, dt, ALU.mult))
            link(ts(t2, t1, INV_2PI, MAGIC, ALU.mult, ALU.add))
            link(ts(t2, t2, -MAGIC, None, ALU.add))
            link(stt(out=t1, in0=t2, scalar=-PI2_A, in1=t1, op0=ALU.mult, op1=ALU.add))
            link(stt(out=t1, in0=t2, scalar=-PI2_B, in1=t1, op0=ALU.mult, op1=ALU.add))
            link(stt(out=t1, in0=t2, scalar=-PI2_C, in1=t1, op0=ALU.mult, op1=ALU.add))
            ts(th, t1, 3.1415925, -3.1415925, ALU.min, ALU.max).then_inc(arg_set, 1)
            dve.wait_ge(arg_set, 2)
            link(ts(t1, th, INV_2PI * L5, None, ALU.mult))
            link(ts(t2, t1, MAGIC, None, ALU.add))
            link(ts(t2, t2, -MAGIC, None, ALU.add))
            tt(phi[:, :], t1, t2, ALU.subtract).then_inc(par_got, 1)
            dve.wait_ge(par_got, 2)
            dve.wait_ge(act_tanh, 1)
            link(ts(t1, tn, -1.0, 1.0, ALU.mult, ALU.add))
            link(dve.reciprocal(t1, t1))
            link(stt(out=E, in0=tn, scalar=2.0, in1=t1, op0=ALU.mult, op1=ALU.mult))
            link(ts(er, E, 1.0, None, ALU.add))
            dve.wait_ge(act_trig, 2)
            link(stt(out=s2, in0=sh, scalar=2.0, in1=sh, op0=ALU.mult, op1=ALU.mult))
            link(ts(cs, s2, -1.0, 1.0, ALU.mult, ALU.add))
            link(stt(out=sn, in0=sh, scalar=2.0, in1=ch, op0=ALU.mult, op1=ALU.mult))
            link(tt(lbi, er, sn, ALU.mult))
            link(tt(t1, E, cs, ALU.mult))
            link(tt(t1, t1, s2, ALU.subtract))
            link(tt(lbr, er, cs, ALU.mult))
            link(tt(den, lr, lr, ALU.mult))
            link(tt(t2, li, li, ALU.mult))
            link(tt(den, den, t2, ALU.add))
            link(dve.reciprocal(den, den))
            link(tt(fr, t1, lr, ALU.mult))
            link(tt(t2, lbi, li, ALU.mult))
            link(tt(fr, fr, t2, ALU.add))
            link(tt(fr, fr, den, ALU.mult))
            link(tt(fi, lbi, lr, ALU.mult))
            link(tt(t2, t1, li, ALU.mult))
            link(tt(fi, fi, t2, ALU.subtract))
            link(tt(fi, fi, den, ALU.mult))
            link(tt(t1, er, er, ALU.mult))
            link(tt(t1, t1, t1, ALU.mult))
            tt(r8[:, :], t1, t1, ALU.mult).then_inc(par_got, 1)
            dve.wait_ge(p0_t, KD)
            link(dve.memset(pn[:, 0, 0, :], 1.0))
            link(dve.memset(pn[:, 1, 0, :], 0.0))
            link(dve.tensor_copy(pn[:, 0, 1, :], lbr))
            link(dve.tensor_copy(pn[:, 1, 1, :], lbi))

            def cmul(lo, n, u, w):
                o, x = slice(lo, lo + n), slice(u, u + n)
                br = pn[:, 0, w:w + 1, :].to_broadcast([P, n, P])
                bi = pn[:, 1, w:w + 1, :].to_broadcast([P, n, P])
                a1 = raw_tmp[:, 0:n, :]
                a2 = raw_tmp[:, n:2 * n, :]
                link(tt(a1, pn[:, 0, x, :], br, ALU.mult))
                link(tt(a2, pn[:, 1, x, :], bi, ALU.mult))
                link(tt(pn[:, 0, o, :], a1, a2, ALU.subtract))
                link(tt(a1, pn[:, 0, x, :], bi, ALU.mult))
                link(tt(a2, pn[:, 1, x, :], br, ALU.mult))
                link(tt(pn[:, 1, o, :], a1, a2, ALU.add))

            raw_tmp = carve(2 * NPW * P, 8, P)
            cmul(2, 1, 1, 1)
            cmul(3, 2, 1, 2)
            cmul(5, 4, 1, 4)
            dve.tensor_copy(pw[:, :, :, 0:GP5], pn[:, :, :, 0:GP5]).then_inc(par_got, 1)
            for z in range(2):
                dve.tensor_copy(pw[:, z, :, GP5:P], pn[:, z, ::-1, GP5:P]).then_inc(par_got, 1)
            dve.wait_ge(unit_free[0], 12)
            dve.wait_ge(unit_free[1], 12)
            frb = fr.unsqueeze(2).to_broadcast([P, P, CH5])
            fib = fi.unsqueeze(2).to_broadcast([P, P, CH5])
            link(tt(tmp_b[:, 0], bcol[:, 0], frb, ALU.mult))
            link(tt(tmp_b[:, 1], bcol[:, 1], fib, ALU.mult))
            link(tt(tmp_b[:, 0], tmp_b[:, 0], tmp_b[:, 1], ALU.subtract))
            link(tt(tmp_b[:, 1], bcol[:, 0], fib, ALU.mult))
            link(tt(bcol[:, 1], bcol[:, 1], frb, ALU.mult))
            link(tt(bcol[:, 1], bcol[:, 1], tmp_b[:, 1], ALU.add))
            dve.tensor_copy(bcol[:, 0], tmp_b[:, 0]).then_inc(bc_scaled, 1)

            modulation(0)
            modulation(1)

            def modulate(l):
                for k in range(KD):
                    o, x = ht[:, k, S:T], xl[:, k, :]
                    if l == 1:
                        o = by_chunk(ht[:, k, :])[:, NCL:NC5]
                        x = x.rearrange("p (c h s) -> p c h s", h=2, s=4)
                    ts(o, x, mod[:, l, KD + k, 1:2], mod[:, l, k, 1:2], ALU.mult, ALU.add)\
                        .then_inc(h_lat, 1)

            dve.wait_ge(mod_set, 2)
            dve.wait_ge(xt_dve, KD)
            dve.wait_ge(xt_act, KD)
            modulate(0)
            dve.wait_ge(bc_spilled, 32)
            at = ring_at["mla_head"]
            dve.wait_ge(slot_done, at + 1)
            for j in range(2):
                dve.tensor_copy(qd[:, j, :], psum[j][:, :]).then_inc(qkv_copied, 1)
            dve.wait_ge(qkv_copied, 2)
            dve.sem_inc(unit_free[unit_at["mla_head"] % 2], 2)
            dve.wait_ge(slot_done, at + 2)
            dve.tensor_copy(kvd, psum[2][:, :]).then_inc(qkv_copied, 1)
            for h in range(2):
                link(dve.tensor_copy(kr[h * ROPE:(h + 1) * ROPE, :], psum[3][0:ROPE, :]))
            dve.wait_ge(qkv_copied, 3)
            dve.sem_inc(unit_free[1 - unit_at["mla_head"] % 2], 2)
            for j in range(2):
                dve.wait_ge(root_set, j + 1)
                link(dve.reciprocal(rs1[:, j, :], rs1[:, j, :]))
            for j in range(2):
                stt(out=qn[:, j, :], in0=qd[:, j, :], scalar=vec("mla_q_norm", j), in1=rs1[:, 0, :], op0=ALU.mult, op1=ALU.mult)\
                    .then_inc(normed, 1)
            stt(out=ckv, in0=kvd, scalar=vec("mla_kv_norm", 0), in1=rs1[:, 1, :], op0=ALU.mult, op1=ALU.mult).then_inc(normed, 1)
            dve.wait_ge(stat, 3)
            link(tt(rot_t, psum[7][:, 0:S], sin, ALU.mult))
            link(tt(kr_rot, kr[:, S:T], cos, ALU.mult))
            tt(kr_rot, kr_rot, rot_t, ALU.add).then_inc(normed, 1)

            def rope(pair, d0):
                dve.wait_ge(qk_set, pair * 5 + 1)
                link(tt(q_rot, q_rope[:, S:T], cos, ALU.mult))
                dve.wait_ge(proj_done, d0 + 2)
                link(tt(rot_t, psum[1][:, 0:S], sin, ALU.mult))
                dve.sem_inc(proj_free[1], 1)
                tt(q_rot, q_rot, rot_t, ALU.add).then_inc(qrot_set, 1)

            def maxima(pair, e):
                for t in range(4):
                    w = S if t < 2 else T
                    dve.wait_ge(score_done, pair * 8 + (4 * e + t + 1))
                    link(dve.tensor_reduce(sm[:, e, 0, t:t + 1], psum[2 + t][:, 0:w], AX.X, ALU.max))
                    ts(sm[:, e, 1, t:t + 1], sm[:, e, 0, t:t + 1], -SM_SCALE, None, ALU.mult).then_inc(bias_set, 1)

            def normalise(pair, e):
                for t in range(4):
                    w = S if t < 2 else T
                    dve.wait_ge(exp_done, pair * 8 + (4 * e + t + 1))
                    link(dve.reciprocal(sm[:, e, 3, t:t + 1], sm[:, e, 2, t:t + 1]))
                    ts(prob[e][:, t, 0:w], prob[e][:, t, 0:w], sm[:, e, 3, t:t + 1], None, ALU.mult).then_inc(prob_set, 1)

            def values(pair, e):
                dve.wait_ge(pt_done, pair * 6 + (3 * e + 1))
                dve.tensor_copy(prob_t[:, 0:512], psum[6 + e][:, :]).then_inc(pt_v, 1)
                dve.wait_ge(uv_done, pair * 2 + (e + 1))
                g = gate[:, bass.ds(pair * 2 + e, 1), :].rearrange("p a t -> p (a t)")
                tt(g, psum[1][:, :], g, ALU.mult).then_inc(av_set, 1)
                dve.wait_ge(av_set, pair * 2 + (e + 1))
                dve.sem_inc(proj_free[1], 1)

            rope(0, 0)
            maxima(0, 0)
            normalise(0, 0)
            maxima(0, 1)
            normalise(0, 1)
            values(0, 0)

            def pair_step(p):
                rope(p, p * 8 - 1)
                maxima(p, 0)
                normalise(p, 0)
                values(p - 1, 1)
                maxima(p, 1)
                normalise(p, 1)
                values(p, 0)

            pair_step(1)
            with turns(dve, 6, 2) as i:
                link.begin(i // 2, 2 * 18)
                for b in range(2):
                    pair_step(i + (b + 2))
                link.end(3)
            values(PAIRS - 1, 1)

            at, u0 = ring_at["mla_out"], unit_at["mla_out"]

            def residual(i, s, l, with_ctx, at, u0, m0, count):
                u = u0 + s
                dve.wait_ge(slot_done, count)
                for m in range(2):
                    k = m0 + (2 * s + m)
                    bank = psum[2 * (u % 2) + m]
                    lo = S if with_ctx else 0
                    for j, x in ((0, xc), (1, xl)):
                        if j == 0 and not with_ctx:
                            continue
                        xk = x[:, bass.ds(k, 1), :].rearrange("p a t -> p (a t)")
                        g = mod[:, l, :, :].rearrange("p m j -> p (m j)")[:, bass.ds(k * 2 + (4 * KD + j), 1)]
                        stt(out=xk, in0=bank[:, j * lo:j * lo + S], scalar=g, in1=xk, op0=ALU.mult, op1=ALU.add)\
                            .then_inc(x_new, 1)

            dve.wait_ge(alpha_set, 2)
            per = 2 * 4
            with turns(dve, 8, NSLOT) as i:
                for s in range(2):
                    residual(i, s, 0, True, at, u0, i, i + (at + 2 * s + 2))
                    dve.wait_ge(x_new, i * 2 + 4 * (s + 1))
                    dve.sem_inc(unit_free[(u0 + s) % 2], 2)

            def layer_norm(n, with_ctx, sums):
                halves = ([(xc, 0)] if with_ctx else []) + [(xl, S)]
                dve.wait_ge(ln_sum, sums)
                for x, lo in halves:
                    tt(x[:, :, :], x[:, :, :], psum[4][:, lo:lo + S].unsqueeze(1).to_broadcast([P, KD, S]), ALU.subtract)\
                        .then_inc(ln_centered, 1)
                dve.wait_ge(root_set, 2 + sums)
                w = slice(halves[0][1], T)
                link(dve.reciprocal(ln_rs[:, w], ln_rs[:, w]))
                for x, lo in halves:
                    tt(x[:, :, :], x[:, :, :], ln_rs[:, lo:lo + S].unsqueeze(1).to_broadcast([P, KD, S]), ALU.mult)\
                        .then_inc(ln_norm, 1)

            dve.wait_ge(ln_sum, 1)
            layer_norm(0, True, 1)
            dve.wait_ge(ln_out, 2 * KD)
            modulate(1)

            with turns(dve, 8, NSLOT) as i:
                for s in range(NSLOT):
                    for q in range(2):
                        dve.wait_ge(ut_done, i * 2 + (2 * s + q + 1))
                        src = psum[4 + q][:, :].rearrange("p (q h c) -> p q h c", q=4, h=2)
                        for g in range(2):
                            for h in range(2):
                                dve.tensor_copy(u5[h * 64:(h + 1) * 64, bass.ds(i * 8 + (8 * s + 4 * q), 4), g, :],
                                                src[g * 64:(g + 1) * 64, :, h, :]).then_inc(ut_free[q], 1)

            dve.wait_ge(p_link, 1)

            def c_tables(b, par):
                dve.wait_ge(bc_in, b * 16 + 16)
                bbv = bb.rearrange("p z d q c -> p (z d q) c")
                bbdv = bbd.rearrange("p z d q g c -> p (z d q) g c")
                for g in range(2):
                    r = slice(g * ST5, (g + 1) * ST5)
                    if g == 0:
                        link(dve.tensor_copy(bbdv[r, :, g, :], bbv[r, :, :]))
                    else:
                        dve.tensor_copy(bbdv[r, :, g, :], bbv[r, :, :]).then_inc(bbd_set, 1)
                dve.wait_ge(cc_in, b * 16 + 16)
                for d in range(2):
                    dims = [P, BLK, NPW, CH5]
                    pr, pi = (pw[:, z, :, bass.ds(b * BLK + d * GP5, BLK)].rearrange("p i q -> p q i").unsqueeze(3).to_broadcast(dims)
                              for z in range(2))
                    cr, ci = (cc[:, z, d, :, :].unsqueeze(2).to_broadcast(dims) for z in range(2))
                    v1, v2 = (v[:, 0:576].rearrange("p (q i c) -> p q i c", q=BLK, i=NPW) for v in gen_v)
                    link(tt(v1, cr, pr, ALU.mult))
                    link(tt(v2, ci, pi, ALU.mult))
                    link(tt(cp[par][:, 0, d], v1, v2, ALU.add))
                    link(tt(v1, ci, pr, ALU.mult))
                    link(tt(v2, cr, pi, ALU.mult))
                    o = tt(cp[par][:, 1, d], v1, v2, ALU.subtract)
                    if d == 0:
                        link(o)
                    else:
                        o.then_inc(cp_set, 1)

            def angles(b):
                dims = [P, 2, BLK, NC5]
                ph = phi[:, :].rearrange("p (d q) -> p d q", d=2)[:, :, bass.ds(b * BLK, BLK)].unsqueeze(3).to_broadcast(dims)
                link(tt(ang, ph, iota.unsqueeze(1).unsqueeze(1).to_broadcast(dims), ALU.mult))
                link(ts(z1, ang, MAGIC, None, ALU.add))
                link(ts(z1, z1, -MAGIC, None, ALU.add))
                rd = r8[:, :].rearrange("p (d q) -> p d q", d=2)[:, :, bass.ds(b * BLK, BLK)].unsqueeze(3)
                link(ts(dec5[:, :, :, 1:NC5], rd.to_broadcast([P, 2, BLK, NC5 - 1]), 1.0, None, ALU.mult))
                tt(ang, ang, z1, ALU.subtract).then_inc(ang_set, 1)

            def kfs(b):
                for f in range(2):
                    dve.wait_ge(kf_done, b * 2 + (f + 1))
                    dve.tensor_copy(kf[0:2 * CH5, 2 * f:2 * f + 2, :].rearrange("p q w -> p (q w)"),
                                    psum[2 + f][0:2 * CH5, 0:2 * KW5]).then_inc(kf_set, 1)

            def flat(v):
                return v.rearrange("p d q c -> p (d q c)")

            def scan(b):
                dve.wait_ge(trig5, b * 2 + 2)
                dve.wait_ge(in_done, b * 2 + 2)
                ir, ii = (psum[4 + z][:, :].rearrange("p (d q c) -> p d q c", d=2, q=BLK) for z in range(2))
                link(tt(z1, ir, cos5, ALU.mult))
                link(tt(z2, ii, sin5, ALU.mult))
                link(tt(z3, ii, cos5, ALU.mult))
                link(tt(z4, ir, sin5, ALU.mult))
                link(tt(z1, z1, z2, ALU.add))
                link(tt(z3, z3, z4, ALU.subtract))
                link(dve.tensor_tensor_scan(flat(z2), flat(dec5), flat(z1), 0.0, ALU.mult, ALU.add))
                link(dve.tensor_tensor_scan(flat(z4), flat(dec5), flat(z3), 0.0, ALU.mult, ALU.add))
                w = slice(NCL - 1, NC5 - 1)
                t1, t2 = z1[:, :, :, 0:NCL], z1[:, :, :, NCL:NC5]
                t3, t4 = z3[:, :, :, 0:NCL], z3[:, :, :, NCL:NC5]
                link(tt(t1, z2[:, :, :, w], cos5[:, :, :, w], ALU.mult))
                link(tt(t2, z4[:, :, :, w], sin5[:, :, :, w], ALU.mult))
                link(tt(t3, z4[:, :, :, w], cos5[:, :, :, w], ALU.mult))
                link(tt(t4, z2[:, :, :, w], sin5[:, :, :, w], ALU.mult))
                tt(xr5, t1, t2, ALU.subtract).then_inc(x5_set, 1)
                tt(xi5, t3, t4, ALU.add).then_inc(x5_set, 1)

            def outs(b):
                dve.wait_ge(y_done, b + 1)
                dve.wait_ge(td_set, b + 1)
                for g in range(2):
                    for h in range(2):
                        r = slice(h * 64, (h + 1) * 64)
                        tt(y2[g * 64:(g + 1) * 64, :, h, :], psum[6 + g][r, 0:BLK * NCL].rearrange("p (q c) -> p q c", q=BLK),
                           td[r, :, g, :], ALU.add).then_inc(y2_set, 1)
                dve.wait_ge(t1_done, b + 1)
                for j in range(2):
                    for x in range(2):
                        q = 2 * j + x
                        dve.tensor_copy(ytok[0:64, :, q * 32:(q + 1) * 32].rearrange("p s (g c) -> p g s c", g=2),
                                        psum[4][x * 64:(x + 1) * 64, j * P:(j + 1) * P].rearrange("p (g s c) -> p g s c", g=2, s=4))\
                            .then_inc(ytok_set, 1)

            c_tables(0, 0)
            kfs(0)
            angles(0)
            with turns(dve, 14, 2) as i:
                link.begin(i // 2, 2 * (12 + 12 + 4))
                for par in range(2):
                    scan(i + par)
                    c_tables(i + (par + 1), 1 - par)
                    dve.wait_ge(t0_in[par], i * 128 + 256)
                    kfs(i + (par + 1))
                    outs(i + par)
                    angles(i + (par + 1))
                link.end(7)
            scan(14)
            c_tables(15, 1)
            dve.wait_ge(t0_in[0], 256 * 8)
            kfs(15)
            outs(14)
            angles(15)
            scan(15)
            outs(15)

            at, u0 = ring_at["glu"], unit_at["glu"]
            with turns(dve, 32, NSLOT) as i:
                link.begin(i // 4, 2)
                dve.wait_ge(sg_set, i // 4 + 1)
                for m in range(2):
                    k = i // 2 + m
                    link(stt(out=glu_t[:, m, :], in0=psum[m][:, 0:S], scalar=vecr("s5_b_glu", k), in1=sgm[:, m, :],
                             op0=ALU.add, op1=ALU.mult))
                    dve.sem_inc(unit_free[0], 1)
                    g = gl[:, bass.ds(k, 1), :].rearrange("p a t -> p (a t)")
                    tt(g, g, glu_t[:, m, :], ALU.mult).then_inc(glu_set, 1)
                link.end(8)
            at, u0 = ring_at["s5_out"], unit_at["s5_out"]
            dve.wait_ge(alpha_set, 3)
            with turns(dve, 8, NSLOT) as i:
                for s in range(2):
                    for m in range(2):
                        dve.wait_ge(sy_set, i + (2 * s + m + 1))
                        xk = xl[:, bass.ds(i + (2 * s + m), 1), :].rearrange("p a t -> p (a t)").rearrange("p (c h s) -> p s h c", h=2, s=4)
                        tt(xk, sy[:, 2 * s + m, :].rearrange("p (s h c) -> p s h c", s=4, h=2), xk, ALU.add).then_inc(x_new, 1)
            layer_norm(2, False, 2)

            def rms(n, name):
                dve.wait_ge(root_set, (5, 9, 10, 11)[n])
                link(dve.reciprocal(rstd, rstd))
                for k in range(KD):
                    o = stt(out=xn[:, k, :], in0=xl[:, k, :], scalar=vec(name, k), in1=rstd, op0=ALU.mult, op1=ALU.mult)
                    if k < KD - 1:
                        link(o)
                    else:
                        o.then_inc(xn_set, 1)

            dve.wait_ge(ln_out, 3 * KD)
            rms(0, "norm_mix_g_2")
            for v in pp:
                link(dve.memset(v[:, :, 0:16], 0.0))
            for t in range(2):
                dve.wait_ge(root_set, 6 + t)
                link(dve.reciprocal(mem_s[:, t, 1:2], mem_s[:, t, 1:2]))
                ts(mem_tok[:, t, :], mem_tok[:, t, :], mem_s[:, t, 1:2], None, ALU.mult).then_inc(mem_set, 1)
            at, u0 = ring_at["w_in"], unit_at["w_in"]
            for s in range(2):
                dve.wait_ge(slot_done, at + s + 1)
                for m in range(2):
                    link(dve.tensor_copy(pp[0][:, 2 * s + m, 16:16 + S], psum[2 * ((u0 + s) % 2) + m][:, 0:S]))
                dve.sem_inc(unit_free[(u0 + s) % 2], 2)
            cur, nxt = pp[0], pp[1]
            body = slice(16, 16 + S)
            for g, w in enumerate(POOLW):
                sh_ = w // 2
                link(tt(pp[2 - g % 2][:, g:4, body], (pp[0] if g == 0 else pp[2 - (g - 1) % 2])[:, g:4, body],
                        (pp[0] if g == 0 else pp[2 - (g - 1) % 2])[:, g:4, 16 - sh_:16 - sh_ + S], ALU.add))
                now = pp[2 - g % 2]
                link(tt(now[:, g, 0:16], now[:, g, 16:32], cst[:, C_CNT + 16 * g:C_CNT + 16 * g + 16], ALU.mult))
                link(stt(out=pp[1][:, g, 32:16 + S], in0=now[:, g, 32:16 + S], scalar=1.0 / w, in1=pp[0][:, g, 32:16 + S],
                         op0=ALU.mult, op1=ALU.subtract))
                tt(pp[1][:, g, 16:32], now[:, g, 0:16], pp[0][:, g, 16:32], ALU.subtract).then_inc(dpool_set, 1)
                dve.wait_ge(dpool_set, g + 1)
            u0 = unit_at["mem"]
            for k in range(KD):
                u = u0 + k // 2
                dve.wait_ge(memt_done, k + 1)
                ts(mem_t[:, k, :], psum[2 * (u % 2) + k % 2][:, 0:S], vec("mem_norm_g_2", k), None, ALU.mult).then_inc(memt_set, 1)
                dve.wait_ge(memt_set, k + 1)
                dve.sem_inc(unit_free[u % 2], 1)
            dve.wait_ge(sgu_stat, 1)
            link(tt(sgu_wt, psum[5][:, :].rearrange("p (h t) -> p h t", h=4),
                    cst[:, C_MASK:C_MASK + P].unsqueeze(1).to_broadcast([P, 4, P]), ALU.mult))
            dve.wait_ge(pool_done, 1)
            for g in range(4):
                ts(cat[:, g, :], psum[6 + g // 2][:, g % 2 * S:(g % 2 + 1) * S], vec("pool_scale_2", g), None, ALU.mult)\
                    .then_inc(cat_set, 1)
            dve.wait_ge(sgu_stat, 2)
            tt(vv, vv, psum[4][:, 0:S].unsqueeze(1).to_broadcast([P, 4, S]), ALU.subtract).then_inc(vn_set, 1)
            dve.wait_ge(root_set, 8)
            link(dve.reciprocal(rstd, rstd))
            for k in range(4):
                o = stt(out=vv[:, k, :], in0=vv[:, k, :], scalar=vec("sgu_g_2", k), in1=rstd, op0=ALU.mult, op1=ALU.mult)
                if k == 0:
                    link(o)
                else:
                    o.then_inc(vn_set, 1)
            for t in range(2):
                dve.wait_ge(vt_done, t + 1)
                dve.tensor_copy(vtok[:, t, :], psum[6 + t][:, :]).then_inc(vtok_set, 1)
            dve.wait_ge(z_done, 1)
            for h in range(4):
                link(tt(sgu_z[:, h, :].rearrange("p (t q) -> p t q", t=2),
                        psum[6 + h // 2][:, (h % 2) * S:(h % 2 + 1) * S].rearrange("p (t q) -> p t q", t=2),
                        sgu_bb[:, h, :].unsqueeze(1).to_broadcast([P, 2, P]), ALU.add))
                tt(cat[:, 4 + h, :], sgu_z[:, h, :], uu[:, h, :], ALU.mult).then_inc(cat_set, 1)

            def add_out(name, slots_per_unit, h0):
                at, u0 = ring_at[name], unit_at[name]
                for s in range(4):
                    dve.wait_ge(slot_done, at + slots_per_unit * (s + 1))
                    for m in range(2):
                        k = 2 * s + m
                        tt(xl[:, k, :], psum[2 * ((u0 + s) % 2) + m][:, 0:S], xl[:, k, :], ALU.add).then_inc(h2_set, 1)
                    dve.wait_ge(h2_set, h0 + 2 * s + 2)
                    dve.sem_inc(unit_free[(u0 + s) % 2], 2)

            add_out("w_out", 1, 0)
            rms(1, "norm_xattn_g_2")
            def softmax2(h):
                b = h % 2
                for t in range(2):
                    dve.wait_ge(s2_done, 2 * h + t + 1)
                    link(dve.tensor_reduce(sm2[:, b, t, 0:1], psum[4 + t][:, 0:S], AX.X, ALU.max))
                    ts(sm2[:, b, t, 1:2], sm2[:, b, t, 0:1], -(float(XHD) ** -0.5), None, ALU.mult).then_inc(b2_set, 1)

            def normalise2(h):
                b = h % 2
                for t in range(2):
                    dve.wait_ge(e2_done, 2 * h + t + 1)
                    link(dve.reciprocal(sm2[:, b, t, 3:4], sm2[:, b, t, 2:3]))
                    ts(prob2[:, b, t, :], prob2[:, b, t, :], sm2[:, b, t, 3:4], None, ALU.mult).then_inc(p2_set, 1)

            def values2(h):
                dve.wait_ge(p2t_done, h + 1)
                if h >= 1:
                    dve.wait_ge(o2_done, h)
                dve.tensor_copy(prob2_t.rearrange("p m t -> p (m t)"), psum[6][:, :]).then_inc(p2t_set, 1)
                dve.wait_ge(o2_done, h + 1)
                dve.tensor_copy(o2[:, 2 * h:2 * h + 2, :].rearrange("p c t -> p (c t)"), psum[7][:, :]).then_inc(o2_set, 1)

            softmax2(0)
            normalise2(0)
            for h in range(XH):
                if h + 1 < XH:
                    softmax2(h + 1)
                    normalise2(h + 1)
                values2(h)
            add_out("wo", 1, 8)
            dve.wait_ge(cat_set, 8)
            dve.memset(hp[:, :, 0:2], 0.0).then_inc(ones_set, 1)
            rms(2, "norm_ffn_g_2")

            def taps(j, n):
                for h in range(4):
                    ch = j * 2 + (h % 2 + h // 2 * KF)
                    dve.wait_ge(conv_in, n + (h + 1))
                    link(stt(out=cv[:, h, :], in0=hp[:, h, 1:1 + S], scalar=vecr("conv_w_2", ch + 2 * KF), in1=cv[:, h, :],
                             op0=ALU.mult, op1=ALU.add))
                    stt(out=cv[:, h, :], in0=hp[:, h, 0:S], scalar=vecr("conv_w_2", ch), in1=cv[:, h, :],
                        op0=ALU.mult, op1=ALU.add).then_inc(conv_out, 1)
                for m in range(2):
                    dve.wait_ge(conv_out, n + (m + 3))
                    dve.wait_ge(silu_set, j * 2 + (m + 1))
                    tt(ff[:, bass.ds(j * 2 + m, 1), :].rearrange("p a t -> p (a t)"), cv[:, m, :], cv[:, 2 + m, :], ALU.mult)\
                        .then_inc(ff_set, 1)

            with turns(dve, 20, NSLOT) as i:
                link.begin(i // 4, 8)
                for s in range(2):
                    taps(i // 2 + s, i * 2 + 4 * s)
                link.end(5)
            taps(10, 40)
            add_out("w_down", 3, 16)
            rms(3, "final_norm_g_2")
            for t in range(2):
                dve.wait_ge(fin_t, 2 * t + 1)
                dve.tensor_copy(orow[:, t, 0:512], psum[2 * t][:, :]).then_inc(fin_set, 1)

        @block.gpsimd
        def _(pool):
            tt = pool.tensor_tensor
            pool.wait_ge(bc_scaled, 1)
            pool.dma_start(spill_b, bcol.rearrange("p z (d q) c -> p (z d) (q c)", d=2)).then_inc(bc_spilled, 16)
            pool.dma_start(spill_c, ccol.rearrange("p z (d q) c -> p (z d) (q c)", d=2)).then_inc(bc_spilled, 16)
            pool.wait_ge(h_ctx, KD)
            pool.tensor_scalar(xc[:, :, :], xc[:, :, :], ALPHA, None, ALU.mult).then_inc(alpha_set, 1)
            pool.wait_ge(h_lat, KD)
            pool.tensor_scalar(xl[:, :, :], xl[:, :, :], ALPHA, None, ALU.mult).then_inc(alpha_set, 1)
            pool.wait_ge(h_lat, 2 * KD)
            pool.tensor_scalar(xl[:, :, :], xl[:, :, :], ALPHA, None, ALU.mult).then_inc(alpha_set, 1)

            pool.wait_ge(slot_done, ring_at["s5_g"] + 8)
            pool.wait_ge(h_ctx, 2 * KD)
            pool.memset(bbd, 0.0)
            pool.memset(dec5, 0.0).then_inc(p_link, 1)
            count = [1]

            def step(ins, i):
                ins.then_inc(p_link, 1)
                count[0] += 1
                pool.wait_ge(p_link, i + count[0])

            HALF = BLK // 2

            def b_tables(b, i, free=True):
                step(pool.tensor_copy(pwb.rearrange("p z i d q -> p (z i) d q"),
                                      pw[:, :, :, :].rearrange("p z i (d q) -> p (z i) d q", d=2)[:, :, :, bass.ds(b * BLK, BLK)]), i)
                pool.wait_ge(bc_in, b * 16 + 16)
                pool.sem_inc(pool_passed, 1)
                if free:
                    pool.wait_ge(btt_done, b * 4)
                    pool.sem_inc(pool_passed, 1)
                for d in range(2):
                    for hf in range(2):
                        qs = slice(hf * HALF, (hf + 1) * HALF)
                        dims = [P, HALF, L5, CH5]
                        v1, v2 = (v[:, 0:HALF * L5 * CH5].rearrange("p (q s c) -> p q s c", q=HALF, s=L5) for v in gen_p)
                        rev = slice(L5 - 1, None, -1) if d == 0 else slice(L5, 0, -1)
                        pr, pi = (pwb[:, z, rev, d, qs].rearrange("p i q -> p q i").unsqueeze(3).to_broadcast(dims)
                                  for z in range(2))
                        br, bi = (bb[:, z, d, qs, :].unsqueeze(2).to_broadcast(dims) for z in range(2))
                        step(tt(v1, br, pr, ALU.mult), i)
                        step(tt(v2, bi, pi, ALU.mult), i)
                        step(tt(bt[:, 0, d, qs], v1, v2, ALU.subtract), i)
                        step(tt(v1, bi, pr, ALU.mult), i)
                        step(tt(v2, br, pi, ALU.mult), i)
                        o = tt(bt[:, 1, d, qs], v1, v2, ALU.add)
                        if hf == 0:
                            step(o, i)
                        else:
                            o.then_inc(bt_set, 1)
                            pool.wait_ge(bt_set, b * 2 + (d + 1))
                            pool.sem_inc(pool_passed, 1)

            def skip(b):
                pool.wait_ge(ub_set, b + 1)
                pool.sem_inc(pool_passed, 1)
                pool.wait_ge(y2_set, b * 4 + 4)
                pool.sem_inc(pool_passed, 1)
                dd = dcol[:, bass.ds(b * (BLK * 2), BLK * 2)].rearrange("p (q g) -> p q g", g=2).unsqueeze(3)\
                    .to_broadcast([P, BLK, 2, NCL])
                tt(td, ub[:, :, :, NCL:NC5], dd, ALU.mult).then_inc(td_set, 1)

            pool.sem_inc(y2_set, 4)
            PER = 2 * 11 + 1
            b_tables(0, 0, False)
            base = count[0]
            with turns(pool, 15, 1) as i:
                count[0] = base
                skip(i)
                b_tables(i + 1, i * PER)
                assert count[0] == base + PER
            skip(15)


_SMALL = ["mla_q_norm"]
_INS = ["x", "c", "ctx", "c_ctx", "w_mod", "b_mod", "ln_g", "ln_b", "mla_w_in", "mla_q_norm", "mla_kv_norm", "mla_w_uq",
        "mla_w_uk", "mla_w_uv", "mla_w_out", "s5_w_in", "s5_lam_re", "s5_lam_im", "s5_log_dt", "s5_b_re", "s5_b_im",
        "s5_c_re", "s5_c_im", "s5_d", "s5_w_glu", "s5_b_glu", "s5_w_out", "mem_2", "norm_mix_g_2", "w_in_2", "pool_w_2",
        "pool_scale_2", "sgu_g_2", "sgu_w_2", "sgu_b_2", "w_out_2", "norm_xattn_g_2", "mem_norm_g_2", "wq_2", "wk_2",
        "wv_2", "wo_2", "norm_ffn_g_2", "w_up_2", "conv_w_2", "conv_b_2", "w_down_2", "final_norm_g_2"]


def kernel(**inputs):
    import concourse.bacc as bacc
    from concourse.bass_utils import run_bass_kernel_spmd

    nc = bacc.Bacc("TRN2", target_bir_lowering=False, num_devices=1)
    arrays = {f"in_{n}": np.ascontiguousarray(inputs[n]) for n in _INS}
    arrays["in_consts"] = shape_constants()
    a = {n[3:]: nc.dram_tensor(n, v.shape, mybir.dt.from_np(v.dtype), kind="ExternalInput").ap() for n, v in arrays.items()}
    out = nc.dram_tensor("out", (1, S, D), F32, kind="ExternalOutput").ap()
    spill = [nc.dram_tensor(n, (P, 4, GP5 * CH5), F32, kind="Internal").ap() for n in ("s5_b_scaled", "s5_c_turned")]
    program(nc, a, out, *spill)
    r = run_bass_kernel_spmd(nc, [arrays], core_ids=[0])
    return r.results[0]["out"]
```

```python
from contextlib import ExitStack, contextmanager

import numpy as np

import concourse.bass as bass
from concourse import mybir

ALU = mybir.AluOpType
ACT = mybir.ActivationFunctionType
AX = mybir.AxisListType
F32 = mybir.dt.float32
I32 = mybir.dt.int32

P = 128
D = 1024
KD = D // P
S = 256
T = 2 * S
DEPTH = 2
E_BR = 2 * D
KE = E_BR // P
HEADS = 16
PAIRS = HEADS // 2
NOPE, ROPE, VDIM = 128, 64, 128
QR, KVR = D // 4, D // 8
HQ = NOPE + ROPE
SM_SCALE = float(HQ) ** -0.5
GRID_W = 64
G5, CH5, ST5 = 128, 16, 64
L5 = 8
NC5 = T // L5
NCL = S // L5
GP5 = G5 // 2
BLK = 4
NB5 = GP5 // BLK
NPW = L5 + 1
KW5 = (2 * L5 - 1) * CH5
ALPHA = (2.0 * DEPTH) ** 0.25
EPS = 1e-6
POOLW = (2, 4, 8, 16)
XH, XHD = 4, 256
FF = 2816
KF = FF // P
NSLOT = 4
MT2 = 256
MAGIC = 12582912.0
LOG2E, LN2_HI, LN2_LO = 1.4426950408889634, 0.693359375, -2.12194440e-4
INV_2PI = 0.15915494309189535
PI2_A = 6.28125
PI2_B = 2029.0 / 2 ** 20
PI2_C = 6.283185307179586 - PI2_A - PI2_B
TWO_PI_DOWN = 6.2831845

C_ID, C_ROT, C_COS, C_SIN = 0, 128, 256, 512
C_CNT, C_MASK, C_IOTA, C_HPI, C_EPS = 768, 832, 960, 1024, 1025
C_DIAG = 1026
C_COLS = C_DIAG + CH5

VEC_TILES = [
    [("b_mod", 48), ("ln_g", 16), ("ln_b", 16), ("mla_q_norm", 2), ("mla_kv_norm", 1), ("s5_b_glu", 32), ("c", 8)],
    [("c_ctx", 8), ("norm_mix_g_2", 8), ("pool_scale_2", 4), ("sgu_g_2", 4), ("norm_xattn_g_2", 8),
     ("mem_norm_g_2", 8), ("norm_ffn_g_2", 8), ("conv_b_2", 44), ("final_norm_g_2", 8)],
    [("conv_w_2", 132)],
]
NVT = 4


def shape_constants():
    c = np.zeros((P, C_COLS), np.float32)
    c[:, C_ID:C_ID + P] = np.eye(P)
    q = ROPE // 4
    for h in range(2):
        for j in range(q):
            for a, b in ((0, 1), (2, 3)):
                lo, hi = h * ROPE + a * q + j, h * ROPE + b * q + j
                c[hi, C_ROT + lo] = -1.0
                c[lo, C_ROT + hi] = 1.0
    inv = (np.float32(10000.0) ** (-np.arange(q, dtype=np.float32) / np.float32(q))).astype(np.float32)
    tok = np.arange(S)
    row = (tok // GRID_W).astype(np.float32)[:, None] * inv
    col = (tok % GRID_W).astype(np.float32)[:, None] * inv
    ang = np.concatenate([row, row, col, col], axis=1).T
    c[:, C_COS:C_COS + S] = np.tile(np.cos(ang), (2, 1))
    c[:, C_SIN:C_SIN + S] = np.tile(np.sin(ang), (2, 1))
    for g, w in enumerate(POOLW):
        c[:, C_CNT + 16 * g:C_CNT + 16 * g + 16] = 1.0 / np.minimum(np.arange(16) + 1, w)
    c[:, C_MASK:C_MASK + P] = np.triu(np.ones((P, P)))
    c[:, C_IOTA:C_IOTA + NC5] = np.arange(NC5)
    c[:, C_HPI] = np.pi / 2
    c[:, C_EPS] = EPS
    c[:, C_DIAG:C_DIAG + CH5] = np.tile(np.eye(CH5), (P // CH5, 1))
    return c


class Step:

    def __init__(self, turn, per):
        self.turn, self.per = turn, per

    def __mul__(self, k):
        return self.turn * (self.per * k)

    def __floordiv__(self, k):
        assert self.per % k == 0
        return self.turn * (self.per // k)

    def __add__(self, k):
        return self.turn * self.per + k


class Link:

    def __init__(self, eng, sem):
        self.eng, self.sem, self.at, self.i, self.k = eng, sem, 0, 0, 0

    def post(self, ins):
        ins.then_inc(self.sem, 1)
        self.k += 1

    def upto(self, back):
        self.eng.wait_ge(self.sem, self.i + (self.at + self.k - back))

    def __call__(self, ins):
        self.post(ins)
        self.upto(0)

    def begin(self, i, per):
        self.at, self.k, self.i, self.per = self.at + self.k, 0, i * per, per

    def end(self, turns):
        assert self.k == self.per, (self.k, self.per)
        self.at, self.k, self.i = self.at + turns * self.per, 0, 0


def program(nc, a, out, spill_b, spill_c):
    ctx = ExitStack()
    with ctx:
        def sb(name, *shape):
            return ctx.enter_context(nc.sbuf_tensor(name, [P, *shape], F32))

        def sem(name):
            return ctx.enter_context(nc.semaphore(name))

        ring = sb("ring", NSLOT, 8, MT2)
        xc = sb("xc", KD, S)
        xl = sb("xl", KD, S)
        ht = sb("ht", KD, T)
        gate = sb("gate", KE, T)
        cst = sb("cst", C_COLS)
        col = sb("col", NVT * P)
        mod = sb("mod", DEPTH, 24, 2)
        cond = sb("cond", KD, 2)
        avg_d = sb("avg_d", P)
        avg_q = sb("avg_q", P)
        avg_kv = sb("avg_kv", P)
        avg_sgu = sb("avg_sgu", P)
        pw = sb("pw", 2, NPW, P)
        phi = sb("phi", P)
        r8 = sb("r8", P)
        dcol = sb("dcol", GP5)
        NA = 23500
        arena = sb("arena", NA)

        psum = [ctx.enter_context(nc.psum_tensor(f"bank{i}", [P, 512], F32)) for i in range(8)]

        def carve(at, *dims, base=arena):
            n = int(np.prod(dims))
            v = base[:, at:at + n]
            if len(dims) == 1:
                return v
            names = "abcdefg"[:len(dims)]
            return v.rearrange(f"p ({' '.join(names)}) -> p {' '.join(names)}", **dict(zip(names, dims)))

        class Carver:
            def __init__(self, at=0, base=arena):
                self.at, self.base = at, base

            def __call__(self, *dims):
                v = carve(self.at, *dims, base=self.base)
                self.at += int(np.prod(dims))
                assert self.at <= self.base.shape[1], self.at
                return v

        ident = cst[:, C_ID:C_ID + P]
        rot = cst[:, C_ROT:C_ROT + P]
        cos = cst[:, C_COS:C_COS + S]
        sin = cst[:, C_SIN:C_SIN + S]
        iota = cst[:, C_IOTA:C_IOTA + NC5]
        half_pi = cst[:, C_HPI:C_HPI + 1]
        eps = cst[:, C_EPS:C_EPS + 1]

        at_col = {}
        for t, names in enumerate(VEC_TILES):
            n = t * P
            for name, rows in names:
                at_col[name] = n
                n += rows

        def vec(name, i):
            j = at_col[name] + i
            return col[:, j:j + 1]

        def vecr(name, i):
            return col[:, bass.ds(i + at_col[name], 1)]

        def by_chunk(row):
            return row.rearrange("p (s h c) -> p c h s", s=4, h=2)

        c0 = Carver()
        xtok = c0(4, D)
        vrow = c0(NVT, P)
        raw_b = c0(2, ST5 * 2 * CH5)
        raw_c = c0(2, ST5 * 2 * CH5)
        lam_rows = c0(2, P)
        d_raw = c0(2 * CH5)
        dt_raw = c0(2)
        dt_t = [c0(2) for _ in range(6)]
        dt_exp = c0(2, ST5)
        pars = [c0(P) for _ in range(20)]
        tmp_b = raw_b.rearrange("p a b -> p (a b)").rearrange("p (z q c) -> p z q c", z=2, c=CH5)
        bcol = gate[:, 0:8, :].rearrange("p a b -> p (a b)").rearrange("p (z q c) -> p z q c", z=2, c=CH5)
        ccol = gate[:, 8:16, :].rearrange("p a b -> p (a b)").rearrange("p (z q c) -> p z q c", z=2, c=CH5)
        pn = carve(0, 2, NPW, P)
        mod_rows = c0(DEPTH, 24 * P)

        ln_rs = carve(22400, T)
        c1 = Carver()
        qd = c1(2, T)
        kvd = c1(T)
        sq1 = c1(3, T)
        rs1 = c1(2, T)
        qn = c1(2, T)
        ckv = c1(T)
        ckv_tok = c1(4, P)
        kr = c1(T)
        kr_rot = c1(S)
        rot_t = c1(S)
        att_uq = [c1(2, 2 * HQ) for _ in range(2)]
        att_uk = [c1(2 * NOPE) for _ in range(2)]
        att_uv = [c1(2 * VDIM) for _ in range(2)]
        qh = [c1(T) for _ in range(2)]
        kh = [c1(T) for _ in range(2)]
        q_rope = c1(T)
        q_rot = c1(S)
        prob = [c1(4, T) for _ in range(2)]
        prob_t = c1(1536)
        pt_ctx = prob_t[:, 0:512].rearrange("p (t k q) -> p t k q", t=2, k=2)
        pt_lat = prob_t[:, 512:1536].rearrange("p (t k q) -> p t k q", t=2, k=4)
        o_lat = c1(T)
        sm = c1(2, 4, 4)

        c2 = Carver()
        u5 = c2(GP5, 2, NC5)
        bt = c2(2, 2, BLK, L5, CH5)
        bmat = c2(2, 2, BLK, P)
        cp = [c2(2, 2, BLK, NPW, CH5) for _ in range(2)]
        bbd = [c2(2, 2, BLK, 2, CH5) for _ in range(2)]
        kf = c2(BLK, KW5)
        t0 = [c2(BLK, 2, P) for _ in range(2)]
        utok = [v.rearrange("p q g c -> p (q g c)").rearrange("p (g s c) -> p g s c", s=4, c=CH5) for v in t0]
        cc = c2(2, 2, BLK, CH5)
        ytok = c2(4, P)
        d_diag = c2(GP5, CH5)
        pwb = c2(2, NPW, 2, BLK)

        hflat = ht[:, :, :].rearrange("p a b -> p (a b)")
        zt = [hflat[:, 512 * i:512 * i + 512].rearrange("p (d q c) -> p d q c", d=2, q=BLK) for i in range(8)]
        ang, cos5, sin5, dec5, z1, z2, z3, z4 = zt
        xcflat = xc[:, :, :].rearrange("p a b -> p (a b)")
        xcs = Carver(2 * BLK * NPW * CH5, xcflat)
        x5 = [[c(2, BLK, NCL) for _ in range(2)] for c in (c2, xcs)]
        rings = Carver(0, ring[:, 0:2].rearrange("p s k m -> p (s k m)"))
        spare = Carver(0, gate[:, 8:16, :].rearrange("p a b -> p (a b)"))
        nb, ncp = BLK * L5 * CH5, BLK * NPW * CH5
        gen_p = [spare(nb) for _ in range(2)]
        gen_v = [[xcflat[:, (2 * d + i) * ncp:(2 * d + i + 1) * ncp] if d == 0 else spare(ncp) for i in range(2)]
                 for d in range(2)]
        gen_w = [[rings(ncp) for _ in range(2)] for _ in range(2)]
        ub = [spare(BLK, 2, NC5) for _ in range(2)]
        bb = [spare(2, 2, BLK, CH5) for _ in range(2)]
        d_block = [spare(BLK, CH5) for _ in range(2)]
        gl = gate[:, 0:8, :].rearrange("p a b -> p (a b)").rearrange("p (k t) -> p k t", k=KE)
        yt = u5.rearrange("p q g c -> p (q g c)").rearrange("p (b x) -> p b x", b=NB5)[:, :, 0:S]

        c3 = Carver(4 * S)
        c4 = Carver(0, gate[:, 8:16, :].rearrange("p a b -> p (a b)"))
        sgm = c4(2, 2, S)
        glu_t = c4(2, 2, S)
        sy = c4(4, S)
        sq = c3(KD, S)
        rstd = c3(S)
        mem_t = c3(KD, S)
        pp = [c3(4, 16 + S) for _ in range(3)]
        uu = c3(4, S)
        vv = c3(4, S)
        vtok = c3(2, 512)
        pool_w = c3(4, P)
        sgu_w = c3(4, P)
        sgu_wt = c3(4, P)
        sgu_bb = c3(4, P)
        sgu_z = c3(4, S)
        end_sgu = c3.at

        cat = gate[:, 0:4, :].rearrange("p a b -> p (a b)").rearrange("p (k t) -> p k t", k=KD)
        k2 = gate[:, 4:8, :].rearrange("p a b -> p (a b)").rearrange("p (k t) -> p k t", k=KD)
        v2 = gate[:, 8:12, :].rearrange("p a b -> p (a b)").rearrange("p (k t) -> p k t", k=2)
        q2 = gate[:, 12:16, :].rearrange("p a b -> p (a b)").rearrange("p (k t) -> p k t", k=KD)
        xn = ht[:, 0:4, :].rearrange("p a b -> p (a b)").rearrange("p (k t) -> p k t", k=KD)
        o2 = ht[:, 4:8, :].rearrange("p a b -> p (a b)").rearrange("p (k t) -> p k t", k=KD)
        prob2 = pp[0].rearrange("p a b -> p (a b)")[:, 0:1024].rearrange("p (b t m) -> p b t m", b=2, t=2)
        prob2_t = pp[1].rearrange("p a b -> p (a b)")[:, 0:512].rearrange("p (m t) -> p m t", m=2)
        mem_tok = c3(2, D)
        mem_sq = c3(D)
        mem_s = c3(2, 2)
        sm2 = c3(2, 2, 4)
        ff = carve(mem_off := 4096, KF, S)
        hp = carve(mem_off + KF * S, 4, S + 2)
        cv = carve(mem_off + KF * S + 4 * (S + 2), 4, S)
        orow = carve(0, 2, D)

        const_in = sem("const_in")
        x_in = sem("x_in")
        vec_clear = sem("vec_clear")
        vec_in = sem("vec_in")
        s5par_in = sem("s5par_in")
        bc_raw_in = sem("bc_raw_in")
        ones_set = sem("ones_set")
        vec_t = sem("vec_t")
        vec_out = sem("vec_out")
        cond_set = sem("cond_set")
        w_in_ = [sem(f"slot{i}_loaded") for i in range(NSLOT)]
        slot_done = sem("slot_done")
        unit_free = [sem(f"unit{i}_free") for i in range(2)]
        p0_t = sem("p0_transposed")
        modrow_set = sem("mod_rows_set")
        modt_done = sem("mod_transposed")
        mod_set = sem("mod_set")
        xt_act = sem("xt_odd_set")
        xt_dve = sem("xt_even_set")
        dt_set = sem("dt_set")
        par_t = sem("s5par_transposed")
        par_got = sem("s5par_got")
        act_tanh = sem("tanh_done")
        act_trig = sem("trig_done")
        arg_set = sem("trig_args")
        bc_scaled = sem("bc_scaled")
        bc_spilled = sem("bc_spilled")
        v_link = sem("v_link")
        a_link = sem("a_link")
        p_link = sem("p_link")
        h_ctx = sem("h_ctx_set")
        h_lat = sem("h_lat_set")
        alpha_set = sem("alpha_set")
        qkv_copied = sem("qkv_copied")
        sq_set = sem("sq_set")
        stat = sem("stat_ready")
        root_set = sem("root_set")
        normed = sem("normed")
        ctok_t = sem("ctok_transposed")
        ctok_set = sem("ctok_set")
        att_in = [sem(f"att_weights{i}") for i in range(2)]
        proj_done = sem("proj_done")
        proj_free = [sem(f"proj_free{i}") for i in range(2)]
        qk_set = sem("qk_set")
        qrot_set = sem("qrot_set")
        score_done = sem("score_done")
        bias_set = sem("bias_set")
        exp_done = sem("exp_done")
        prob_set = sem("prob_set")
        pt_done = sem("pt_done")
        pt_v = sem("pt_evacuated_v")
        pt_a = sem("pt_evacuated_a")
        olat_set = sem("olat_set")
        uv_done = sem("uv_done")
        av_set = sem("av_set")
        x_new = sem("x_new")
        ln_sum = sem("ln_sum")
        ln_centered = sem("ln_centered")
        ln_sq = sem("ln_sq")
        ln_var = sem("ln_var")
        ln_norm = sem("ln_norm")
        ln_out = sem("ln_out")
        ln_lat = sem("ln_out_latent")
        utok_set = sem("utok_set")
        ut_done = sem("ut_done")
        ut_free = [sem(f"ut_free{i}") for i in range(2)]
        bb_in = [sem(f"bb_in{i}") for i in range(2)]
        cc_in = sem("cc_in")
        bt_set = sem("bt_set")
        bbd_set = sem("bbd_set")
        cc_read = sem("cc_read")
        cp_set = sem("cp_set")
        btt_done = sem("btt_done")
        bmat_set = sem("bmat_set")
        kf_done = sem("kf_done")
        kf_set = sem("kf_set")
        t0_in = [sem(f"t0_in{i}") for i in range(2)]
        ub_set = sem("ub_set")
        in_done = sem("in_done")
        decays_clear = sem("decays_clear")
        diag_set = sem("d_diag_set")
        ang_set = sem("ang_set")
        trig5 = sem("trig5_set")
        in_read = sem("chunk_inputs_read")
        x5_set = sem("x5_set")
        y_half = sem("y_half_done")
        y_done = sem("y_done")
        ytok_set = sem("ytok_set")
        t2_done = sem("t2_done")
        yt_set = sem("yt_set")
        sg_set = sem("sigmoid_set")
        glu_set = sem("glu_set")
        glu_free = [sem(f"glu_banks{i}_free") for i in range(2)]
        sy_set = sem("s5_out_gated")
        sq_done = sem("sq_done")
        ms_done = sem("ms_done")
        xn_set = sem("xn_set")
        mem_in = sem("mem_in")
        mix_in = sem("mix_in")
        mem_set = sem("mem_set")
        memt_done = sem("memt_done")
        memt_set = sem("memt_set")
        uv_set = sem("uv_set")
        dpool_set = sem("dpool_set")
        pool_done = sem("pool_done")
        cat_set = sem("cat_set")
        vsq_set = sem("vsq_set")
        sgu_stat = sem("sgu_stat")
        vn_set = sem("vn_set")
        vt_done = sem("vt_done")
        vtok_set = sem("vtok_set")
        z_done = sem("z_done")
        kv2_set = sem("kv2_set")
        q2_set = sem("q2_set")
        s2_done = sem("s2_done")
        b2_set = sem("b2_set")
        e2_done = sem("e2_done")
        p2_set = sem("p2_set")
        p2t_done = sem("p2t_done")
        p2t_set = sem("p2t_set")
        o2_done = sem("o2_done")
        o2_set = sem("o2_set")
        h2_set = sem("h2_set")
        conv_in = sem("conv_in")
        conv_out = sem("conv_out")
        silu_set = sem("silu_set")
        ff_set = sem("ff_set")
        fin_t = sem("fin_transposed")
        fin_set = sem("fin_set")
        stored = sem("stored")
        pool_passed = sem("pool_passed")
        sp_passed = sem("sp_passed")
        pe_passed = sem("pe_passed")

        block = ctx.enter_context(nc.Block())

        RM = []
        PHASES = [("mod0", 12), ("mod1", 12), ("mla_head", 2), ("mla_gate", 8), ("mla_out", 8),
                  ("s5_u", 8), ("s5_g", 8), ("glu", 32), ("s5_out", 8), ("wk_a", 2), ("w_in", 6), ("wk_b", 2), ("wv", 4),
                  ("w_out", 4), ("wq", 4), ("wo", 4), ("w_up", 22), ("w_down", 12)]
        ring_at = {}
        n = 0
        for name, k in PHASES:
            ring_at[name] = n
            n += k
        UNITS = [("stage0", 12), ("mla_head", 2), ("mla_gate", 8), ("mla_out", 4), ("s5_u", 8), ("s5_g", 8),
                 ("s5_out", 4), ("wk_a", 2), ("w_in", 6), ("wk_b", 2), ("wv", 4), ("w_out", 4),
                 ("wq", 4), ("wo", 4), ("w_up", 22), ("w_down", 4)]
        unit_at = {}
        n = 0
        for name, k in UNITS:
            unit_at[name] = n
            n += k

        @contextmanager
        def turns(eng, lot, per):
            assert lot % per == 0
            with eng.Fori(0, lot // per) as t:
                yield Step(t, per)

        @block.sync
        def _(sp):
            sp.dma_start(cst[:, :], a["consts"]).then_inc(const_in, 16)
            sp.dma_start(xtok[:, 0:2, :], a["ctx"].rearrange("b (t p) d -> p (b t) d", p=P)).then_inc(x_in, 16)
            sp.dma_start(xtok[:, 2:4, :], a["x"].rearrange("b (t p) d -> p (b t) d", p=P)).then_inc(x_in, 16)
            sp.wait_ge(vec_clear, 1)
            for t, names in enumerate(VEC_TILES):
                r = 0
                for name, rows in names:
                    v = a[name]
                    v = v.rearrange({1: "(r p) -> r p", 2: "l (r p) -> (l r) p", 3: "l k (r p) -> (l k r) p"}[len(v.shape)], p=P)
                    first = min(rows, P - r)
                    sp.dma_start(vrow[r:r + first, t, :], v[0:first, :]).then_inc(vec_in, 16)
                    if rows > first:
                        sp.dma_start(vrow[0:rows - first, t + 1, :], v[first:rows, :]).then_inc(vec_in, 16)
                    r += rows

            def load(slot, src):
                sp.dma_start(ring[:, slot, 0:src.shape[1], 0:src.shape[2]], src).then_inc(w_in_[slot], 16)

            def rows8(w, kg, c0, n=MT2, k=8):
                return w[kg * 8 * P:(kg * 8 + k) * P, bass.ds(c0, n)].rearrange("(c p) m -> p c m", p=P)

            wm = a["w_mod"]
            for s in range(NSLOT):
                load(s, rows8(wm[0], 0, s * MT2))
            for z, n in ((0, "s5_lam_re"), (1, "s5_lam_im")):
                sp.dma_start(lam_rows[:, z, :], a[n][0].rearrange("d (q g) s -> (d q) (g s)", g=2)).then_inc(s5par_in, 16)
            sp.dma_start(dt_raw, a["s5_log_dt"][0].rearrange("d (q g) -> (d q) g", g=2)).then_inc(s5par_in, 16)
            sp.dma_start(d_raw[0:GP5, :], a["s5_d"][0].rearrange("(q r) -> q r", q=GP5)).then_inc(s5par_in, 16)
            for s in range(4, 8):
                sp.wait_ge(slot_done, s - NSLOT + 1)
                load(s % NSLOT, rows8(wm[0], 0, s * MT2))
            for z, n in ((0, "s5_b_re"), (1, "s5_b_im")):
                sp.dma_start(raw_b[:, z, :], a[n][0].rearrange("d (q g) s c -> (d q) (g s c)", g=2)).then_inc(bc_raw_in, 16)
            for z, n in ((0, "s5_c_re"), (1, "s5_c_im")):
                for g in range(2):
                    sp.dma_start(raw_c[:, z, :].rearrange("p (c g s) -> p c g s", c=CH5, g=2)[:, :, g, :],
                                 a[n][0].rearrange("d (q g) c s -> g (d q) c s", g=2)[g]).then_inc(bc_raw_in, 16)
            for s in range(8, 12):
                sp.wait_ge(slot_done, s - NSLOT + 1)
                load(s % NSLOT, rows8(wm[0], 0, s * MT2))
            at = ring_at["mod1"]
            with turns(sp, 12, 4) as i:
                for s in range(NSLOT):
                    sp.wait_ge(slot_done, i + (at + s - NSLOT + 1))
                    sp.sem_inc(sp_passed, 1)
                    load(s, rows8(wm[1], 0, (i + s) * MT2))

            def stream(name, w, groups, units, last=8):
                at = ring_at[name]
                lot = groups * units
                whole = lot // NSLOT * NSLOT if NSLOT % groups == 0 else 0
                if whole > NSLOT:
                    with turns(sp, whole, NSLOT) as i:
                        for s in range(NSLOT):
                            sp.wait_ge(slot_done, i + (at + s - NSLOT + 1))
                            sp.sem_inc(sp_passed, 1)
                            c0 = (i + s) * MT2 if groups == 1 else i * (MT2 // groups) + s // groups * MT2
                            load((at + s) % NSLOT, rows8(w, s % groups, c0))
                else:
                    whole = 0
                for s in range(whole, lot):
                    sp.wait_ge(slot_done, at + s - NSLOT + 1)
                    kg = s % groups
                    load((at + s) % NSLOT, rows8(w, kg, s // groups * MT2, k=last if kg == groups - 1 else 8))

            wi = a["mla_w_in"][0]
            at = ring_at["mla_head"]
            for s, n in ((0, QR), (1, KVR + ROPE)):
                sp.wait_ge(slot_done, at + s - NSLOT + 1)
                load((at + s) % NSLOT, rows8(wi, 0, s * QR, n))
            stream("mla_gate", wi[:, QR + KVR + ROPE:], 1, 8)

            def load_heads(p, b):
                for c in range(2):
                    src = a["mla_w_uq"][0][c * P:(c + 1) * P, bass.ds(p * (2 * HQ), 2 * HQ)].rearrange("p (h m) -> p h m", h=2)
                    for lo, n, to in ((0, NOPE, 0), (NOPE, ROPE, 2 * NOPE)):
                        sp.dma_start(att_uq[b][:, c, to:to + 2 * n].rearrange("p (h m) -> p h m", h=2), src[:, :, lo:lo + n])\
                            .then_inc(att_in[b], 16)
                sp.dma_start(att_uk[b], a["mla_w_uk"][0].rearrange("c h d -> c (h d)")[:, bass.ds(p * (2 * NOPE), 2 * NOPE)])\
                    .then_inc(att_in[b], 16)
                sp.dma_start(att_uv[b], a["mla_w_uv"][0].rearrange("c h d -> c (h d)")[:, bass.ds(p * (2 * VDIM), 2 * VDIM)])\
                    .then_inc(att_in[b], 16)

            sp.wait_ge(bc_spilled, 32)
            sp.wait_ge(par_got, 6)
            for p in range(2):
                load_heads(p, p)
            with turns(sp, 6, 2) as i:
                for b in range(2):
                    sp.wait_ge(uv_done, i * 2 + (2 * b + 2))
                    sp.sem_inc(sp_passed, 1)
                    load_heads(i + (b + 2), b)
            stream("mla_out", a["mla_w_out"][0], 2, 4)
            w5 = a["s5_w_in"][0]
            stream("s5_u", w5[:, 0:E_BR], 1, 8)
            stream("s5_g", w5[:, E_BR:2 * E_BR], 1, 8)

            def load_b(b, par):
                sp.dma_start(bb[par].rearrange("p z d q c -> p (z d) (q c)"),
                             spill_b[:, :, bass.ds(b * (BLK * CH5), BLK * CH5)]).then_inc(bb_in[par], 16)

            def load_c(b):
                sp.dma_start(cc.rearrange("p z d q c -> p (z d) (q c)"),
                             spill_c[:, :, bass.ds(b * (BLK * CH5), BLK * CH5)]).then_inc(cc_in, 16)

            def spread(par):
                for s in range(L5):
                    for g in range(2):
                        lo = (L5 - 1 - s) * CH5
                        sp.dma_start(t0[par][s * CH5:(s + 1) * CH5, :, g, :],
                                     kf[g * CH5:(g + 1) * CH5, :, lo:lo + P]).then_inc(t0_in[par], 16)

            sp.wait_ge(av_set, HEADS)
            load_c(0)
            sp.wait_ge(slot_done, ring_at["mla_out"] + 8)
            for b in range(2):
                load_b(b, b)
            wg = a["s5_w_glu"][0]
            at = ring_at["glu"]
            assert at % NSLOT == 2
            for s in range(2):
                sp.wait_ge(slot_done, at + s - NSLOT + 1)
                load((at + s) % NSLOT, rows8(wg, s % 2, s // 2 * E_BR))
            sp.wait_ge(cc_read, 1)
            load_c(1)
            for b in range(2):
                sp.wait_ge(bt_set, 2 * b + 2)
                sp.wait_ge(bbd_set, b + 1)
                load_b(b + 2, b)
            sp.wait_ge(kf_set, 2)
            spread(0)
            sp.wait_ge(cc_read, 2)
            load_c(2)
            with turns(sp, 14, 2) as i:
                for par in range(2):
                    sp.wait_ge(kf_set, i * 2 + (2 * par + 4))
                    sp.sem_inc(sp_passed, 1)
                    spread(1 - par)
            sp.wait_ge(kf_set, 2 * NB5)
            spread(1)

            sp.wait_ge(cp_set, 2 * NB5)
            for s in range(2, NSLOT):
                load((at + s) % NSLOT, rows8(wg, s % 2, s // 2 * E_BR))
            sp.wait_ge(yt_set, NB5 + 1)
            sp.dma_start(mem_tok, a["mem_2"].rearrange("b (t p) d -> p (b t) d", p=P)).then_inc(mem_in, 16)
            sp.dma_start(pool_w, a["pool_w_2"][0].rearrange("g c d -> c g d")).then_inc(mix_in, 16)
            sp.dma_start(sgu_w, a["sgu_w_2"][0].rearrange("h t s -> t h s")).then_inc(mix_in, 16)
            sp.dma_start(sgu_bb.rearrange("p h t -> p (h t)"),
                         a["sgu_b_2"][0].rearrange("h t -> (h t)").partition_broadcast(P)).then_inc(mix_in, 16)
            with turns(sp, 28, NSLOT) as i:
                for s in range(NSLOT):
                    sp.wait_ge(slot_done, i + (at + s + 1))
                    sp.sem_inc(sp_passed, 1)
                    load((at + s) % NSLOT, rows8(wg, s % 2, i * (MT2 // 4) + (MT2 + s // 2 * E_BR)))
            stream("s5_out", a["s5_w_out"][0], 2, 4)
            stream("wk_a", a["wk_2"][0], 1, 2)
            stream("w_in", a["w_in_2"][0], 1, 6)
            stream("wk_b", a["wk_2"][0][:, 2 * MT2:4 * MT2], 1, 2)
            stream("wv", a["wv_2"][0], 1, 4)
            stream("w_out", a["w_out_2"][0], 1, 4)
            stream("wq", a["wq_2"][0], 1, 4)
            stream("wo", a["wo_2"][0], 1, 4)
            wu = a["w_up_2"][0]
            at = ring_at["w_up"]
            with turns(sp, 20, NSLOT) as i:
                for s in range(NSLOT):
                    sp.wait_ge(slot_done, i + (at + s - NSLOT + 1))
                    sp.sem_inc(sp_passed, 1)
                    load((at + s) % NSLOT, rows8(wu, 0, i * (MT2 // 2) + (s // 2 * MT2 + s % 2 * FF)))
            for s in range(20, 22):
                sp.wait_ge(slot_done, at + s - NSLOT + 1)
                load((at + s) % NSLOT, rows8(wu, 0, s // 2 * MT2 + s % 2 * FF))
            stream("w_down", a["w_down_2"][0], 3, 4, last=KF - 16)
            sp.wait_ge(fin_set, 4)
            sp.dma_start(out.rearrange("b (t p) d -> p (b t) d", p=P), orow).then_inc(stored, 16)
            sp.wait_ge(stored, 16)

        @block.tensor
        def _(pe):
            def free(u):
                return unit_free[u % 2], 2 * (u // 2)

            pe.wait_ge(const_in, 16)
            pe.wait_ge(vec_in, 16 * (sum(len(t) for t in VEC_TILES) + 1))
            for t in range(NVT):
                mm = pe.transpose(psum[4][:, t * P:(t + 1) * P], vrow[:, t, :], ident)
            mm.then_inc(vec_t, 1)
            pe.wait_ge(x_in, 32)
            for k in range(KD):
                u = k // 2
                if u >= 2 and k % 2 == 0:
                    pe.wait_ge(*free(u))
                for t in range(4):
                    mm = pe.transpose(psum[2 * (u % 2) + k % 2][:, t * P:(t + 1) * P],
                                      xtok[:, t, k * P:(k + 1) * P], ident)
                mm.then_inc(p0_t, 1)
            def s5_parameters():
                pe.wait_ge(s5par_in, 4 * 16)
                pe.wait_ge(dt_set, 1)
                for z in range(2):
                    pe.transpose(psum[5][:, z * P:(z + 1) * P], lam_rows[:, z, :], ident)
                pe.transpose(psum[5][:, 2 * P:3 * P], dt_exp.rearrange("p g s -> p (g s)"), ident)
                pe.transpose(psum[5][0:2 * CH5, 3 * P:3 * P + GP5], d_raw[0:GP5, :], ident[0:GP5, 0:GP5]).then_inc(par_t, 1)

            def s5_b_and_c():
                pe.wait_ge(bc_raw_in, 6 * 16)
                for f in range(16):
                    u = 4 + f // 2
                    if f % 2 == 0:
                        pe.wait_ge(*free(u))
                    z, c4 = f // 4, f % 4
                    for j in range(4):
                        c = 4 * c4 + j
                        if z < 2:
                            src = raw_b[:, z, :].rearrange("p (r c) -> p c r", c=CH5)[:, c, :]
                        else:
                            src = raw_c[:, z - 2, c * 2 * ST5:(c + 1) * 2 * ST5]
                        mm = pe.transpose(psum[2 * (u % 2) + f % 2][:, j * P:(j + 1) * P], src, ident)
                    mm.then_inc(p0_t, 1)

            pe.sem_inc(modrow_set, 2)

            def modulation(l, i, slots):
                at = ring_at[f"mod{l}"]
                for s in slots:
                    pe.wait_ge(w_in_[s % NSLOT], i * 4 + (16 * ((at + s) // NSLOT) + 16))
                    pe.wait_ge(modrow_set, i + (12 * l + s + 1))
                    for k in range(KD):
                        mm = pe.matmul(psum[6 + s % 2][0:2, 0:MT2], cond[:, k, :], ring[:, s % NSLOT, k, :],
                                       start=(k == 0), stop=(k == KD - 1))
                    mm.then_inc(slot_done, 1)

            def mod_columns(l):
                pe.wait_ge(modrow_set, 12 * l + 14)
                for m in range(24):
                    mm = pe.transpose(psum[4 + l][:, 2 * m:2 * m + 2], mod_rows[0:2, l, m * P:(m + 1) * P], ident[0:2, 0:2])
                mm.then_inc(modt_done, 1)

            pe.wait_ge(cond_set, 2)
            modulation(0, 0, range(NSLOT))
            s5_parameters()
            with turns(pe, 8, NSLOT) as i:
                modulation(0, i, range(NSLOT, 2 * NSLOT))
            mod_columns(0)
            s5_b_and_c()
            with turns(pe, 12, NSLOT) as i:
                modulation(1, i, range(NSLOT))
            pe.wait_ge(par_got, 1)
            mod_columns(1)

            def linear(name, groups, units, moving, last=8, first=0, ready=None):
                at, u0 = ring_at[name] + first * groups, unit_at[name] + first
                lot = groups * units

                def step(i, s):
                    sl = (at + s) % NSLOT
                    u, kg = u0 + s // groups, s % groups
                    pe.wait_ge(w_in_[sl], i * 4 + (16 * ((at + s) // NSLOT) + 16))
                    if kg == 0:
                        pe.wait_ge(unit_free[u % 2], (i if groups == 1 else i // 2) + 2 * (u // 2))
                    nk = last if kg == groups - 1 else 8
                    for m in range(2):
                        for k in range(nk):
                            mv = moving(kg * 8 + k)
                            if ready and s // groups == 0 and m == 0:
                                pe.wait_ge(*ready(kg * 8 + k))
                            mm = pe.matmul(psum[2 * (u % 2) + m][:, 0:mv.free_size()], ring[:, sl, k, m * P:(m + 1) * P], mv,
                                           start=(kg == 0 and k == 0), stop=(kg == groups - 1 and k == nk - 1))
                    mm.then_inc(slot_done, 1)

                whole = lot // NSLOT * NSLOT if NSLOT % groups == 0 and lot > NSLOT else 0
                if whole:
                    with turns(pe, whole, NSLOT) as i:
                        for s in range(NSLOT):
                            step(i, s)
                for s in range(whole, lot):
                    step(Step(0, NSLOT), s)

            pe.wait_ge(h_ctx, KD)
            pe.wait_ge(h_lat, KD)
            at, u0 = ring_at["mla_head"], unit_at["mla_head"]
            for s in range(2):
                sl = (at + s) % NSLOT
                pe.wait_ge(w_in_[sl], 16 * ((at + s) // NSLOT) + 16)
                pe.wait_ge(*free(u0 + s))
                for m in range(2):
                    M = ROPE if s == 1 and m == 1 else P
                    for k in range(KD):
                        mm = pe.matmul(psum[2 * s + m][0:M, :], ring[:, sl, k, m * P:m * P + M], ht[:, k, :],
                                       start=(k == 0), stop=(k == KD - 1))
                mm.then_inc(slot_done, 1)
            linear("mla_gate", 1, 4, lambda k: ht[:, k, :])
            pe.wait_ge(sq_set, 3)
            pe.matmul(psum[4][:, :], avg_q[:, :], sq1[:, 0, :], start=True, stop=False)
            pe.matmul(psum[4][:, :], avg_q[:, :], sq1[:, 1, :], start=False, stop=True).then_inc(stat, 1)
            pe.matmul(psum[5][:, :], avg_kv[:, :], sq1[:, 2, :], start=True, stop=True).then_inc(stat, 1)
            pe.matmul(psum[7][:, 0:S], rot, kr[:, S:T], start=True, stop=True).then_inc(stat, 1)
            linear("mla_gate", 1, 4, lambda k: ht[:, k, :], first=4)
            pe.wait_ge(normed, 3)
            for t in range(4):
                mm = pe.transpose(psum[6][:, t * P:(t + 1) * P], ckv[:, t * P:(t + 1) * P], ident)
            mm.then_inc(ctok_t, 1)
            pe.wait_ge(ctok_set, 1)
            pe.wait_ge(normed, 4)

            class Proj:

                def __init__(self, pair, before):
                    self.p, self.uses = pair, [before, before]

                def bank(self, b):
                    pe.wait_ge(proj_free[b], self.p * 5 + self.uses[b])
                    self.uses[b] += 1
                    return psum[b]

            def project(pr, b, h0_wait, pair):
                pe.wait_ge(att_in[b], h0_wait)

                def queries(bank, lo, hi):
                    for c in range(2):
                        mm = pe.matmul(bank[:, :], att_uq[b][:, c, lo:hi], qn[:, c, :], start=(c == 0), stop=(c == 1))
                    mm.then_inc(proj_done, 1)

                def keys(bank, h):
                    pe.matmul(bank[:, :], att_uk[b][:, h * NOPE:(h + 1) * NOPE], ckv, start=True, stop=True)\
                        .then_inc(proj_done, 1)

                queries(pr.bank(0), 2 * NOPE, 2 * HQ)
                queries(pr.bank(1), 0, NOPE)
                bank = pr.bank(0)
                pe.wait_ge(qk_set, pair * 5 + 1)
                pe.matmul(bank[:, 0:S], rot, q_rope[:, S:T], start=True, stop=True).then_inc(proj_done, 1)
                keys(pr.bank(1), 0)
                queries(pr.bank(0), NOPE, 2 * NOPE)
                keys(pr.bank(1), 1)

            def scores(pair, e, first):
                pe.wait_ge(qk_set, pair * 5 + (3 + 2 * e))
                pe.wait_ge(qrot_set, pair + 1)
                r = slice(e * ROPE, (e + 1) * ROPE)
                for t in range(4):
                    if not first:
                        pe.wait_ge(exp_done, pair * 8 + (4 * e + t - 3))
                    tok = slice(t * P, (t + 1) * P)
                    bank = psum[2 + t]
                    if t < 2:
                        pe.matmul(bank[:, 0:S], qh[e][:, tok], kh[e][:, 0:S], start=True, stop=False)
                        mm = pe.matmul(bank[:, 0:S], q_rope[r, tok], kr[r, 0:S], start=False, stop=True)
                    else:
                        pe.matmul(bank[:, 0:S], qh[e][:, tok], kh[e][:, 0:S], start=True, stop=False)
                        pe.matmul(bank[:, 0:S], q_rope[r, tok], kr[r, 0:S], start=False, stop=True)
                        pe.matmul(bank[:, S:T], qh[e][:, tok], kh[e][:, S:T], start=True, stop=False)
                        mm = pe.matmul(bank[:, S:T], q_rot[r, (t - 2) * P:(t - 1) * P], kr_rot[r, :], start=False, stop=True)
                    mm.then_inc(score_done, 1)

            def values(pr, pair, e, b, first):
                for f in range(3):
                    bank = psum[6 + (3 * e + f) % 2]
                    if not (first and f < 2):
                        if f == 2:
                            pe.wait_ge(pt_v, pair * 2 + (e + 1))
                        else:
                            pe.wait_ge(pt_a, pair * 4 + (2 * e + f - 1))
                    for t in ((0, 1), (2,), (3,))[f]:
                        pe.wait_ge(prob_set, pair * 8 + (4 * e + t + 1))
                        nk = 2 if t < 2 else 4
                        for k in range(nk):
                            at = (t * 2 + k) if t < 2 else k
                            mm = pe.transpose(bank[:, at * P:(at + 1) * P], prob[e][:, t, k * P:(k + 1) * P], ident)
                    mm.then_inc(pt_done, 1)
                bank = pr.bank(0)
                pe.wait_ge(pt_v, pair * 2 + (e + 1))
                for k in range(2):
                    pe.matmul(bank[:, 0:S], ckv_tok[:, k, :], pt_ctx[:, :, k, :], start=(k == 0), stop=(k == 1))
                pe.wait_ge(pt_a, pair * 4 + (2 * e + 2))
                for k in range(4):
                    mm = pe.matmul(bank[:, S:T], ckv_tok[:, k, :], pt_lat[:, :, k, :], start=(k == 0), stop=(k == 3))
                mm.then_inc(proj_done, 1)
                bank = pr.bank(1)
                pe.wait_ge(olat_set, pair * 2 + (e + 1))
                pe.matmul(bank[:, :], att_uv[b][:, e * VDIM:(e + 1) * VDIM], o_lat, start=True, stop=True).then_inc(uv_done, 1)

            pr = Proj(0, 0)
            project(pr, 0, 96, 0)
            scores(0, 0, True)
            scores(0, 1, False)
            values(pr, 0, 0, 0, True)

            def pair_step(p, b, wait_in):
                pr = Proj(p, -1)
                project(pr, b, wait_in, p)
                scores(p, 0, False)
                values(pr, p - 1, 1, 1 - b, False)
                scores(p, 1, False)
                values(pr, p, 0, b, False)

            pair_step(1, 1, 96)
            with turns(pe, 6, 2) as i:
                for b in range(2):
                    pair_step(i + (b + 2), b, i * 48 + 192)
            pr = Proj(PAIRS, -1)
            values(pr, PAIRS - 1, 1, 1, False)

            def layer_sums(n, with_ctx, base_new, meanwhile=None):
                pe.wait_ge(x_new, base_new)
                halves = ([(xc, 0)] if with_ctx else []) + [(xl, S)]
                for x, lo in halves:
                    for k in range(KD):
                        mm = pe.matmul(psum[4][:, lo:lo + S], avg_d[:, :], x[:, k, :], start=(k == 0), stop=(k == KD - 1))
                mm.then_inc(ln_sum, 1)
                if meanwhile:
                    meanwhile()
                for h, (x, lo) in enumerate(halves):
                    pe.wait_ge(ln_sq, n + h + 1)
                    for k in range(KD):
                        mm = pe.matmul(psum[5][:, lo:lo + S], avg_d[:, :], ht[:, k, lo:lo + S], start=(k == 0),
                                       stop=(k == KD - 1))
                mm.then_inc(ln_var, 1)

            pe.wait_ge(av_set, HEADS)
            linear("mla_out", 2, 4, lambda k: gate[:, k, :])
            layer_sums(0, True, 16)

            pe.wait_ge(h_ctx, 2 * KD)
            pe.wait_ge(h_lat, 2 * KD)
            at, u0 = ring_at["s5_u"], unit_at["s5_u"]
            for q in range(2):
                pe.sem_inc(ut_free[q], 4)
            def u_rows(i, s):
                sl, u = (at + s) % NSLOT, u0 + s
                pe.wait_ge(w_in_[sl], i * 4 + (16 * ((at + s) // NSLOT) + 16))
                pe.wait_ge(unit_free[u % 2], i + 2 * (u // 2))
                for s4 in range(4):
                    for k in range(KD):
                        mm = pe.matmul(psum[2 * (u % 2) + s4 // 2][:, s4 % 2 * S:(s4 % 2 + 1) * S],
                                       ht[:, k, s4 * P:(s4 + 1) * P], ring[:, sl, k, :], start=(k == 0), stop=(k == KD - 1))
                mm.then_inc(slot_done, 1)

            def u_columns(i, s):
                pe.wait_ge(utok_set, i * 2 + (2 * s + 2))
                for q in range(2):
                    pe.wait_ge(ut_free[q], i * 4 + (4 * s + 4))
                    for j in range(4):
                        g = (4 * q + j) * 2
                        mm = pe.transpose(psum[4 + q][:, j * P:(j + 1) * P],
                                          utok[s % 2][:, g:g + 2, :, :].rearrange("p g s c -> p (g s c)"), ident)
                    mm.then_inc(ut_done, 1)

            with turns(pe, 8, NSLOT) as i:
                u_rows(i, 0)
                for s in range(1, NSLOT):
                    u_rows(i, s)
                    u_columns(i, s - 1)
                u_columns(i, NSLOT - 1)
            linear("s5_g", 1, 8, lambda k: ht[:, k, :].rearrange("p (j c) -> p j c", c=NC5)[:, :, NCL:NC5])

            def tables(b, d):
                pe.wait_ge(bt_set, b * 2 + (d + 1))
                for z in range(2):
                    f = 2 * d + z
                    pe.wait_ge(bmat_set, b * 4 + max(f - 1, 0))
                    for q in range(BLK):
                        mm = pe.transpose(psum[z][:, q * P:(q + 1) * P], bt[:, z, d, q, :, :].rearrange("p s c -> p (s c)"), ident)
                    mm.then_inc(btt_done, 1)

            def responses(b, par):
                pe.wait_ge(bbd_set, b + 1)
                pe.wait_ge(kf_set, b * 2)
                for f in range(2):
                    pe.wait_ge(cp_set, b * 2 + (f + 1))
                    for j in range(2):
                        q = 2 * f + j
                        o = psum[2 + f][0:2 * CH5, j * KW5:(j + 1) * KW5]
                        for n, (d, z) in enumerate(((1, 0), (1, 1), (0, 0), (0, 1))):
                            lo = 0 if d == 1 else (L5 - 1) * CH5
                            mm = pe.matmul(o[:, lo:lo + P], bbd[par][:, z, d, q, :, :].rearrange("p g c -> p (g c)"),
                                           cp[par][:, z, d, q, :, :].rearrange("p i c -> p (i c)")[:, d * CH5:d * CH5 + P],
                                           start=(n == 0), stop=False, skip_group_check=True)
                        mm = pe.matmul(o[:, (L5 - 1) * CH5:L5 * CH5], ident[0:2 * CH5, 0:2 * CH5],
                                       d_block[par][0:2 * CH5, q, :],
                                       start=False, stop=True, skip_group_check=True)
                    mm.then_inc(kf_done, 1)

            def inputs(b, par):
                pe.wait_ge(bmat_set, b * 4 + 4)
                pe.wait_ge(ub_set, b + 1)
                pe.wait_ge(in_read, b)
                for z in range(2):
                    for d in range(2):
                        for q in range(BLK):
                            for g in range(2):
                                mv = ub[par][:, q, g, :].rearrange("p (h c) -> p h c", h=2)
                                if d == 1:
                                    mv = mv[:, :, ::-1]
                                mm = pe.matmul(psum[4 + z][g * ST5:(g + 1) * ST5, (d * BLK + q) * NC5:(d * BLK + q + 1) * NC5],
                                               bmat[:, z, d, q, g * ST5:(g + 1) * ST5], mv, start=True, stop=True)
                    mm.then_inc(in_done, 1)

            def outputs(b, par, n_use):
                pe.wait_ge(x5_set, b * 4 + 4)
                pe.wait_ge(yt_set, b + 1)
                pe.wait_ge(t0_in[par], n_use)
                for q in range(BLK):
                    for g in range(2):
                        r = slice(g * ST5, (g + 1) * ST5)
                        o = psum[6 + g][0:NCL, q * P:(q + 1) * P]
                        pe.matmul(o, ub[par][:, q, g, NCL:NC5], t0[par][:, q, g, :], start=True, stop=False)
                        for d in range(2):
                            for z, x in enumerate(x5[par]):
                                lo = CH5 if d == 0 else 0
                                mm = pe.matmul(o, x[r, d, q, :], cp[par][r, z, d, q, :, :].rearrange("p i c -> p (i c)")[:, lo:lo + P],
                                               start=False, stop=(d == 1 and z == 1))
                    if q == BLK // 2 - 1:
                        mm.then_inc(y_half, 1)
                mm.then_inc(y_done, 1)

            def back(b):
                pe.wait_ge(ytok_set, b * 4 + 4)
                pe.sem_inc(pe_passed, 1)
                for s4 in range(4):
                    mm = pe.transpose(psum[6][:, s4 * 64:(s4 + 1) * 64], ytok[0:64, s4, :], ident[0:64, 0:64])
                mm.then_inc(t2_done, 1)

            pe.sem_inc(yt_set, 1)
            pe.sem_inc(y_half, 1)
            pe.sem_inc(y_done, 1)
            for q in range(2):
                pe.wait_ge(unit_free[q], unit_at["s5_out"])
            for d in range(2):
                tables(0, d)
            inputs(0, 0)
            for d in range(2):
                tables(1, d)
            responses(0, 0)

            def block_step(b, par, n_use, tables_after):
                responses(b + 1, 1 - par)
                inputs(b + 1, 1 - par)
                if tables_after:
                    tables(b + 2, 0)
                outputs(b, par, n_use)
                if tables_after:
                    tables(b + 2, 1)
                back(b)

            with turns(pe, 14, 2) as i:
                for par in range(2):
                    block_step(i + par, par, i * 128 + 256, True)
            block_step(14, 0, 256 * 8, False)
            outputs(15, 1, 256 * 8)
            back(15)

            pe.wait_ge(yt_set, NB5 + 1)
            at = ring_at["glu"]
            for par in range(2):
                pe.sem_inc(glu_free[par], 2)
            with turns(pe, 32, 2 * NSLOT) as i:
                for par in range(2):
                    pe.wait_ge(glu_free[par], i // 4 + 2)
                    for s in range(NSLOT):
                        sl, kg = (at + s) % NSLOT, s % 2
                        pe.wait_ge(w_in_[sl], i * 4 + (16 * ((at + s) // NSLOT + par) + 16))
                        for m in range(2):
                            for k in range(8):
                                mm = pe.matmul(psum[4 * par + 2 * (s // 2) + m][:, 0:S], ring[:, sl, k, m * P:(m + 1) * P],
                                               yt[:, kg * 8 + k, :], start=(kg == 0 and k == 0), stop=(kg == 1 and k == 7))
                        mm.then_inc(slot_done, 1)
            pe.wait_ge(mem_set, 2)
            pe.wait_ge(glu_free[1], 2 + 2 * 4)
            for k in range(KD):
                for t in range(2):
                    mm = pe.transpose(psum[4 + k // 2][:, k % 2 * S + t * P:k % 2 * S + (t + 1) * P],
                                      mem_tok[:, t, k * P:(k + 1) * P], ident)
                if k % 2:
                    mm.then_inc(memt_done, 1)
            pe.wait_ge(glu_set, 20)
            linear("s5_out", 2, 4, lambda k: gl[:, k, :])
            pe.wait_ge(memt_set, KD)
            layer_sums(2, False, 16 + 8, lambda: linear("wk_a", 1, 1, lambda k: mem_t[:, k, :]))
            linear("wk_a", 1, 1, lambda k: mem_t[:, k, :], first=1)

            def mean_square(n):
                for k in range(KD):
                    pe.wait_ge(sq_done, n * KD + k + 1)
                    mm = pe.matmul(psum[4][:, 0:S], avg_d[:, :], sq[:, k, :], start=(k == 0), stop=(k == KD - 1))
                mm.then_inc(ms_done, 1)

            mean_square(0)
            linear("w_in", 1, 6, lambda k: xn[:, k, :], ready=lambda k: (xn_set, 0 + k + 1))
            pe.wait_ge(mix_in, 48)
            pe.wait_ge(dpool_set, 4)
            for g in range(4):
                mm = pe.matmul(psum[6 + g // 2][:, g % 2 * S:(g % 2 + 1) * S], pool_w[:, g, :], pp[1][:, g, 16:16 + S],
                               start=True, stop=True)
            mm.then_inc(pool_done, 1)
            for h in range(4):
                mm = pe.transpose(psum[5][:, h * P:(h + 1) * P], sgu_w[:, h, :], ident)
            mm.then_inc(sgu_stat, 1)
            pe.wait_ge(uv_set, 8)
            for k in range(4):
                mm = pe.matmul(psum[4][:, 0:S], avg_sgu[:, :], vv[:, k, :], start=(k == 0), stop=(k == 3))
            mm.then_inc(sgu_stat, 1)
            pe.wait_ge(vsq_set, 1)
            for k in range(4):
                mm = pe.matmul(psum[4][:, S:T], avg_sgu[:, :], sq[:, k, :], start=(k == 0), stop=(k == 3))
            mm.then_inc(sgu_stat, 1)
            linear("wk_b", 1, 2, lambda k: mem_t[:, k, :])
            at, u0 = ring_at["wv"], unit_at["wv"]
            for s in range(4):
                sl = (at + s) % NSLOT
                pe.wait_ge(w_in_[sl], 16 * ((at + s) // NSLOT) + 16)
                pe.wait_ge(*free(u0 + s))
                for m in range(2):
                    for k in range(KD):
                        mm = pe.matmul(psum[2 * ((u0 + s) % 2) + m][:, 0:MT2], mem_t[:, k, m * P:(m + 1) * P], ring[:, sl, k, :],
                                       start=(k == 0), stop=(k == KD - 1))
                mm.then_inc(slot_done, 1)
            pe.wait_ge(vn_set, 4)
            pe.wait_ge(cat_set, 4)
            for t in range(2):
                for k in range(4):
                    mm = pe.transpose(psum[6 + t][:, k * P:(k + 1) * P], vv[:, k, t * P:(t + 1) * P], ident)
                mm.then_inc(vt_done, 1)
            pe.wait_ge(vtok_set, 2)
            for h in range(4):
                for t in range(2):
                    mm = pe.matmul(psum[6 + h // 2][:, (h % 2) * S + t * P:(h % 2) * S + (t + 1) * P],
                                   vtok[:, t, h * P:(h + 1) * P], sgu_wt[:, h, :], start=True, stop=True)
            mm.then_inc(z_done, 1)
            pe.wait_ge(cat_set, 8)
            linear("w_out", 1, 4, lambda k: cat[:, k, :])
            mean_square(1)
            linear("wq", 1, 4, lambda k: xn[:, k, :], ready=lambda k: (xn_set, 8 + k + 1))
            pe.wait_ge(kv2_set, 16)
            pe.wait_ge(q2_set, 8)

            def scores2(h):
                for t in range(2):
                    if h >= 1:
                        pe.wait_ge(e2_done, 2 * h - 1 + t)
                    for c in range(2):
                        mm = pe.matmul(psum[4 + t][:, 0:S], q2[:, 2 * h + c, t * P:(t + 1) * P], k2[:, 2 * h + c, :],
                                       start=(c == 0), stop=(c == 1))
                    mm.then_inc(s2_done, 1)

            def values2(h):
                if h >= 1:
                    pe.wait_ge(p2t_set, h)
                for t in range(2):
                    pe.wait_ge(p2_set, 2 * h + t + 1)
                    for m in range(2):
                        mm = pe.transpose(psum[6][:, (2 * m + t) * P:(2 * m + t + 1) * P], prob2[:, h % 2, t, m * P:(m + 1) * P], ident)
                mm.then_inc(p2t_done, 1)
                pe.wait_ge(p2t_set, h + 1)
                if h >= 1:
                    pe.wait_ge(o2_set, h)
                for c in range(2):
                    for m in range(2):
                        mm = pe.matmul(psum[7][:, c * S:(c + 1) * S], v2[:, m, (2 * h + c) * P:(2 * h + c + 1) * P], prob2_t[:, m, :],
                                       start=(m == 0), stop=(m == 1))
                mm.then_inc(o2_done, 1)

            scores2(0)
            for h in range(XH):
                if h + 1 < XH:
                    scores2(h + 1)
                values2(h)
            pe.wait_ge(o2_set, XH)
            linear("wo", 1, 4, lambda k: o2[:, k, :])
            mean_square(2)
            linear("w_up", 1, 22, lambda k: xn[:, k, :], ready=lambda k: (xn_set, 16 + k + 1))
            pe.wait_ge(ff_set, KF + 2)
            linear("w_down", 3, 4, lambda k: ff[:, k, :], last=KF - 16)
            mean_square(3)
            pe.wait_ge(xn_set, 4 * KD)
            for t in range(2):
                for f in range(2):
                    for j in range(4):
                        mm = pe.transpose(psum[2 * t + f][:, j * P:(j + 1) * P], xn[:, 4 * f + j, t * P:(t + 1) * P], ident)
                    mm.then_inc(fin_t, 1)

        @block.scalar
        def _(act):
            link = Link(act, a_link)
            def root(o, mean, scale=1.0):
                act.activation(o, mean, ACT.Sqrt, bias=eps, scale=scale).then_inc(root_set, 1)

            act.wait_ge(vec_out, 1)
            for j, name in enumerate(("c_ctx", "c")):
                act.activation(cond[:, :, j], col[:, at_col[name]:at_col[name] + KD], ACT.Silu).then_inc(cond_set, 1)
            for k in range(1, KD, 2):
                act.wait_ge(p0_t, k + 1)
                act.copy(xc[:, k, :], psum[2 * (k // 2 % 2) + 1][:, 0:S]).then_inc(xt_act, 1)
                act.copy(xl[:, k, :], psum[2 * (k // 2 % 2) + 1][:, S:T]).then_inc(xt_act, 1)
                act.wait_ge(xt_act, k + 1)
                act.sem_inc(unit_free[k // 2 % 2], 1)
            def mod_rows_out(l, i, slots):
                at = ring_at[f"mod{l}"]
                for s in slots:
                    act.wait_ge(slot_done, i + (at + s + 1))
                    act.copy(mod_rows[0:2, l, bass.ds(i * MT2 + s * MT2, MT2)], psum[6 + s % 2][0:2, 0:MT2]).then_inc(modrow_set, 1)

            mod_rows_out(0, Step(0, NSLOT), range(NSLOT))
            mod_rows_out(0, Step(0, NSLOT), range(NSLOT, 2 * NSLOT))
            act.wait_ge(arg_set, 1)
            act.activation(pars[4], pars[3], ACT.Tanh, scale=0.5).then_inc(act_tanh, 1)
            act.wait_ge(arg_set, 2)
            act.activation(pars[6], pars[5], ACT.Sin, scale=0.5).then_inc(act_trig, 1)
            link(act.activation(pars[7], pars[5], ACT.Abs))
            act.activation(pars[7], pars[7], ACT.Sin, scale=-0.5, bias=half_pi).then_inc(act_trig, 1)

            def modulate(l):
                for k in range(KD):
                    o, x = ht[:, k, 0:S], xc[:, k, :]
                    if l == 1:
                        o = by_chunk(ht[:, k, :])[:, 0:NCL]
                        x = x.rearrange("p (c h s) -> p c h s", h=2, s=4)
                    act.activation(o, x, ACT.Identity, bias=mod[:, l, k, 0:1],
                                   scale=mod[:, l, KD + k, 0:1]).then_inc(h_ctx, 1)

            mod_rows_out(0, Step(0, NSLOT), range(2 * NSLOT, 3 * NSLOT))
            for f in range(16):
                act.wait_ge(p0_t, KD + f + 1)
                z, c4 = f // 4, f % 4
                dst = (bcol if z < 2 else ccol)[:, z % 2, :, 4 * c4:4 * c4 + 4].rearrange("p q c -> p c q")
                u = 4 + f // 2
                src = psum[2 * (u % 2) + f % 2][:, :].rearrange("p (c q) -> p c q", c=4)
                act.mul(dst, src, -1.0 if z == 3 else 1.0).then_inc(unit_free[u % 2], 1)
            with turns(act, 12, NSLOT) as i:
                mod_rows_out(1, i, range(NSLOT))
            act.wait_ge(mod_set, 1)
            act.wait_ge(xt_dve, KD)
            act.wait_ge(xt_act, KD)
            modulate(0)
            for j in range(2):
                act.wait_ge(qkv_copied, j + 1)
                act.activation(sq1[:, j, :], qd[:, j, :], ACT.Square).then_inc(sq_set, 1)
            act.wait_ge(qkv_copied, 3)
            act.activation(sq1[:, 2, :], kvd, ACT.Square).then_inc(sq_set, 1)
            at, u0 = ring_at["mla_gate"], unit_at["mla_gate"]
            act.wait_ge(bc_spilled, 32)
            def gate_silu(s):
                act.wait_ge(slot_done, at + s + 1)
                for m in range(2):
                    act.activation(gate[:, 2 * s + m, :], psum[2 * ((u0 + s) % 2) + m][:, :], ACT.Silu)\
                        .then_inc(unit_free[(u0 + s) % 2], 1)

            for s in range(4):
                gate_silu(s)
            act.wait_ge(stat, 2)
            for j in range(2):
                root(rs1[:, j, :], psum[4 + j][:, :])
            for s in range(4, 8):
                gate_silu(s)
            act.wait_ge(ctok_t, 1)
            act.copy(ckv_tok.rearrange("p k c -> p (k c)"), psum[6][:, :]).then_inc(ctok_set, 1)

            def project(pair, d0):
                act.wait_ge(proj_done, d0 + 1)
                act.copy(q_rope, psum[0][:, :]).then_inc(qk_set, 1)
                act.wait_ge(qk_set, pair * 5 + 1)
                act.sem_inc(proj_free[0], 1)
                for n, (f, o, b) in enumerate(((2, qh[0], 1), (4, kh[0], 1), (5, qh[1], 0), (6, kh[1], 1))):
                    act.wait_ge(proj_done, d0 + f)
                    act.copy(o, psum[b][:, :]).then_inc(qk_set, 1)
                    act.wait_ge(qk_set, pair * 5 + (n + 2))
                    act.sem_inc(proj_free[b], 1)

            def exps(pair, e):
                for t in range(4):
                    w = S if t < 2 else T
                    act.wait_ge(bias_set, pair * 8 + (4 * e + t + 1))
                    act.activation(prob[e][:, t, 0:w], psum[2 + t][:, 0:w], ACT.Exp, bias=sm[:, e, 1, t:t + 1],
                                   scale=SM_SCALE, accum_out=sm[:, e, 2, t:t + 1]).then_inc(exp_done, 1)

            def values(pair, e, d0):
                for t in range(2):
                    act.wait_ge(pt_done, pair * 6 + (3 * e + t + 2))
                    act.copy(pt_lat[:, t, :, :].rearrange("p k q -> p (k q)"), psum[6 + (3 * e + t + 1) % 2][:, :]).then_inc(pt_a, 1)
                act.wait_ge(proj_done, d0 + 1)
                act.copy(o_lat, psum[0][:, :]).then_inc(olat_set, 1)
                act.wait_ge(olat_set, pair * 2 + (e + 1))
                act.sem_inc(proj_free[0], 1)

            project(0, 0)
            exps(0, 0)
            exps(0, 1)
            values(0, 0, 6)

            def pair_step(p):
                d0 = p * 8 - 1
                project(p, d0)
                exps(p, 0)
                values(p - 1, 1, d0 + 6)
                exps(p, 1)
                values(p, 0, d0 + 7)

            pair_step(1)
            with turns(act, 6, 2) as i:
                for b in range(2):
                    pair_step(i + (b + 2))
            values(PAIRS - 1, 1, 8 * PAIRS - 1)

            def keys_out(s):
                at, u = (ring_at["wk_a"] + s, unit_at["wk_a"] + s) if s < 2 else (ring_at["wk_b"] + s - 2, unit_at["wk_b"] + s - 2)
                act.wait_ge(slot_done, at + 1)
                for m in range(2):
                    act.copy(k2[:, 2 * s + m, :], psum[2 * (u % 2) + m][:, 0:S]).then_inc(kv2_set, 1)
                act.wait_ge(kv2_set, 2 * s + 2)
                act.sem_inc(unit_free[u % 2], 2)

            def layer_norm(l, n, with_ctx):
                halves = ([(xc, 0)] if with_ctx else []) + [(xl, S)]
                for h, (x, lo) in enumerate(halves):
                    act.wait_ge(ln_centered, n + h + 1)
                    act.activation(ht[:, :, lo:lo + S], x[:, :, :], ACT.Square).then_inc(ln_sq, 1)
                if not with_ctx:
                    keys_out(0)
                act.wait_ge(ln_var, l + 1)
                w = slice(halves[0][1], T)
                root(ln_rs[:, w], psum[5][:, w])

            layer_norm(0, 0, True)
            act.wait_ge(ln_norm, 1)
            act.wait_ge(mod_set, 3)
            modulate(1)
            at, u0 = ring_at["s5_u"], unit_at["s5_u"]
            with turns(act, 8, NSLOT) as i:
                for s in range(NSLOT):
                    u = u0 + s
                    act.wait_ge(slot_done, i + (at + s + 1))
                    for m in range(2):
                        act.copy(utok[s % 2][:, :, 2 * m:2 * m + 2, :].rearrange("p g s c -> p s g c"),
                                 psum[2 * (u % 2) + m][:, :].rearrange("p (s g c) -> p s g c", s=2, c=CH5)).then_inc(utok_set, 1)
                    act.wait_ge(utok_set, i * 2 + (2 * s + 2))
                    act.sem_inc(unit_free[u % 2], 2)
            at, u0 = ring_at["s5_g"], unit_at["s5_g"]
            with turns(act, 8, NSLOT) as i:
                for s in range(4):
                    u = u0 + s
                    act.wait_ge(slot_done, i + (at + s + 1))
                    for m in range(2):
                        act.activation(gl[:, bass.ds(i * 2 + (2 * s + m), 1), :].rearrange("p a t -> p (a t)"),
                                       psum[2 * (u % 2) + m][:, 0:S], ACT.Silu).then_inc(unit_free[u % 2], 1)

            def trig(b):
                act.wait_ge(ang_set, b + 1)
                rd = r8[:, :].rearrange("p (d q) -> p d q", d=2)[:, :, bass.ds(b * BLK, BLK)].unsqueeze(3)
                act.copy(dec5[:, :, :, 1:NC5], rd.to_broadcast([P, 2, BLK, NC5 - 1]))
                act.activation(sin5, ang, ACT.Sin, scale=-TWO_PI_DOWN).then_inc(trig5, 1)
                link(act.activation(cos5, ang, ACT.Abs))
                act.activation(cos5, cos5, ACT.Sin, scale=-TWO_PI_DOWN, bias=half_pi).then_inc(trig5, 1)

            def bmats(b, d):
                for z in range(2):
                    act.wait_ge(btt_done, b * 4 + (2 * d + z + 1))
                    act.copy(bmat[:, z, d, :, :].rearrange("p q r -> p (q r)"), psum[z][:, :]).then_inc(bmat_set, 1)

            def u_block(b, par):
                act.copy(ub[par].rearrange("p q g c -> p (q g c)"),
                         u5.rearrange("p q g c -> p (q g c)")[:, bass.ds(b * (BLK * 2 * NC5), BLK * 2 * NC5)]).then_inc(ub_set, 1)

            def b_diagonal(b, par, n_use):
                act.wait_ge(bb_in[par], n_use)
                bbv = bb[par].rearrange("p z d q c -> p (z d q) c")
                bbdv = bbd[par].rearrange("p z d q g c -> p (z d q) g c")
                act.copy(d_block[par][0:2 * CH5].rearrange("p q c -> p (q c)"),
                         d_diag.rearrange("p q c -> p (q c)")[0:2 * CH5, bass.ds(b * (BLK * CH5), BLK * CH5)])
                act.copy(bbdv[0:ST5, :, 0, :], bbv[0:ST5, :, :])
                act.copy(bbdv[ST5:P, :, 1, :], bbv[ST5:P, :, :]).then_inc(bbd_set, 1)

            def kfs(b):
                for f in range(2):
                    act.wait_ge(kf_done, b * 2 + (f + 1))
                    act.copy(kf[0:2 * CH5, 2 * f:2 * f + 2, :].rearrange("p q w -> p (q w)"),
                             psum[2 + f][0:2 * CH5, 0:2 * KW5]).then_inc(kf_set, 1)

            def tokens(b):
                act.wait_ge(y_done, b + 2)
                for g in range(2):
                    for h in range(2):
                        act.copy(ytok[h * NCL:(h + 1) * NCL, :, :].rearrange("p s (q g c) -> p q s g c", q=BLK, g=2)[:, :, :, g, :],
                                 psum[6 + g][0:NCL, :].rearrange("p (q h s c) -> p q h s c", q=BLK, h=2, s=4)[:, :, h, :, :])\
                            .then_inc(ytok_set, 1)

            def back(b):
                act.wait_ge(t2_done, b + 1)
                act.activation(yt[:, bass.ds(b, 1), :].rearrange("p a t -> p (a t)"), psum[6][:, 0:S], ACT.Gelu_apprx_tanh)\
                    .then_inc(yt_set, 1)

            act.wait_ge(p_link, 1)
            act.wait_ge(diag_set, 1)
            b_diagonal(0, 0, 16)
            act.wait_ge(ut_free[0], 36)
            act.wait_ge(ut_free[1], 36)
            for b in range(2):
                u_block(b, b)
            for d in range(2):
                bmats(0, d)
            act.wait_ge(decays_clear, 1)
            trig(0)
            for d in range(2):
                bmats(1, d)
            b_diagonal(1, 1, 16)
            kfs(0)

            def block_step(b, par, n_use, more, with_b=True, with_c=True):
                act.wait_ge(x5_set, b * 4 + 4)
                trig(b + 1)
                act.wait_ge(t0_in[par], n_use * 16)
                kfs(b + 1)
                if more:
                    bmats(b + 2, 0)
                    b_diagonal(b + 2, par, n_use + 16)
                if with_c:
                    act.wait_ge(cc_read, b + 3)
                    act.dma_start(cc.rearrange("p z d q c -> p (z d) (q c)"),
                                  spill_c[:, :, bass.ds((b + 3) * (BLK * CH5), BLK * CH5)]).then_inc(cc_in, 16)
                tokens(b)
                if more:
                    u_block(b + 2, par)
                    bmats(b + 2, 1)
                back(b)
                if with_b:
                    act.wait_ge(bbd_set, b + 3)
                    act.wait_ge(bt_set, b * 2 + 6)
                    act.dma_start(bb[par].rearrange("p z d q c -> p (z d) (q c)"),
                                  spill_b[:, :, bass.ds((b + 4) * (BLK * CH5), BLK * CH5)]).then_inc(bb_in[par], 16)

            with turns(act, 12, 2) as i:
                link.begin(i // 2, 2)
                for par in range(2):
                    block_step(i + par, par, i * 8 + 16, True)
                link.end(6)
            block_step(12, 0, 8 * 14, True, False)
            block_step(13, 1, 8 * 14, True, False, False)
            block_step(14, 0, 8 * 16, False, False, False)
            tokens(15)
            back(15)

            act.wait_ge(mem_in, 16)
            for t in range(2):
                link(act.activation(mem_sq, mem_tok[:, t, :], ACT.Square, accum_out=mem_s[:, t, 0:1]))
            for t in range(2):
                root(mem_s[:, t, 1:2], mem_s[:, t, 0:1], 1.0 / D)
            at = ring_at["glu"]
            act.sem_inc(glu_set, 4)
            with turns(act, 32, 2 * NSLOT) as i:
                for par in range(2):
                    act.wait_ge(slot_done, i + (at + 4 * par + 4))
                    act.wait_ge(glu_set, i // 2 + (2 * par + 2))
                    for m in range(2):
                        act.activation(sgm[:, par, m, :], psum[4 * par + 2 + m][:, 0:S], ACT.Sigmoid,
                                       bias=vecr("s5_b_glu", i // 2 + (2 * par + 16 + m))).then_inc(sg_set, 1)
            at, u0 = ring_at["s5_out"], unit_at["s5_out"]
            with turns(act, 8, NSLOT) as i:
                for s in range(2):
                    u = u0 + s
                    act.wait_ge(slot_done, i + (at + 2 * s + 2))
                    for m in range(2):
                        act.wait_ge(x_new, i + (16 + 2 * s + m - 4 + 1))
                        g = mod[:, 1, :, :].rearrange("p m j -> p (m j)")[:, bass.ds(i * 2 + (2 * (2 * s + m) + 4 * KD + 1), 1)]
                        act.activation(sy[:, 2 * s + m, :], psum[2 * (u % 2) + m][:, 0:S], ACT.Copy, scale=g).then_inc(sy_set, 1)
                    act.wait_ge(sy_set, i + (2 * s + 2))
                    act.sem_inc(unit_free[u % 2], 2)
            def squares(n, sem, base):
                for k in range(KD):
                    act.wait_ge(sem, base + k + 1)
                    act.activation(sq[:, k, :], xl[:, k, :], ACT.Square).then_inc(sq_done, 1)

            def root_mean(n):
                act.wait_ge(ms_done, n + 1)
                root(rstd, psum[4][:, 0:S])

            layer_norm(1, 2, False)
            act.wait_ge(ln_norm, 3)
            for k in range(KD):
                act.activation(xl[:, k, :], xl[:, k, :], ACT.Identity, bias=vec("ln_b", KD + k), scale=vec("ln_g", KD + k))\
                    .then_inc(ln_out, 1)
            squares(0, ln_out, 0)
            keys_out(1)
            root_mean(0)
            at, u0 = ring_at["w_in"], unit_at["w_in"]
            for s in range(2, 6):
                act.wait_ge(slot_done, at + s + 1)
                for m in range(2):
                    t = 2 * (s - 2) + m
                    dst = uu[:, t, :] if t < 4 else vv[:, t - 4, :]
                    act.activation(dst, psum[2 * ((u0 + s) % 2) + m][:, 0:S], ACT.Gelu).then_inc(uv_set, 1)
                act.wait_ge(uv_set, 2 * (s - 1))
                act.sem_inc(unit_free[(u0 + s) % 2], 2)
            act.wait_ge(vn_set, 1)
            act.wait_ge(ms_done, 1)
            act.activation(sq[:, 0:4, :], vv, ACT.Square).then_inc(vsq_set, 1)
            act.wait_ge(sgu_stat, 3)
            root(rstd, psum[4][:, S:T])
            for s in range(2, 4):
                keys_out(s)
            at, u0 = ring_at["wv"], unit_at["wv"]
            for s in range(4):
                act.wait_ge(slot_done, at + s + 1)
                for m in range(2):
                    act.copy(v2[:, m, s * MT2:(s + 1) * MT2], psum[2 * ((u0 + s) % 2) + m][:, 0:MT2]).then_inc(kv2_set, 1)
                act.wait_ge(kv2_set, 8 + 2 * s + 2)
                act.sem_inc(unit_free[(u0 + s) % 2], 2)
            squares(1, h2_set, 0)
            root_mean(1)
            at, u0 = ring_at["wq"], unit_at["wq"]
            for s in range(4):
                act.wait_ge(slot_done, at + s + 1)
                for m in range(2):
                    act.copy(q2[:, 2 * s + m, :], psum[2 * ((u0 + s) % 2) + m][:, 0:S]).then_inc(q2_set, 1)
                act.wait_ge(q2_set, 2 * s + 2)
                act.sem_inc(unit_free[(u0 + s) % 2], 2)
            for h in range(XH):
                for t in range(2):
                    act.wait_ge(b2_set, 2 * h + t + 1)
                    if h >= 2 and t == 0:
                        act.wait_ge(p2t_done, h - 1)
                    act.activation(prob2[:, h % 2, t, :], psum[4 + t][:, 0:S], ACT.Exp, bias=sm2[:, h % 2, t, 1:2],
                                   scale=float(XHD) ** -0.5, accum_out=sm2[:, h % 2, t, 2:3]).then_inc(e2_done, 1)
            squares(2, h2_set, 8)
            root_mean(2)

            at, u0 = ring_at["w_up"], unit_at["w_up"]

            def conv(i, s, j):
                u = u0 + s
                act.wait_ge(slot_done, i + (at + s + 1))
                for m in range(2):
                    h = s % 2 * 2 + m
                    ch = j * 2 + (m + s % 2 * KF)
                    act.wait_ge(ff_set, j * 2 + 2)
                    link(act.copy(hp[:, h, 2:2 + S], psum[2 * (u % 2) + m][:, 0:S]))
                    act.activation(cv[:, h, :], psum[2 * (u % 2) + m][:, 0:S], ACT.Identity, bias=vecr("conv_b_2", ch),
                                   scale=vecr("conv_w_2", ch + 2 * 2 * KF)).then_inc(unit_free[u % 2], 1)
                    act.wait_ge(unit_free[u % 2], i + (2 * (u // 2) + m + 1))
                    act.sem_inc(conv_in, 1)

            def silu(j):
                for m in range(2):
                    act.wait_ge(conv_out, j * 4 + (m + 1))
                    act.activation(cv[:, m, :], cv[:, m, :], ACT.Silu).then_inc(silu_set, 1)

            act.wait_ge(ones_set, 2)
            act.sem_inc(ff_set, 2)
            with turns(act, 20, NSLOT) as i:
                link.begin(i // 4, 8)
                for s in range(NSLOT):
                    conv(i, s, i // 2 + s // 2)
                    if s % 2:
                        silu(i // 2 + s // 2)
                link.end(5)
            for s in range(20, 22):
                conv(0, s, 10)
            silu(10)
            squares(3, h2_set, 16)
            root_mean(3)
            for t in range(2):
                act.wait_ge(fin_t, 2 * t + 2)
                act.copy(orow[:, t, 512:1024], psum[2 * t + 1][:, :]).then_inc(fin_set, 1)

        @block.vector
        def _(dve):
            link = Link(dve, v_link)
            tt, ts, stt = dve.tensor_tensor, dve.tensor_scalar, dve.scalar_tensor_tensor
            dve.memset(vrow, 0.0).then_inc(vec_clear, 1)
            for v, n in ((avg_d, D), (avg_q, QR), (avg_kv, KVR)):
                link(dve.memset(v[:, :], 1.0 / n))
            dve.memset(avg_sgu[:, :], 1.0 / 512).then_inc(ones_set, 1)
            dve.wait_ge(vec_t, 1)
            dve.tensor_copy(col[:, :], psum[4][:, :]).then_inc(vec_out, 1)
            for k in range(0, KD, 2):
                dve.wait_ge(p0_t, k + 1)
                dve.tensor_copy(xc[:, k, :], psum[2 * (k // 2 % 2)][:, 0:S]).then_inc(xt_dve, 1)
                dve.tensor_copy(xl[:, k, :], psum[2 * (k // 2 % 2)][:, S:T]).then_inc(xt_dve, 1)
                dve.wait_ge(xt_dve, k + 2)
                dve.sem_inc(unit_free[k // 2 % 2], 1)

            dve.wait_ge(s5par_in, 4 * 16)
            x, n, r, p, m, e = dt_t
            link(ts(x, dt_raw, 88.0, -87.0, ALU.min, ALU.max))
            link(ts(n, x, LOG2E, MAGIC, ALU.mult, ALU.add))
            link(ts(n, n, -MAGIC, None, ALU.add))
            link(stt(out=r, in0=n, scalar=-LN2_HI, in1=x, op0=ALU.mult, op1=ALU.add))
            link(stt(out=r, in0=n, scalar=-LN2_LO, in1=r, op0=ALU.mult, op1=ALU.add))
            link(ts(p, r, 1.0 / 5040, 1.0 / 720, ALU.mult, ALU.add))
            for c in (1.0 / 120, 1.0 / 24, 1.0 / 6, 0.5, 1.0, 1.0):
                link(tt(p, p, r, ALU.mult))
                link(ts(p, p, c, None, ALU.add))
            link(ts(m, n, 127.0, 8388608.0, ALU.add, ALU.mult))
            link(dve.tensor_copy(e.bitcast(I32), m))
            link(tt(p, p, e, ALU.mult))
            dve.tensor_copy(dt_exp, p.unsqueeze(2).to_broadcast([P, 2, ST5])).then_inc(dt_set, 1)
            def modulation(l):
                b = at_col["b_mod"] + 24 * l
                dve.wait_ge(modt_done, l + 1)
                link(tt(mod[:, l, :, :], psum[4 + l][:, 0:48].rearrange("p (m j) -> p m j", j=2),
                        col[:, b:b + 24].unsqueeze(2).to_broadcast([P, 24, 2]), ALU.add))
                ts(mod[:, l, KD:2 * KD, :], mod[:, l, KD:2 * KD, :], 1.0, None, ALU.add).then_inc(mod_set, 1)

            dve.wait_ge(par_t, 1)
            lr, li, dt, ar, tn, th, sh, ch, E, er, s2, cs, sn, nr, den, t1, t2, fr, fi, x9 = pars
            lbr, lbi = nr, sn
            link(ts(lr, psum[5][:, 0:P], -1e-4, None, ALU.min))
            link(dve.tensor_copy(li, psum[5][:, P:2 * P]))
            link(dve.tensor_copy(dt, psum[5][:, 2 * P:3 * P]))
            dve.tensor_copy(dcol[0:2 * CH5, :], psum[5][0:2 * CH5, 3 * P:3 * P + GP5]).then_inc(par_got, 1)
            tt(ar, lr, dt, ALU.mult).then_inc(arg_set, 1)
            link(tt(t1, li, dt, ALU.mult))
            link(ts(t2, t1, INV_2PI, MAGIC, ALU.mult, ALU.add))
            link(ts(t2, t2, -MAGIC, None, ALU.add))
            link(stt(out=t1, in0=t2, scalar=-PI2_A, in1=t1, op0=ALU.mult, op1=ALU.add))
            link(stt(out=t1, in0=t2, scalar=-PI2_B, in1=t1, op0=ALU.mult, op1=ALU.add))
            link(stt(out=t1, in0=t2, scalar=-PI2_C, in1=t1, op0=ALU.mult, op1=ALU.add))
            ts(th, t1, 3.1415925, -3.1415925, ALU.min, ALU.max).then_inc(arg_set, 1)
            dve.wait_ge(arg_set, 2)
            link(ts(t1, th, INV_2PI * L5, None, ALU.mult))
            link(ts(t2, t1, MAGIC, None, ALU.add))
            link(ts(t2, t2, -MAGIC, None, ALU.add))
            tt(phi[:, :], t1, t2, ALU.subtract).then_inc(par_got, 1)
            dve.wait_ge(par_got, 2)
            dve.wait_ge(act_tanh, 1)
            link(ts(t1, tn, -1.0, 1.0, ALU.mult, ALU.add))
            link(dve.reciprocal(t1, t1))
            link(stt(out=E, in0=tn, scalar=2.0, in1=t1, op0=ALU.mult, op1=ALU.mult))
            link(ts(er, E, 1.0, None, ALU.add))
            dve.wait_ge(act_trig, 2)
            link(stt(out=s2, in0=sh, scalar=2.0, in1=sh, op0=ALU.mult, op1=ALU.mult))
            link(ts(cs, s2, -1.0, 1.0, ALU.mult, ALU.add))
            link(stt(out=sn, in0=sh, scalar=2.0, in1=ch, op0=ALU.mult, op1=ALU.mult))
            link(tt(lbi, er, sn, ALU.mult))
            link(tt(t1, E, cs, ALU.mult))
            link(tt(t1, t1, s2, ALU.subtract))
            link(tt(lbr, er, cs, ALU.mult))
            link(tt(den, lr, lr, ALU.mult))
            link(tt(t2, li, li, ALU.mult))
            link(tt(den, den, t2, ALU.add))
            link(dve.reciprocal(den, den))
            link(tt(fr, t1, lr, ALU.mult))
            link(tt(t2, lbi, li, ALU.mult))
            link(tt(fr, fr, t2, ALU.add))
            link(tt(fr, fr, den, ALU.mult))
            link(tt(fi, lbi, lr, ALU.mult))
            link(tt(t2, t1, li, ALU.mult))
            link(tt(fi, fi, t2, ALU.subtract))
            link(tt(fi, fi, den, ALU.mult))
            link(tt(t1, er, er, ALU.mult))
            link(tt(t1, t1, t1, ALU.mult))
            tt(r8[:, :], t1, t1, ALU.mult).then_inc(par_got, 1)
            dve.wait_ge(p0_t, KD)
            link(dve.memset(pn[:, 0, 0, :], 1.0))
            link(dve.memset(pn[:, 1, 0, :], 0.0))
            link(dve.tensor_copy(pn[:, 0, 1, :], lbr))
            link(dve.tensor_copy(pn[:, 1, 1, :], lbi))

            def cmul(lo, n, u, w):
                o, x = slice(lo, lo + n), slice(u, u + n)
                br = pn[:, 0, w:w + 1, :].to_broadcast([P, n, P])
                bi = pn[:, 1, w:w + 1, :].to_broadcast([P, n, P])
                a1 = raw_tmp[:, 0:n, :]
                a2 = raw_tmp[:, n:2 * n, :]
                link(tt(a1, pn[:, 0, x, :], br, ALU.mult))
                link(tt(a2, pn[:, 1, x, :], bi, ALU.mult))
                link(tt(pn[:, 0, o, :], a1, a2, ALU.subtract))
                link(tt(a1, pn[:, 0, x, :], bi, ALU.mult))
                link(tt(a2, pn[:, 1, x, :], br, ALU.mult))
                link(tt(pn[:, 1, o, :], a1, a2, ALU.add))

            raw_tmp = carve(2 * NPW * P, 8, P)
            cmul(2, 1, 1, 1)
            cmul(3, 2, 1, 2)
            cmul(5, 4, 1, 4)
            dve.tensor_copy(pw[:, :, :, 0:GP5], pn[:, :, :, 0:GP5]).then_inc(par_got, 1)
            for z in range(2):
                dve.tensor_copy(pw[:, z, :, GP5:P], pn[:, z, ::-1, GP5:P]).then_inc(par_got, 1)
            def modulate(l):
                for k in range(KD):
                    o, x = ht[:, k, S:T], xl[:, k, :]
                    if l == 1:
                        o = by_chunk(ht[:, k, :])[:, NCL:NC5]
                        x = x.rearrange("p (c h s) -> p c h s", h=2, s=4)
                    ts(o, x, mod[:, l, KD + k, 1:2], mod[:, l, k, 1:2], ALU.mult, ALU.add)\
                        .then_inc(h_lat, 1)

            modulation(0)
            dve.wait_ge(mod_set, 1)
            dve.wait_ge(xt_dve, KD)
            dve.wait_ge(xt_act, KD)
            modulate(0)
            dve.wait_ge(unit_free[0], 12)
            dve.wait_ge(unit_free[1], 12)
            frb = fr.unsqueeze(2).to_broadcast([P, P, CH5])
            fib = fi.unsqueeze(2).to_broadcast([P, P, CH5])
            link(tt(tmp_b[:, 0], bcol[:, 0], frb, ALU.mult))
            link(tt(tmp_b[:, 1], bcol[:, 1], fib, ALU.mult))
            link(tt(tmp_b[:, 0], tmp_b[:, 0], tmp_b[:, 1], ALU.subtract))
            link(tt(tmp_b[:, 1], bcol[:, 0], fib, ALU.mult))
            link(tt(bcol[:, 1], bcol[:, 1], frb, ALU.mult))
            link(tt(bcol[:, 1], bcol[:, 1], tmp_b[:, 1], ALU.add))
            dve.tensor_copy(bcol[:, 0], tmp_b[:, 0]).then_inc(bc_scaled, 1)

            modulation(1)
            dve.wait_ge(mod_set, 2)
            gain, bias = (col[:, at_col[n]:at_col[n] + KD].unsqueeze(2).to_broadcast([P, KD, 2]) for n in ("ln_g", "ln_b"))
            link(tt(cond[:, :, :], mod[:, 1, KD:2 * KD, :], bias, ALU.mult))
            link(tt(mod[:, 1, 0:KD, :], mod[:, 1, 0:KD, :], cond[:, :, :], ALU.add))
            tt(mod[:, 1, KD:2 * KD, :], mod[:, 1, KD:2 * KD, :], gain, ALU.mult).then_inc(mod_set, 1)
            dve.wait_ge(bc_spilled, 32)
            at = ring_at["mla_head"]
            dve.wait_ge(slot_done, at + 1)
            for j in range(2):
                dve.tensor_copy(qd[:, j, :], psum[j][:, :]).then_inc(qkv_copied, 1)
            dve.wait_ge(qkv_copied, 2)
            dve.sem_inc(unit_free[unit_at["mla_head"] % 2], 2)
            dve.wait_ge(slot_done, at + 2)
            dve.tensor_copy(kvd, psum[2][:, :]).then_inc(qkv_copied, 1)
            for h in range(2):
                link(dve.tensor_copy(kr[h * ROPE:(h + 1) * ROPE, :], psum[3][0:ROPE, :]))
            dve.wait_ge(qkv_copied, 3)
            dve.sem_inc(unit_free[1 - unit_at["mla_head"] % 2], 2)
            dve.wait_ge(root_set, 2)
            for j in range(2):
                link(dve.reciprocal(rs1[:, j, :], rs1[:, j, :]))
            for j in range(2):
                stt(out=qn[:, j, :], in0=qd[:, j, :], scalar=vec("mla_q_norm", j), in1=rs1[:, 0, :], op0=ALU.mult, op1=ALU.mult)\
                    .then_inc(normed, 1)
            stt(out=ckv, in0=kvd, scalar=vec("mla_kv_norm", 0), in1=rs1[:, 1, :], op0=ALU.mult, op1=ALU.mult).then_inc(normed, 1)
            dve.wait_ge(stat, 3)
            link(tt(rot_t, psum[7][:, 0:S], sin, ALU.mult))
            link(tt(kr_rot, kr[:, S:T], cos, ALU.mult))
            tt(kr_rot, kr_rot, rot_t, ALU.add).then_inc(normed, 1)

            def rope(pair, d0):
                dve.wait_ge(qk_set, pair * 5 + 1)
                link(tt(q_rot, q_rope[:, S:T], cos, ALU.mult))
                dve.wait_ge(proj_done, d0 + 3)
                link(tt(rot_t, psum[0][:, 0:S], sin, ALU.mult))
                dve.sem_inc(proj_free[0], 1)
                tt(q_rot, q_rot, rot_t, ALU.add).then_inc(qrot_set, 1)

            def maxima(pair, e):
                for t in range(4):
                    w = S if t < 2 else T
                    dve.wait_ge(score_done, pair * 8 + (4 * e + t + 1))
                    link(dve.tensor_reduce(sm[:, e, 0, t:t + 1], psum[2 + t][:, 0:w], AX.X, ALU.max))
                    ts(sm[:, e, 1, t:t + 1], sm[:, e, 0, t:t + 1], -SM_SCALE, None, ALU.mult).then_inc(bias_set, 1)

            def normalise(pair, e):
                for t in range(4):
                    w = S if t < 2 else T
                    dve.wait_ge(exp_done, pair * 8 + (4 * e + t + 1))
                    link(dve.reciprocal(sm[:, e, 3, t:t + 1], sm[:, e, 2, t:t + 1]))
                    ts(prob[e][:, t, 0:w], prob[e][:, t, 0:w], sm[:, e, 3, t:t + 1], None, ALU.mult).then_inc(prob_set, 1)

            def turned(pair, e):
                dve.wait_ge(pt_done, pair * 6 + (3 * e + 1))
                dve.tensor_copy(prob_t[:, 0:512], psum[6 + e][:, :]).then_inc(pt_v, 1)

            def values(pair, e):
                dve.wait_ge(uv_done, pair * 2 + (e + 1))
                g = gate[:, bass.ds(pair * 2 + e, 1), :].rearrange("p a t -> p (a t)")
                tt(g, psum[1][:, :], g, ALU.mult).then_inc(av_set, 1)
                dve.wait_ge(av_set, pair * 2 + (e + 1))
                dve.sem_inc(proj_free[1], 1)

            rope(0, 0)
            maxima(0, 0)
            normalise(0, 0)
            maxima(0, 1)
            turned(0, 0)
            normalise(0, 1)
            values(0, 0)

            def pair_step(p):
                rope(p, p * 8 - 1)
                maxima(p, 0)
                turned(p - 1, 1)
                normalise(p, 0)
                values(p - 1, 1)
                maxima(p, 1)
                turned(p, 0)
                normalise(p, 1)
                values(p, 0)

            pair_step(1)
            with turns(dve, 6, 2) as i:
                link.begin(i // 2, 2 * 18)
                for b in range(2):
                    pair_step(i + (b + 2))
                link.end(3)
            turned(PAIRS - 1, 1)
            values(PAIRS - 1, 1)

            at, u0 = ring_at["mla_out"], unit_at["mla_out"]

            def residual(i, s, l, with_ctx, at, u0, m0, count):
                u = u0 + s
                dve.wait_ge(slot_done, count)
                for m in range(2):
                    k = m0 + (2 * s + m)
                    bank = psum[2 * (u % 2) + m]
                    lo = S if with_ctx else 0
                    for j, x in ((0, xc), (1, xl)):
                        if j == 0 and not with_ctx:
                            continue
                        xk = x[:, bass.ds(k, 1), :].rearrange("p a t -> p (a t)")
                        g = mod[:, l, :, :].rearrange("p m j -> p (m j)")[:, bass.ds(k * 2 + (4 * KD + j), 1)]
                        stt(out=xk, in0=bank[:, j * lo:j * lo + S], scalar=g, in1=xk, op0=ALU.mult, op1=ALU.add)\
                            .then_inc(x_new, 1)

            dve.wait_ge(alpha_set, 2)
            with turns(dve, 8, NSLOT) as i:
                for s in range(2):
                    residual(i, s, 0, True, at, u0, i, i + (at + 2 * s + 2))
                    dve.wait_ge(x_new, i * 2 + 4 * (s + 1))
                    dve.sem_inc(unit_free[(u0 + s) % 2], 2)

            def layer_norm(n, with_ctx, sums):
                halves = ([(xc, 0)] if with_ctx else []) + [(xl, S)]
                dve.wait_ge(ln_sum, sums)
                for x, lo in halves:
                    tt(x[:, :, :], x[:, :, :], psum[4][:, lo:lo + S].unsqueeze(1).to_broadcast([P, KD, S]), ALU.subtract)\
                        .then_inc(ln_centered, 1)
                dve.wait_ge(root_set, 3 if with_ctx else 6)
                w = slice(halves[0][1], T)
                link(dve.reciprocal(ln_rs[:, w], ln_rs[:, w]))
                for x, lo in halves:
                    tt(x[:, :, :], x[:, :, :], ln_rs[:, lo:lo + S].unsqueeze(1).to_broadcast([P, KD, S]), ALU.mult)\
                        .then_inc(ln_norm, 1)

            dve.wait_ge(ln_sum, 1)
            layer_norm(0, True, 1)
            dve.wait_ge(ln_norm, 2)
            dve.wait_ge(mod_set, 3)
            modulate(1)
            dve.wait_ge(h_lat, 2 * KD)
            for k in range(KD):
                ts(xl[:, k, :], xl[:, k, :], vec("ln_g", k), vec("ln_b", k), ALU.mult, ALU.add).then_inc(ln_lat, 1)

            with turns(dve, 8, NSLOT) as i:
                for s in range(NSLOT):
                    for q in range(2):
                        dve.wait_ge(ut_done, i * 2 + (2 * s + q + 1))
                        src = psum[4 + q][:, :].rearrange("p (q h c) -> p q h c", q=4, h=2)
                        for g in range(2):
                            for h in range(2):
                                dve.tensor_copy(u5[h * 64:(h + 1) * 64, bass.ds(i * 8 + (8 * s + 4 * q), 4), g, :],
                                                src[g * 64:(g + 1) * 64, :, h, :]).then_inc(ut_free[q], 1)

            def c_products(b, first=False):
                dve.wait_ge(cc_in, b * 16 + 16)
                dims = [P, BLK, NPW, CH5]
                link.upto(0)
                for v, way in ((gen_v, 1), (gen_w, -1)):
                    if way == -1:
                        link.upto(3)
                    if first and way == -1:
                        dve.wait_ge(slot_done, ring_at["s5_g"] + 8)
                    for d in range(2):
                        pr, pi = (pw[:, z, :, bass.ds(b * BLK + d * GP5, BLK)].rearrange("p i q -> p q i").unsqueeze(3)
                                  .to_broadcast(dims) for z in range(2))
                        for x, pz in enumerate((pr, pi)):
                            c = cc[:, x if way == 1 else 1 - x, d, :, :].unsqueeze(2).to_broadcast(dims)
                            o = tt(v[d][x].rearrange("p (q i c) -> p q i c", q=BLK, i=NPW), c, pz, ALU.mult)
                            if (way, d, x) == (-1, 1, 1):
                                o.then_inc(cc_read, 1)
                            else:
                                link.post(o)

            def c_sums(b, par):
                half = BLK // 2
                link.upto(0)
                dve.wait_ge(cc_read, b + 1)
                for f, read in enumerate((y_half, y_done)):
                    dve.wait_ge(read, b)
                    for z, (v, op) in enumerate(((gen_v, ALU.add), (gen_w, ALU.subtract))):
                        for d in range(2):
                            x, y = (v[d][n].rearrange("p (q r) -> p q r", q=BLK)[:, f * half:(f + 1) * half, :] for n in range(2))
                            o = tt(cp[par][:, z, d, f * half:(f + 1) * half].rearrange("p q i c -> p q (i c)"), x, y, op)
                            if z == 0 or d == 0:
                                link.post(o)
                            else:
                                o.then_inc(cp_set, 1)

            def angles(b):
                dims = [P, 2, BLK, NC5]
                ph = phi[:, :].rearrange("p (d q) -> p d q", d=2)[:, :, bass.ds(b * BLK, BLK)].unsqueeze(3).to_broadcast(dims)
                link(tt(ang, ph, iota.unsqueeze(1).unsqueeze(1).to_broadcast(dims), ALU.mult))
                link(ts(z1, ang, MAGIC, None, ALU.add))
                stt(out=ang, in0=z1, scalar=-MAGIC, in1=ang, op0=ALU.add, op1=ALU.subtract).then_inc(ang_set, 1)

            def flat(v):
                return v.rearrange("p d q c -> p (d q c)")

            def scan(b, par):
                dve.wait_ge(trig5, b * 2 + 2)
                dve.wait_ge(in_done, b * 2 + 2)
                ir, ii = (psum[4 + z][:, :].rearrange("p (d q c) -> p d q c", d=2, q=BLK) for z in range(2))
                link.post(tt(z1, ir, cos5, ALU.mult))
                link.post(tt(z2, ii, sin5, ALU.mult))
                link.post(tt(z3, ii, cos5, ALU.mult))
                link.post(tt(z4, ir, sin5, ALU.mult))
                link.upto(2)
                link.post(tt(z1, z1, z2, ALU.add))
                link.upto(1)
                dve.sem_inc(in_read, 1)
                link.post(tt(z3, z3, z4, ALU.subtract))
                link.upto(1)
                link.post(dve.tensor_tensor_scan(flat(z2), flat(dec5), flat(z1), 0.0, ALU.mult, ALU.add))
                link.upto(1)
                link.post(dve.tensor_tensor_scan(flat(z4), flat(dec5), flat(z3), 0.0, ALU.mult, ALU.add))
                w = slice(NCL - 1, NC5 - 1)
                t1, t2 = z1[:, :, :, 0:NCL], z1[:, :, :, NCL:NC5]
                t3, t4 = z3[:, :, :, 0:NCL], z3[:, :, :, NCL:NC5]
                link.upto(1)
                link.post(tt(t1, z2[:, :, :, w], cos5[:, :, :, w], ALU.mult))
                link.upto(1)
                link.post(tt(t2, z4[:, :, :, w], sin5[:, :, :, w], ALU.mult))
                link.post(tt(t3, z4[:, :, :, w], cos5[:, :, :, w], ALU.mult))
                link.post(tt(t4, z2[:, :, :, w], sin5[:, :, :, w], ALU.mult))
                link.upto(2)
                for z, (p, m, op) in enumerate(((t1, t2, ALU.subtract), (t3, t4, ALU.add))):
                    o = x5[par][z]
                    if z == 1:
                        link.upto(0)
                    for d, way in ((0, 1), (1, -1)):
                        tt(o[:, d], p[:, d, :, ::way], m[:, d, :, ::way], op).then_inc(x5_set, 1)

            tt(d_diag[0:2 * CH5], cst[0:2 * CH5, C_DIAG:C_DIAG + CH5].unsqueeze(1).to_broadcast([2 * CH5, GP5, CH5]),
               dcol[0:2 * CH5, :].unsqueeze(2).to_broadcast([2 * CH5, GP5, CH5]), ALU.mult).then_inc(diag_set, 1)
            c_products(0, True)
            c_sums(0, 0)
            angles(0)
            with turns(dve, 14, 2) as i:
                link.begin(i // 2, 2 * (7 + 12 + 6 + 2))
                for par in range(2):
                    c_products(i + (par + 1))
                    scan(i + par, par)
                    c_sums(i + (par + 1), 1 - par)
                    angles(i + (par + 1))
                link.end(7)
            c_products(15)
            scan(14, 0)
            c_sums(15, 1)
            angles(15)
            scan(15, 1)

            for t in range(2):
                dve.wait_ge(root_set, 4 + t)
                link(dve.reciprocal(mem_s[:, t, 1:2], mem_s[:, t, 1:2]))
                ts(mem_tok[:, t, :], mem_tok[:, t, :], mem_s[:, t, 1:2], None, ALU.mult).then_inc(mem_set, 1)
            with turns(dve, 32, 2 * NSLOT) as i:
                link.begin(i // 8, 4)
                for par in range(2):
                    for m in range(2):
                        k = i // 2 + (2 * par + m)
                        dve.wait_ge(sg_set, i // 2 + (2 * par + m + 1))
                        link(stt(out=glu_t[:, par, m, :], in0=psum[4 * par + m][:, 0:S], scalar=vecr("s5_b_glu", k),
                                 in1=sgm[:, par, m, :], op0=ALU.add, op1=ALU.mult))
                        dve.sem_inc(glu_free[par], 1)
                        g = gl[:, bass.ds(k, 1), :].rearrange("p a t -> p (a t)")
                        tt(g, g, glu_t[:, par, m, :], ALU.mult).then_inc(glu_set, 1)
                link.end(4)
            for k in range(KD):
                dve.wait_ge(memt_done, k // 2 + 1)
                ts(mem_t[:, k, :], psum[4 + k // 2][:, k % 2 * S:(k % 2 + 1) * S], vec("mem_norm_g_2", k), None, ALU.mult)\
                    .then_inc(memt_set, 1)
            at, u0 = ring_at["s5_out"], unit_at["s5_out"]
            dve.wait_ge(alpha_set, 3)
            with turns(dve, 8, NSLOT) as i:
                for s in range(2):
                    for m in range(2):
                        dve.wait_ge(sy_set, i + (2 * s + m + 1))
                        xk = xl[:, bass.ds(i + (2 * s + m), 1), :].rearrange("p a t -> p (a t)").rearrange("p (c h s) -> p s h c", h=2, s=4)
                        tt(xk, sy[:, 2 * s + m, :].rearrange("p (s h c) -> p s h c", s=4, h=2), xk, ALU.add).then_inc(x_new, 1)
            layer_norm(2, False, 2)

            def rms(n, name):
                dve.wait_ge(root_set, (7, 9, 10, 11)[n])
                link(dve.reciprocal(rstd, rstd))
                for k in range(KD):
                    stt(out=xn[:, k, :], in0=xl[:, k, :], scalar=vec(name, k), in1=rstd, op0=ALU.mult, op1=ALU.mult)\
                        .then_inc(xn_set, 1)

            dve.wait_ge(ln_out, KD)
            rms(0, "norm_mix_g_2")
            for v in pp:
                link(dve.memset(v[:, :, 0:16], 0.0))
            at, u0 = ring_at["w_in"], unit_at["w_in"]
            for s in range(2):
                dve.wait_ge(slot_done, at + s + 1)
                for m in range(2):
                    link(dve.tensor_copy(pp[0][:, 2 * s + m, 16:16 + S], psum[2 * ((u0 + s) % 2) + m][:, 0:S]))
                dve.sem_inc(unit_free[(u0 + s) % 2], 2)
            body = slice(16, 16 + S)
            for g, w in enumerate(POOLW):
                sh_ = w // 2
                link(tt(pp[2 - g % 2][:, g:4, body], (pp[0] if g == 0 else pp[2 - (g - 1) % 2])[:, g:4, body],
                        (pp[0] if g == 0 else pp[2 - (g - 1) % 2])[:, g:4, 16 - sh_:16 - sh_ + S], ALU.add))
                now = pp[2 - g % 2]
                link(tt(now[:, g, 0:16], now[:, g, 16:32], cst[:, C_CNT + 16 * g:C_CNT + 16 * g + 16], ALU.mult))
                link(stt(out=pp[1][:, g, 32:16 + S], in0=now[:, g, 32:16 + S], scalar=1.0 / w, in1=pp[0][:, g, 32:16 + S],
                         op0=ALU.mult, op1=ALU.subtract))
                tt(pp[1][:, g, 16:32], now[:, g, 0:16], pp[0][:, g, 16:32], ALU.subtract).then_inc(dpool_set, 1)
                dve.wait_ge(dpool_set, g + 1)
            dve.wait_ge(sgu_stat, 1)
            link(tt(sgu_wt, psum[5][:, :].rearrange("p (h t) -> p h t", h=4),
                    cst[:, C_MASK:C_MASK + P].unsqueeze(1).to_broadcast([P, 4, P]), ALU.mult))
            dve.wait_ge(pool_done, 1)
            for g in range(4):
                ts(cat[:, g, :], psum[6 + g // 2][:, g % 2 * S:(g % 2 + 1) * S], vec("pool_scale_2", g), None, ALU.mult)\
                    .then_inc(cat_set, 1)
            dve.wait_ge(sgu_stat, 2)
            tt(vv, vv, psum[4][:, 0:S].unsqueeze(1).to_broadcast([P, 4, S]), ALU.subtract).then_inc(vn_set, 1)
            dve.wait_ge(root_set, 8)
            link(dve.reciprocal(rstd, rstd))
            for k in range(4):
                o = stt(out=vv[:, k, :], in0=vv[:, k, :], scalar=vec("sgu_g_2", k), in1=rstd, op0=ALU.mult, op1=ALU.mult)
                if k == 0:
                    link(o)
                else:
                    o.then_inc(vn_set, 1)
            for t in range(2):
                dve.wait_ge(vt_done, t + 1)
                dve.tensor_copy(vtok[:, t, :], psum[6 + t][:, :]).then_inc(vtok_set, 1)
            dve.wait_ge(z_done, 1)
            for h in range(4):
                link(tt(sgu_z[:, h, :].rearrange("p (t q) -> p t q", t=2),
                        psum[6 + h // 2][:, (h % 2) * S:(h % 2 + 1) * S].rearrange("p (t q) -> p t q", t=2),
                        sgu_bb[:, h, :].unsqueeze(1).to_broadcast([P, 2, P]), ALU.add))
                tt(cat[:, 4 + h, :], sgu_z[:, h, :], uu[:, h, :], ALU.mult).then_inc(cat_set, 1)

            def add_out(name, slots_per_unit, h0):
                at, u0 = ring_at[name], unit_at[name]
                for s in range(4):
                    dve.wait_ge(slot_done, at + slots_per_unit * (s + 1))
                    for m in range(2):
                        k = 2 * s + m
                        tt(xl[:, k, :], psum[2 * ((u0 + s) % 2) + m][:, 0:S], xl[:, k, :], ALU.add).then_inc(h2_set, 1)
                    dve.wait_ge(h2_set, h0 + 2 * s + 2)
                    dve.sem_inc(unit_free[(u0 + s) % 2], 2)

            add_out("w_out", 1, 0)
            rms(1, "norm_xattn_g_2")
            def softmax2(h):
                b = h % 2
                for t in range(2):
                    dve.wait_ge(s2_done, 2 * h + t + 1)
                    link(dve.tensor_reduce(sm2[:, b, t, 0:1], psum[4 + t][:, 0:S], AX.X, ALU.max))
                    ts(sm2[:, b, t, 1:2], sm2[:, b, t, 0:1], -(float(XHD) ** -0.5), None, ALU.mult).then_inc(b2_set, 1)

            def normalise2(h):
                b = h % 2
                for t in range(2):
                    dve.wait_ge(e2_done, 2 * h + t + 1)
                    link(dve.reciprocal(sm2[:, b, t, 3:4], sm2[:, b, t, 2:3]))
                    ts(prob2[:, b, t, :], prob2[:, b, t, :], sm2[:, b, t, 3:4], None, ALU.mult).then_inc(p2_set, 1)

            def values2(h):
                dve.wait_ge(p2t_done, h + 1)
                if h >= 1:
                    dve.wait_ge(o2_done, h)
                dve.tensor_copy(prob2_t.rearrange("p m t -> p (m t)"), psum[6][:, :]).then_inc(p2t_set, 1)
                dve.wait_ge(o2_done, h + 1)
                dve.tensor_copy(o2[:, 2 * h:2 * h + 2, :].rearrange("p c t -> p (c t)"), psum[7][:, :]).then_inc(o2_set, 1)

            softmax2(0)
            normalise2(0)
            for h in range(XH):
                if h + 1 < XH:
                    softmax2(h + 1)
                    normalise2(h + 1)
                values2(h)
            add_out("wo", 1, 8)
            dve.wait_ge(cat_set, 8)
            dve.memset(hp[:, :, 0:2], 0.0).then_inc(ones_set, 1)
            rms(2, "norm_ffn_g_2")

            def taps(j, n):
                for h in range(4):
                    ch = j * 2 + (h % 2 + h // 2 * KF)
                    dve.wait_ge(conv_in, n + (h + 1))
                    link(stt(out=cv[:, h, :], in0=hp[:, h, 1:1 + S], scalar=vecr("conv_w_2", ch + 2 * KF), in1=cv[:, h, :],
                             op0=ALU.mult, op1=ALU.add))
                    stt(out=cv[:, h, :], in0=hp[:, h, 0:S], scalar=vecr("conv_w_2", ch), in1=cv[:, h, :],
                        op0=ALU.mult, op1=ALU.add).then_inc(conv_out, 1)
                for m in range(2):
                    dve.wait_ge(conv_out, n + (m + 3))
                    dve.wait_ge(silu_set, j * 2 + (m + 1))
                    tt(ff[:, bass.ds(j * 2 + m, 1), :].rearrange("p a t -> p (a t)"), cv[:, m, :], cv[:, 2 + m, :], ALU.mult)\
                        .then_inc(ff_set, 1)

            with turns(dve, 20, NSLOT) as i:
                link.begin(i // 4, 8)
                for s in range(2):
                    taps(i // 2 + s, i * 2 + 4 * s)
                link.end(5)
            taps(10, 40)
            add_out("w_down", 3, 16)
            rms(3, "final_norm_g_2")
            for t in range(2):
                dve.wait_ge(fin_t, 2 * t + 1)
                dve.tensor_copy(orow[:, t, 0:512], psum[2 * t][:, :]).then_inc(fin_set, 1)

        @block.gpsimd
        def _(pool):
            tt = pool.tensor_tensor
            pool.wait_ge(bc_scaled, 1)
            pool.dma_start(spill_b, bcol.rearrange("p z (d q) c -> p (z d) (q c)", d=2)).then_inc(bc_spilled, 16)
            pool.dma_start(spill_c, ccol.rearrange("p z (d q) c -> p (z d) (q c)", d=2)).then_inc(bc_spilled, 16)
            pool.wait_ge(h_ctx, KD)
            pool.tensor_scalar(xc[:, :, :], xc[:, :, :], ALPHA, None, ALU.mult).then_inc(alpha_set, 1)
            pool.wait_ge(h_lat, KD)
            pool.tensor_scalar(xl[:, :, :], xl[:, :, :], ALPHA, None, ALU.mult).then_inc(alpha_set, 1)
            pool.wait_ge(ln_lat, KD)
            pool.tensor_scalar(xl[:, :, :], xl[:, :, :], ALPHA, None, ALU.mult).then_inc(alpha_set, 1)

            pool.wait_ge(slot_done, ring_at["mla_out"] + 8)
            pool.memset(bbd[0], 0.0)
            pool.memset(bbd[1], 0.0).then_inc(p_link, 1)
            count = [1]

            def step(ins, i):
                ins.then_inc(p_link, 1)
                count[0] += 1
                pool.wait_ge(p_link, i + count[0])

            def b_tables(b, par, n_use, i, free=True):
                step(pool.tensor_copy(pwb.rearrange("p z i d q -> p (z i) d q"),
                                      pw[:, :, :, :].rearrange("p z i (d q) -> p (z i) d q", d=2)[:, :, :, bass.ds(b * BLK, BLK)]), i)
                pool.wait_ge(bb_in[par], n_use)
                pool.sem_inc(pool_passed, 1)
                for d in range(2):
                    if free:
                        pool.wait_ge(btt_done, b * 4 + (2 * d - 2))
                        pool.sem_inc(pool_passed, 1)
                    dims = [P, BLK, L5, CH5]
                    v1, v2 = (v.rearrange("p (q s c) -> p q s c", q=BLK, s=L5) for v in gen_p)
                    rev = slice(L5 - 1, None, -1) if d == 0 else slice(L5, 0, -1)
                    pr, pi = (pwb[:, z, rev, d, :].rearrange("p i q -> p q i").unsqueeze(3).to_broadcast(dims) for z in range(2))
                    br, bi = (bb[par][:, z, d, :, :].unsqueeze(2).to_broadcast(dims) for z in range(2))
                    step(tt(v1, br, pr, ALU.mult), i)
                    step(tt(v2, bi, pi, ALU.mult), i)
                    step(tt(bt[:, 0, d], v1, v2, ALU.subtract), i)
                    step(tt(v1, bi, pr, ALU.mult), i)
                    step(tt(v2, br, pi, ALU.mult), i)
                    tt(bt[:, 1, d], v1, v2, ALU.add).then_inc(bt_set, 1)
                    pool.wait_ge(bt_set, b * 2 + (d + 1))
                    pool.sem_inc(pool_passed, 1)

            b_tables(0, 0, 16, 0, False)
            pool.wait_ge(slot_done, ring_at["s5_g"] + 8)
            pool.memset(dec5, 0.0).then_inc(decays_clear, 1)
            b_tables(1, 1, 16, 0)
            base = count[0]
            with turns(pool, 14, 2) as i:
                count[0] = base
                for par in range(2):
                    b_tables(i + (par + 2), par, i * 8 + 32, i * 11)
                assert count[0] == base + 2 * 11


_INS = ["x", "c", "ctx", "c_ctx", "w_mod", "b_mod", "ln_g", "ln_b", "mla_w_in", "mla_q_norm", "mla_kv_norm", "mla_w_uq",
        "mla_w_uk", "mla_w_uv", "mla_w_out", "s5_w_in", "s5_lam_re", "s5_lam_im", "s5_log_dt", "s5_b_re", "s5_b_im",
        "s5_c_re", "s5_c_im", "s5_d", "s5_w_glu", "s5_b_glu", "s5_w_out", "mem_2", "norm_mix_g_2", "w_in_2", "pool_w_2",
        "pool_scale_2", "sgu_g_2", "sgu_w_2", "sgu_b_2", "w_out_2", "norm_xattn_g_2", "mem_norm_g_2", "wq_2", "wk_2",
        "wv_2", "wo_2", "norm_ffn_g_2", "w_up_2", "conv_w_2", "conv_b_2", "w_down_2", "final_norm_g_2"]


def kernel(**inputs):
    import concourse.bacc as bacc
    from concourse.bass_utils import run_bass_kernel_spmd

    nc = bacc.Bacc("TRN2", target_bir_lowering=False, num_devices=1)
    arrays = {f"in_{n}": np.ascontiguousarray(inputs[n]) for n in _INS}
    arrays["in_consts"] = shape_constants()
    a = {n[3:]: nc.dram_tensor(n, v.shape, mybir.dt.from_np(v.dtype), kind="ExternalInput").ap() for n, v in arrays.items()}
    out = nc.dram_tensor("out", (1, S, D), F32, kind="ExternalOutput").ap()
    spill = [nc.dram_tensor(n, (P, 4, GP5 * CH5), F32, kind="Internal").ap() for n in ("s5_b_scaled", "s5_c_turned")]
    program(nc, a, out, *spill)
    r = run_bass_kernel_spmd(nc, [arrays], core_ids=[0])
    return r.results[0]["out"]
```
